# Optimizing a Trainium2 kernel written in Bass

```python
import jax, jax.numpy as jnp
from jax import lax
import numpy as np

D_MODEL = 1024
BATCH = 1
SEQ = 512
DEPTH = 2

N_MIXERS = 2
N_A = (DEPTH + N_MIXERS - 1) // N_MIXERS
N_B = DEPTH // N_MIXERS

CHUNK = 128
GM_HALF = D_MODEL
GM_GROUPS = 8
GM_GROUP_DIM = GM_HALF // GM_GROUPS

ATT_HEADS = 8
ATT_HEAD_DIM = D_MODEL // ATT_HEADS
KV_LATENT = 256
IDX_HEADS = 8
IDX_DIM = 64
TOPK_MAX = 256
Q_BLOCK = 128
Q_WIDTH = ATT_HEADS * ATT_HEAD_DIM
PROJ_B = Q_WIDTH + KV_LATENT + IDX_HEADS * IDX_DIM + IDX_DIM + IDX_HEADS
SPLITS_B = (Q_WIDTH, Q_WIDTH + KV_LATENT, Q_WIDTH + KV_LATENT + IDX_HEADS * IDX_DIM,
            Q_WIDTH + KV_LATENT + IDX_HEADS * IDX_DIM + IDX_DIM)

N_EGROUPS = 4
EXPERTS_PER_GROUP = 8
N_EXPERTS = N_EGROUPS * EXPERTS_PER_GROUP
TOPK_E = 2
EXPERT_FF = 256

PLE_DIM = 256

ALPHA = (2 * DEPTH) ** 0.25
BETA = (8 * DEPTH) ** -0.25

kernel_name = 'hybrid_gmlp_dsa_hiermoe_deepnorm'

def _layer_norm(x, g, b, eps=1e-5):
    xf = x.astype(jnp.float32)
    mu = jnp.mean(xf, axis=-1, keepdims=True)
    var = jnp.mean(jnp.square(xf - mu), axis=-1, keepdims=True)
    return ((xf - mu) * lax.rsqrt(var + eps)).astype(x.dtype) * g + b

def _rms_norm(x, g, eps=1e-6):
    xf = x.astype(jnp.float32)
    ms = jnp.mean(jnp.square(xf), axis=-1, keepdims=True)
    return (xf * lax.rsqrt(ms + eps)).astype(x.dtype) * g

def chunked_gmlp(x, w_in, b_in, vn_g, vn_b, w_s, b_s, w_out):
    bsz, seq, _ = x.shape
    z = jax.nn.gelu(x @ w_in + b_in, approximate=False)
    u, v = jnp.split(z, 2, axis=-1)
    v = _layer_norm(v, vn_g, vn_b)
    v = v.reshape(bsz, seq // CHUNK, CHUNK, GM_GROUPS, GM_GROUP_DIM)
    causal = jnp.tril(jnp.ones((CHUNK, CHUNK), dtype=bool))
    w_c = jnp.where(causal[None], w_s, jnp.zeros_like(w_s))
    s = jnp.einsum('gts,bcsgd->bctgd', w_c, v) + b_s.T[:, :, None]
    return (u * s.reshape(bsz, seq, GM_HALF)) @ w_out

def dsa_attention(x, w_in, kv_g, w_uk, w_uv, w_out):
    bsz, seq, _ = x.shape
    k_sel = min(TOPK_MAX, seq // 4)
    n_blk = seq // Q_BLOCK
    proj = x @ w_in
    q, c_kv, q_idx, k_idx, w_idx = jnp.split(proj, SPLITS_B, axis=-1)
    q = q.reshape(bsz, seq, ATT_HEADS, ATT_HEAD_DIM)
    c_kv = _rms_norm(c_kv, kv_g)
    q_idx = q_idx.reshape(bsz, seq, IDX_HEADS, IDX_DIM)
    w_idx = w_idx * (IDX_HEADS * IDX_DIM) ** -0.5
    q_lat = jnp.einsum('blhd,hcd->blhc', q, w_uk) * ATT_HEAD_DIM ** -0.5
    key_pos = jnp.arange(seq)

    def to_blocks(a):
        return a.reshape((bsz, n_blk, Q_BLOCK) + a.shape[2:]).swapaxes(0, 1)

    def block(args):
        ql_b, qi_b, wi_b, t0 = args
        tq = t0 + jnp.arange(Q_BLOCK)
        rel = jax.nn.relu(jnp.einsum('bqhd,bsd->bqhs', qi_b, k_idx))
        score = jnp.einsum('bqhs,bqh->bqs', rel, wi_b).astype(jnp.float32)
        causal = key_pos[None, :] <= tq[:, None]
        score = jnp.where(causal[None], score, -jnp.inf)
        _, idx = lax.top_k(score, k_sel)
        c_sel = jax.vmap(lambda c, i: c[i])(c_kv, idx)
        valid = idx <= tq[None, :, None]
        logits = jnp.einsum('bqhc,bqkc->bqhk', ql_b, c_sel).astype(jnp.float32)
        logits = jnp.where(valid[:, :, None, :], logits, -jnp.inf)
        probs = jax.nn.softmax(logits, axis=-1).astype(c_sel.dtype)
        return jnp.einsum('bqhk,bqkc->bqhc', probs, c_sel)

    o = lax.map(block, (to_blocks(q_lat), to_blocks(q_idx), to_blocks(w_idx),
                        jnp.arange(n_blk) * Q_BLOCK))
    o = o.swapaxes(0, 1).reshape(bsz, seq, ATT_HEADS, KV_LATENT)
    o = jnp.einsum('blhc,hcd->blhd', o, w_uv).reshape(bsz, seq, Q_WIDTH)
    return o @ w_out

def hier_moe(x, wg, bg, we, be, w_in, w_out):
    bsz, seq, dm = x.shape
    xt = x.reshape(bsz * seq, dm)
    g_logit = (xt @ wg + bg).astype(jnp.float32)
    g_prob = jax.nn.softmax(g_logit, axis=-1)
    g_sel = jnp.argmax(g_logit, axis=-1)
    p_g = jnp.take_along_axis(g_prob, g_sel[:, None], axis=1)[:, 0]
    e_logit = (xt @ we + be).astype(jnp.float32).reshape(-1, N_EGROUPS, EXPERTS_PER_GROUP)
    e_logit = jnp.take_along_axis(e_logit, g_sel[:, None, None], axis=1)[:, 0]
    top_p, top_i = lax.top_k(jax.nn.softmax(e_logit, axis=-1), TOPK_E)
    top_p = top_p / jnp.sum(top_p, axis=-1, keepdims=True) * p_g[:, None]
    in_group = jnp.sum(jax.nn.one_hot(top_i, EXPERTS_PER_GROUP) * top_p[..., None], axis=1)
    gate = (jax.nn.one_hot(g_sel, N_EGROUPS)[:, :, None] * in_group[:, None, :]).astype(x.dtype)
    w_in_g = w_in.reshape(N_EGROUPS, EXPERTS_PER_GROUP, dm, 2 * EXPERT_FF)
    w_out_g = w_out.reshape(N_EGROUPS, EXPERTS_PER_GROUP, EXPERT_FF, dm)
    out = jnp.zeros_like(xt)
    for g in range(N_EGROUPS):
        h = jnp.einsum('td,edf->tef', xt, w_in_g[g])
        a, b = jnp.split(h, 2, axis=-1)
        h = jax.nn.silu(a) * b * gate[:, g, :, None]
        out = out + jnp.einsum('tef,efd->td', h, w_out_g[g])
    return out.reshape(bsz, seq, dm)

def setup_inputs(seed: int = 0) -> dict:
    key = jax.random.key(seed)
    ks = iter(jax.random.split(key, 40))

    def nrm(shape, scale):
        return jax.random.normal(next(ks), shape, jnp.float32) * scale

    def gain(shape):
        return 1.0 + nrm(shape, 0.05)

    d = D_MODEL
    return {
        'x': nrm((BATCH, SEQ, d), 1.0),
        'p': nrm((DEPTH, BATCH, SEQ, PLE_DIM), 1.0),
        'a_w_in': nrm((N_A, d, 2 * GM_HALF), d ** -0.5),
        'a_b_in': nrm((N_A, 2 * GM_HALF), 0.02),
        'a_vn_g': gain((N_A, GM_HALF)),
        'a_vn_b': nrm((N_A, GM_HALF), 0.02),
        'a_w_s': nrm((N_A, GM_GROUPS, CHUNK, CHUNK), CHUNK ** -0.5),
        'a_b_s': 1.0 + nrm((N_A, GM_GROUPS, CHUNK), 0.1),
        'a_w_out': nrm((N_A, GM_HALF, d), BETA * GM_HALF ** -0.5),
        'b_w_in': nrm((N_B, d, PROJ_B), d ** -0.5),
        'b_kv_g': gain((N_B, KV_LATENT)),
        'b_w_uk': nrm((N_B, ATT_HEADS, KV_LATENT, ATT_HEAD_DIM), KV_LATENT ** -0.5),
        'b_w_uv': nrm((N_B, ATT_HEADS, KV_LATENT, ATT_HEAD_DIM), KV_LATENT ** -0.5),
        'b_w_out': nrm((N_B, Q_WIDTH, d), BETA * Q_WIDTH ** -0.5),
        'ln1_g': gain((DEPTH, d)),
        'ln1_b': nrm((DEPTH, d), 0.02),
        'ln2_g': gain((DEPTH, d)),
        'ln2_b': nrm((DEPTH, d), 0.02),
        'r_wg': nrm((DEPTH, d, N_EGROUPS), d ** -0.5),
        'r_bg': nrm((DEPTH, N_EGROUPS), 0.01),
        'r_we': nrm((DEPTH, d, N_EXPERTS), d ** -0.5),
        'r_be': nrm((DEPTH, N_EXPERTS), 0.01),
        'e_w_in': nrm((DEPTH, N_EXPERTS, d, 2 * EXPERT_FF), d ** -0.5),
        'e_w_out': nrm((DEPTH, N_EXPERTS, EXPERT_FF, d), BETA * EXPERT_FF ** -0.5),
        'ple_w': nrm((DEPTH, PLE_DIM, d), PLE_DIM ** -0.5),
        'ple_gw': nrm((DEPTH, d, d), d ** -0.5),
        'ple_gb': nrm((DEPTH, d), 0.02),
    }

def reference(x, p, a_w_in, a_b_in, a_vn_g, a_vn_b, a_w_s, a_b_s, a_w_out,
              b_w_in, b_kv_g, b_w_uk, b_w_uv, b_w_out,
              ln1_g, ln1_b, ln2_g, ln2_b,
              r_wg, r_bg, r_we, r_be, e_w_in, e_w_out,
              ple_w, ple_gw, ple_gb):
    for i in range(DEPTH):
        j = i // N_MIXERS
        if i % N_MIXERS == 0:
            mix = chunked_gmlp(x, a_w_in[j], a_b_in[j], a_vn_g[j], a_vn_b[j],
                               a_w_s[j], a_b_s[j], a_w_out[j])
        else:
            mix = dsa_attention(x, b_w_in[j], b_kv_g[j], b_w_uk[j], b_w_uv[j], b_w_out[j])
        x = _layer_norm(ALPHA * x + mix, ln1_g[i], ln1_b[i])
        ffn = hier_moe(x, r_wg[i], r_bg[i], r_we[i], r_be[i], e_w_in[i], e_w_out[i])
        x = _layer_norm(ALPHA * x + ffn, ln2_g[i], ln2_b[i])
        x = x + (p[i] @ ple_w[i]) * jax.nn.sigmoid(x @ ple_gw[i] + ple_gb[i])
    return x


_drawn_inputs = setup_inputs


def setup_inputs(seed=0):
    import zlib

    import numpy as np

    out = dict(_drawn_inputs(seed))
    spreads = {}
    factors = {'a_b_in': 5.375,
     'a_vn_g': 5.251,
     'a_vn_b': 8.0,
     'b_kv_g': 7.99,
     'r_bg': 8.0,
     'r_be': 8.0,
     'ple_gb': 7.741}
    for name, (base, spread) in spreads.items():
        noise = np.random.default_rng([zlib.crc32(name.encode()), seed]).standard_normal(out[name].shape)
        drawn = base * np.exp(spread * noise) if base else spread * noise
        out[name] = __import__('jax').numpy.asarray(drawn.astype(out[name].dtype))
    for name, factor in factors.items():
        out[name] = (out[name] * factor).astype(out[name].dtype)
    return out
```

```python
from contextlib import ExitStack

import numpy as np

import concourse.bass as bass
from concourse import mybir

F32 = mybir.dt.float32
BF16 = mybir.dt.bfloat16
I32 = mybir.dt.int32
U32 = mybir.dt.uint32
ALU = mybir.AluOpType
ACT = mybir.ActivationFunctionType
AX = mybir.AxisListType

P = 128
DEPTH = 2
ALPHA = (2 * DEPTH) ** 0.25
LN_EPS, RMS_EPS = 1e-5, 1e-6
BIG = 1e30
TAKEN = -3e38

T, D = 512, 1024
NT, KD, BANK = T // P, D // P, 512
NB = D // BANK
HEADS, HD, LAT = 8, 128, 256
IH, ID = 8, 64
TOPK = min(256, T // 4)
NG, EPG = 4, 8
NE = NG * EPG
FF = 256
PLE = 256
BLK = 64
NCH = T // BLK - 1
NOV = 2 * T // BLK - 1
NU = 48
NONE = 4096
RING = 4


class Job:

    def __init__(self, n, engine, nth):
        self.n, self.bank, self.engine, self.nth = n, 4 + n % 4, engine, nth


class Jobs:

    def __init__(self):
        self.order, self.by, self.count = [], {}, {"act": 0, "dve": 0}

    def add(self, engine, *name):
        self.count[engine] += 1
        job = Job(len(self.order), engine, self.count[engine])
        self.order.append(job)
        self.by[name] = job

    def __getitem__(self, name):
        return self.by[name]


UNITS = [(qt, hg) for qt in range(NT) for hg in range(2)]


def plan_jobs():
    jobs = Jobs()
    for q in range(2):
        jobs.add("act", "ws", q)
    for w in range(4):
        for i in range(NT):
            jobs.add("dve", "in", w, i)
    for g in range(8):
        jobs.add("dve", "sp", g)
    for l in range(DEPTH):
        if l == 1:
            for q in range(4):
                jobs.add("act", "uk", q)
            jobs.add("act", "ki")
            for i in range(NT):
                jobs.add("dve", "ck", i)
            for b in range(4):
                jobs.add("act", "qi", b)
            for qt in range(1, NT):
                for h in range(IH):
                    jobs.add("act", "ix", qt, h)
            for cc in range(2):
                jobs.add("act", "ct", cc)
            for h in range(HEADS):
                jobs.add("act", "q", h)
            for h in range(HEADS):
                for cc in range(2):
                    jobs.add("act", "ql", h, cc)
            for u, (qt, hg) in enumerate(UNITS):
                for kt in range(qt + 1):
                    jobs.add("act" if kt % 2 else "dve", "tr", u, kt)
                for cc in range(2):
                    jobs.add("dve" if cc else "act", "pv", u, cc)
                jobs.add("act", "uv", u)
        for step in range(NT + 1):
            if step < NT:
                for n in range(NB):
                    jobs.add("dve", "out", l, step, n)
            if step:
                jobs.add("dve", "rt", l, step - 1)
        for cc in range(2):
            jobs.add("act", "pt", l, cc)
        for i in range(NT):
            for kind in ("g", "pp"):
                for n in range(NB):
                    jobs.add("dve", kind, l, i, n)
    return jobs


def trunk(nc, x, p, a_w_in, a_b_in, a_vn_g, a_vn_b, a_w_s, a_b_s, a_w_out,
          b_w_in, b_kv_g, b_w_uk, b_w_uv, b_w_out, ln1_g, ln1_b, ln2_g, ln2_b,
          r_wg, r_bg, r_we, r_be, e_w_in, e_w_out, ple_w, ple_gw, ple_gb, out):
    jobs = plan_jobs()
    x_rows = nc.dram_tensor("x_rows", [T, D], F32, kind="Internal").ap()
    y_rows = nc.dram_tensor("y_rows", [2 * T, D], F32, kind="Internal").ap()

    Q0, K0, I0, KI0 = 0, HEADS * HD, HEADS * HD + LAT, HEADS * HD + LAT + IH * ID
    half = lambda w, n: [(w[:, n * BANK:(n + 1) * BANK], 0, BANK)]
    misc = [(b_w_in[0][:, K0:K0 + LAT], 0, LAT),
            (b_w_in[0][:, KI0:KI0 + ID], LAT, ID),
            (b_w_in[0][:, KI0:KI0 + ID + IH], LAT + ID, ID + IH)]
    wa_head = [
        [half(a_w_in[0], 2), half(a_w_in[0], 3), half(a_w_in[0], 0), half(a_w_in[0], 1),
         half(a_w_out[0], 0), half(a_w_out[0], 1)],
        [misc, [(b_w_in[0][:, I0:I0 + BANK], 0, BANK)], half(b_w_in[0], 0), half(b_w_in[0], 1),
         half(b_w_out[0], 0), half(b_w_out[0], 1)],
    ]
    WA_E = [6, 6 + NE + 2 + 6]
    WB_E = [0, NE + 3]
    WA_HEAD = [0, 6 + NE + 2]
    WA_GW = [WA_E[0] + NE, WA_E[1] + NE]
    WB_PLE = [WB_E[0] + NE, WB_E[1] + NE]
    WB_UK, WB_UV = NE + 1, NE + 2
    FLAT = "(a p) n -> p a n"

    wa_last, wb_last = {}, {WB_UK: ("uk", 3), WB_UV: ("uv", len(UNITS) - 1)}
    for w in range(4):
        wa_last[w] = ("in", w, NT - 1)
    for n, name in enumerate([("ck", NT - 1), ("qi", 3), ("q", 3), ("q", 7)]):
        wa_last[WA_HEAD[1] + n] = name
    for l in range(DEPTH):
        for n in range(NB):
            wa_last[WA_HEAD[l] + 4 + n] = ("out", l, NT - 1, n)
            wa_last[WA_GW[l] + n] = ("g", l, NT - 1, n)
        wb_last[WB_PLE[l]] = ("pp", l, NT - 1, NB - 1)
    MISC = WA_HEAD[1]

    def wa_turn(n):
        extra = len(misc) - 1 if n >= MISC and n % RING == MISC % RING else 0
        return 16 * (n // RING + 1 + extra)

    ctx = ExitStack()
    with ctx:
        def sb(name, shape, dt=F32):
            return ctx.enter_context(nc.sbuf_tensor(name, shape, dt))

        def sem(name):
            return ctx.enter_context(nc.semaphore(name))

        ps = ctx.enter_context(nc.psum_tensor("ps", [P, 8, BANK], F32))
        wa = [sb(f"wa{r}", [P, KD, BANK]) for r in range(RING)]
        wb = [sb(f"wb{r}", [P, 2, D]) for r in range(RING)]
        wbh = [w[:].rearrange("p a (h d) -> p (a h) d", d=HD) for w in wb]
        X = sb("X", [P, NT, D])
        XT = sb("XT", [P, KD * T])
        A = sb("A", [P, KD * T])
        B = sb("B", [P, KD * T])
        C = sb("C", [P, 9216])
        LNG, LNB = sb("LNG", [P, D]), sb("LNB", [P, D])

        def cut(area, at, *dims):
            n = int(np.prod(dims))
            v = area[:, at:at + n]
            if len(dims) == 2:
                v = v.rearrange("p (a b) -> p a b", a=dims[0])
            if len(dims) == 3:
                v = v.rearrange("p (a b c) -> p a b c", a=dims[0], b=dims[1])
            if len(dims) == 4:
                v = v.rearrange("p (a b c d) -> p a b c d", a=dims[0], b=dims[1], c=dims[2])
            return v

        XTv, AT = cut(XT, 0, KD, T), cut(A, 0, KD, T)
        V, U = cut(A, 0, NT, D), cut(B, 0, NT, D)
        BINV, BINU, VNG, VNB = (C[:, D * n:D * (n + 1)] for n in range(4))
        WS, WCT, BS = cut(C, 4096, 8, P), cut(C, 5120, 8, P), C[:, 6144:6152]
        QIT, KIT, CK, CKT = cut(C, 0, 4, T), C[:, 2048:2560], cut(C, 2560, NT, LAT), cut(C, 3584, 2, T)
        UKT, SELS, OL, KVG = cut(C, 4608, HEADS, LAT), C[:, 6656:7936], cut(C, 7936, 2, BANK), C[:, 8960:9216]
        SEL = [SELS[:, P * (q * (q + 1) // 2):][:, :P * (q + 1)] for q in range(NT)]
        PR, PT = cut(C, 0, 4, BANK), cut(C, 4608, NT, BANK)
        RL = cut(B, 0, 2, BANK)
        JUNK = cut(B, 1024, NT, LAT)
        QL = [cut(B if h < 4 else XT, (h % 4) * 2 * T, 2, T) for h in range(HEADS)]
        LG = cut(C, 8192, NT, NG + NE)
        at = [0]

        def tmp(*dims):
            v = cut(A, at[0], *dims)
            at[0] += int(np.prod(dims))
            return v

        gmax, gkey, gsum, m1, m2, key, dexp, den = (tmp(NT) for _ in range(8))
        geq, gsel, gexp, pen = (tmp(NT, NG) for _ in range(4))
        em, eq = tmp(NT, NE), tmp(NT, NE)
        EK, EW = tmp(2, NT, NE), tmp(2, NT, NE)
        MB = cut(A, at[0], NT * NE // 2).bitcast(BF16).rearrange("p (a b) -> p a b", a=NT)
        at[0] += NT * NE // 2
        cex, cin, extra, one, c0 = (tmp(NE) for _ in range(5))
        rank, base, eidx, blk, slot, unit, further_blk = (tmp(2 * NT) for _ in range(7))
        ints, inti, intc = (tmp(n).bitcast(I32) for n in (2 * NT, 2 * NT, NE))
        RSH, UVH = tmp(2 * NT, BLK), tmp(2 * NT, NU)
        whose, owner = tmp(NOV, NE), tmp(NOV)
        rowf, offs = tmp(NU), tmp(NU)
        XG, YO = ([area[:, D * s:D * (s + 1)] for s in range(RING)] for area in (B, A))
        OYO = XG[1]
        XGT = [cut(XT, 512 * s, KD, BLK) for s in range(2)]
        SA = [cut(XT, 1024 + 128 * s, 2, BLK) for s in range(2)]
        HT = [cut(XT, 1280 + 128 * s, 2, BLK) for s in range(2)]
        HS = [cut(XT, 1536 + FF * s, FF) for s in range(2)]
        OWA, OWB = cut(A, 0, KD, BANK), cut(XT, 2048, 2, D)
        RR = [cut(A, 2048 * s, 2, D) for s in range(2)]
        PIN, PTT, GBB = cut(C, 0, NT, PLE), cut(C, 1024, 2, T), C[:, 2048:3072]
        GT = [B[:, 512 * s:512 * (s + 1)] for s in range(4)]

        ident = sb("ident", [P, P])
        strict = sb("strict", [P, P], BF16)
        ones = sb("ones", [P, P], BF16)
        iota = sb("iota", [P, BLK])
        rev = sb("rev", [P, NE])
        val = sb("val", [P, 2 * NT])
        rw = sb("rw", [P, KD, NG + NE])
        rb = sb("rb", [P, NG + NE])
        idx_tok = sb("idx_tok", [BLK, NU], U32)
        idx_row = sb("idx_row", [BLK, NU], U32)
        meta = sb("meta", [1, NOV + 1], I32)
        stg = sb("stg", [BLK, 4], U32)
        sts = sb("sts", [BLK, 4], U32)
        gates = sb("gates", [P, 2, NT])
        WI = sb("WI", [P, NT, IH])
        bn = sb("bn", [P, 2, 6])
        mv = sb("mv", [P, 2])
        rstd = sb("rstd", [P, 1])
        minus_half = sb("minus_half", [P, 1])
        m8 = sb("m8", [P, 8])
        ss = sb("ss", [P, NT])
        mx, nmx, rs, rc = (sb(n, [P, 4]) for n in ("mx", "nmx", "rs", "rc"))

        consts_ready, x_loaded, gm_loaded = sem("consts_ready"), sem("x_loaded"), sem("gm_loaded")
        wa_full = [sem(f"wa_full{r}") for r in range(RING)]
        wb_full = [sem(f"wb_full{r}") for r in range(RING)]
        wa_used, wb_used = sem("wa_used"), sem("wb_used")
        tr_ps, tr_a, tr_v = sem("tr_ps"), sem("tr_a"), sem("tr_v")
        job_done, job_a, job_v = sem("job_done"), sem("job_a"), sem("job_v")
        z_done = sem("z_done")
        ln_pre, ln_done, lnp_loaded = sem("ln_pre"), sem("ln_done"), sem("lnp_loaded")
        chain_v, chain_p = sem("chain_v"), sem("chain_p")
        wct_ready = sem("wct_ready")
        rw_loaded, ple_in, kvg_loaded = sem("rw_loaded"), sem("ple_in"), sem("kvg_loaded")
        rows_stored = sem("rows_stored")
        gate_in, gate_exp = sem("gate_in"), sem("gate_exp")
        picks, ranked, coded, unit_ps, units_ready = (sem(n) for n in ("picks", "ranked", "coded", "unit_ps", "units_ready"))
        xg_zero = sem("xg_zero")
        staged = [sem(f"staged{l}") for l in range(DEPTH)]
        xg_full = [sem(f"xg_full{s}") for s in range(RING)]
        sc_done = [sem(f"sc_done{s}") for s in range(RING)]
        xg_used, xgt_ready, hs_ready, hs_ps, sa_ready, ht_ready, yo_a, yo_v = (
            [sem(f"{n}{l}") for l in range(DEPTH)]
            for n in ("xg_used", "xgt_ready", "hs_ready", "hs_ps", "sa_ready", "ht_ready", "yo_a", "yo_v"))
        ov_free, ov_w, ov_g, ov_t, ov_x, ov_h, ov_s, ov_m, ov_y, ov_e, ov_d, moe_done = (
            [sem(f"{n}{l}") for l in range(DEPTH)]
            for n in ("ov_free", "ov_w", "ov_g", "ov_t", "ov_x", "ov_h", "ov_s", "ov_m", "ov_y", "ov_e", "ov_d", "moe_done"))
        rr_full = [sem(f"rr_full{s}") for s in range(2)]
        rr_scaled, rr_used = sem("rr_scaled"), sem("rr_used")
        g_sig, ple_done = sem("g_sig"), sem("ple_done")
        var_ready, rstd_ready, rl_used, sel_mask = (sem(n) for n in ("var_ready", "rstd_ready", "rl_used", "sel_mask"))
        lg_ps, lg_read, lg_max, p_exp, p_norm = (sem(n) for n in ("lg_ps", "lg_read", "lg_max", "p_exp", "p_norm"))
        out_done = sem("out_done")
        passed = sem("passed")

        TR = {}
        for s, name in enumerate(["x0", "gated", "x1a", "x2a", "x3a", "x1b", "x2b"]):
            for i in range(NT):
                TR[name, i] = None
        order = [("x0", i) for i in range(NT)] + [("gated", i) for i in range(NT)] + [("x1a", i) for i in range(NT)]
        ple_order = []
        for i in range(NT):
            ple_order.append(("x2a", i))
            if i:
                ple_order.append(("x3a", i - 1))
        ple_order.append(("x3a", NT - 1))
        order += ple_order + [("x1b", i) for i in range(NT)] + [("x2b", i) for i in range(NT)]
        for n, tile_name in enumerate(order):
            TR[tile_name] = n
        LN = {"v": 0, (0, 1): NT, (0, 2): 2 * NT, (1, 1): 3 * NT, (1, 2): 4 * NT}
        LNP = {(0, 1): 1, (0, 2): 2, (1, 1): 3, (1, 2): 4}

        def drained(eng, job):
            eng.wait_ge(job_a if job.engine == "act" else job_v, job.nth)

        links_v, norms, rstds = [0], [0], [0]
        block = ctx.enter_context(nc.Block())

        @block.sync
        def _(sp):
            def slot_free(n, last, used, first_expert):
                if n < 0:
                    return
                if n in last:
                    sp.wait_ge(job_done, jobs[last[n]].n + 1)
                else:
                    l = 1 if n >= first_expert[1] else 0
                    sp.wait_ge(used, l * NE + n - first_expert[l] + 1)

            def load_wa(n, parts):
                slot_free(n - RING, wa_last, wa_used, WA_E)
                s = n % RING
                for src, at, w in parts:
                    sp.dma_start(wa[s][:, :, at:at + w], src.rearrange(FLAT, p=P)).then_inc(wa_full[s], 16)

            def load_wb(n, dst, src):
                slot_free(n - RING, wb_last, wb_used, WB_E)
                sp.dma_start(dst, src).then_inc(wb_full[n % RING], 16)

            def load_experts(l, it):
                for j in range(RING):
                    e = sp.snap(it * RING + j)
                    before = sp.snap(it * RING + (l * NE + j + 1 - RING))
                    sa, sb_ = (WA_E[l] + j) % RING, (WB_E[l] + j) % RING
                    sp.wait_ge(wa_used, before)
                    sp.dma_start(wa[sa][:], e_w_in[l, bass.ds(e, 1)].rearrange("o (a p) f -> p (o a) f", p=P)).then_inc(wa_full[sa], 16)
                    sp.wait_ge(wb_used, before)
                    sp.dma_start(wb[sb_][:], e_w_out[l, bass.ds(e, 1)].rearrange("o (a p) f -> p (o a) f", p=P)).then_inc(wb_full[sb_], 16)

            for i in range(NT):
                sp.dma_start(X[:, i, :], x[0, i * P:(i + 1) * P, :]).then_inc(x_loaded, 16)
            for l in range(DEPTH):
                for n, parts in enumerate(wa_head[l]):
                    load_wa(WA_HEAD[l] + n, parts)
                    if l == 1 and n == 1:
                        load_wb(WB_UK, wbh[WB_UK % RING], b_w_uk[0].rearrange("h (a p) d -> p (h a) d", p=P))
                    if l == 1 and n == 3:
                        load_wb(WB_UV, wbh[WB_UV % RING], b_w_uv[0].rearrange("h (a p) d -> p (h a) d", p=P))
                for e in range(RING):
                    load_wa(WA_E[l] + e, [(e_w_in[l, e], 0, BANK)])
                    load_wb(WB_E[l] + e, wb[(WB_E[l] + e) % RING][:], e_w_out[l, e].rearrange(FLAT, p=P))
                with sp.Fori(1, NE // RING) as it:
                    load_experts(l, it)
                sp.wait_ge(units_ready, l + 1)
                further = sp.value_load(meta[0:1, NOV:NOV + 1], min_val=0, max_val=NOV)
                with sp.If(further > 0):
                    with sp.Fori(0, NOV) as u:
                        with sp.If(u < further):
                            e = sp.value_load(meta[0:1, bass.ds(u, 1)], min_val=0, max_val=NE - 1)
                            turn = sp.snap(u + 1)
                            sp.wait_ge(ov_free[l], turn)
                            sp.dma_start(OWA, e_w_in[l, bass.ds(e, 1)].rearrange("o (a p) f -> p (o a) f", p=P)).then_inc(ov_w[l], 16)
                            sp.dma_start(OWB, e_w_out[l, bass.ds(e, 1)].rearrange("o (a p) f -> p (o a) f", p=P)).then_inc(ov_w[l], 16)
                        sp.nop()
                for n in range(NB):
                    load_wa(WA_GW[l] + n, half(ple_gw[l], n))
                load_wb(WB_PLE[l], wb[WB_PLE[l] % RING][:], ple_w[l].rearrange(FLAT, p=P))
            for i in range(NT):
                sp.wait_ge(ple_done, NB * (NT + i + 1))
                sp.dma_start(out[0, i * P:(i + 1) * P, :], X[:, i, :]).then_inc(out_done, 16)
            sp.wait_ge(out_done, 16 * NT)

        @block.gpsimd
        def _(pool):
            links = [0]

            def link(ins):
                links[0] += 1
                ins.then_inc(chain_p, 1)
                pool.wait_ge(chain_p, links[0])

            g = nc.gpsimd
            last_tok, last_row = pool.to_reg(T - 1), pool.to_reg(2 * T - 1)
            link(g.memset(ident[:], 0.0))
            link(g.affine_select(out=ident[:], in_=ident[:], compare_op=ALU.not_equal, fill=1.0, base=0,
                                 pattern=[[-1, P]], channel_multiplier=1))
            link(g.memset(minus_half[:], -0.5))
            link(g.memset(ones[:], 1.0))
            link(g.affine_select(out=strict[:], in_=ones[:], compare_op=ALU.is_gt, fill=0.0, base=0,
                                 pattern=[[1, P]], channel_multiplier=-1))
            link(g.iota(iota[:], pattern=[[1, BLK]], base=0, channel_multiplier=0, allow_small_or_imprecise_dtypes=True))
            link(g.iota(rev[:], pattern=[[-1, NE]], base=NE, channel_multiplier=0, allow_small_or_imprecise_dtypes=True))
            link(g.iota(val[:], pattern=[[T, 2], [P, NT]], base=-NONE, channel_multiplier=1,
                        allow_small_or_imprecise_dtypes=True))
            g.sem_inc(consts_ready, 1)

            def load_ln(gain, bias):
                for dst, src in ((LNG, gain), (LNB, bias)):
                    pool.dma_start(dst[:], src.partition_broadcast(P)).then_inc(lnp_loaded, 16)

            def add_ln_bias(first, tile, bias, tiles=range(NT)):
                for i in tiles:
                    rstds[0] += 1
                    pool.wait_ge(var_ready, rstds[0])
                    link(g.tensor_scalar(rstd[:], mv[:, 1:2], LN_EPS, None, ALU.add))
                    g.tensor_tensor(rstd[:], rstd[:], minus_half[:], ALU.pow).then_inc(rstd_ready, 1)
                    pool.wait_ge(ln_pre, first + i + 1)
                    g.tensor_tensor(tile(i), tile(i), bias, ALU.add).then_inc(ln_done, 1)

            load_ln(ln1_g[0], ln1_b[0])
            drained(pool, jobs["ws", 1])
            g.affine_select(out=WCT, in_=WCT, compare_op=ALU.is_ge, fill=0.0, base=0,
                            pattern=[[0, 8], [1, P]], channel_multiplier=-1).then_inc(wct_ready, 1)
            add_ln_bias(LN["v"], lambda i: V[:, i, :], VNB)

            for l in range(DEPTH):
                if l == 1:
                    for i in range(NT):
                        rstds[0] += 1
                        pool.wait_ge(var_ready, rstds[0])
                        link(g.tensor_scalar(ss[:, i:i + 1], ss[:, i:i + 1], 1.0 / LAT, RMS_EPS, ALU.mult, ALU.add))
                        g.tensor_tensor(ss[:, i:i + 1], ss[:, i:i + 1], minus_half[:], ALU.pow).then_inc(rstd_ready, 1)
                    g.memset(SEL[0], 0.0).then_inc(chain_p, 1)
                    links[0] += 1
                    pool.wait_ge(chain_p, links[0])
                    g.affine_select(out=SEL[0], in_=SEL[0], compare_op=ALU.is_ge, fill=-BIG, base=0,
                                    pattern=[[-1, P]], channel_multiplier=1).then_inc(sel_mask, 1)
                    for qt in range(1, NT):
                        pool.wait_ge(rl_used, IH * qt)
                        own = SEL[qt][:, qt * P:]
                        g.affine_select(out=own, in_=own, compare_op=ALU.is_ge, fill=-BIG, base=0,
                                        pattern=[[-1, P]], channel_multiplier=1).then_inc(sel_mask, 1)
                pool.wait_ge(lnp_loaded, 32 * LNP[l, 1])
                add_ln_bias(LN[l, 1], lambda i: X[:, i, :], LNB[:])
                for s in range(RING):
                    g.memset(XG[s], 0.0).then_inc(xg_zero, 1)
                pool.wait_ge(ln_done, LN[l, 1] + NT)
                load_ln(ln2_g[l], ln2_b[l])
                pool.wait_ge(xg_zero, RING * (l + 1))
                pool.wait_ge(rows_stored, 16 * NT * (l + 1))
                pool.wait_ge(units_ready, l + 1)

                def gather(col, s, done):
                    pool.indirect_dma_start(XG[s][0:BLK, :], None, x_rows,
                                            bass.IndirectOffsetOnAxis(ap=col, axis=0),
                                            bounds_check=last_tok, oob_is_err=False).then_inc(done, 16)

                def scatter(col, src, done):
                    pool.indirect_dma_start(y_rows, bass.IndirectOffsetOnAxis(ap=col, axis=0),
                                            src[0:BLK, :], None,
                                            bounds_check=last_row, oob_is_err=False).then_inc(done, 16)

                for s in range(RING):
                    gather(idx_tok[:, s:s + 1], s, xg_full[s])

                def blocks(it, last):
                    static = isinstance(it, int)
                    num = (lambda a: a) if static else pool.snap
                    for j in range(RING):
                        turn = num(it * RING + (j + 1))
                        copies = it * (2 * RING) + 2 * j
                        column = (lambda e: slice(e, e + 1)) if static else (lambda e: bass.ds(e, 1))
                        if not last:
                            pool.wait_ge(xg_used[l], turn)
                            pool.sem_inc(passed, 1)
                            g.tensor_copy(stg[:, j:j + 1], idx_tok[:, column(num(it * RING + (RING + j)))]).then_inc(staged[l], 1)
                            pool.wait_ge(staged[l], num(copies + 1))
                            pool.sem_inc(passed, 1)
                            gather(stg[:, j:j + 1], j, xg_full[j])
                        pool.wait_ge(yo_a[l], turn)
                        pool.wait_ge(yo_v[l], turn)
                        pool.sem_inc(passed, 1)
                        g.tensor_copy(sts[:, j:j + 1], idx_row[:, column(num(it * RING + j))]).then_inc(staged[l], 1)
                        pool.wait_ge(staged[l], copies - j + 1 if last else num(copies + 2))
                        pool.sem_inc(passed, 1)
                        scatter(sts[:, j:j + 1], YO[j], sc_done[j])

                blocks(0, False)
                with pool.Fori(1, NE // RING - 1) as it:
                    blocks(it, False)
                blocks(NE // RING - 1, True)
                for s in range(RING):
                    pool.wait_ge(sc_done[s], 16 * NE // RING * (l + 1))
                further = pool.value_load(meta[0:1, NOV:NOV + 1], min_val=0, max_val=NOV)
                with pool.If(further > 0):
                    pool.sem_inc(ov_free[l], 1)
                    with pool.Fori(0, NOV) as u:
                        with pool.If(u < further):
                            turn = pool.snap(u + 1)
                            landed = pool.snap(u * 16 + 16)
                            outputs = pool.snap(u * 2 + 2)
                            staged_n = pool.snap(u * 2 + (2 * NE - RING + 2))
                            g.tensor_copy(stg[:, 0:1], idx_tok[:, bass.ds(u + NE, 1)]).then_inc(staged[l], 1)
                            g.tensor_copy(sts[:, 0:1], idx_row[:, bass.ds(u + NE, 1)]).then_inc(staged[l], 1)
                            pool.wait_ge(staged[l], staged_n)
                            pool.sem_inc(passed, 1)
                            gather(stg[:, 0:1], 0, ov_g[l])
                            pool.wait_ge(ov_e[l], outputs)
                            pool.sem_inc(passed, 1)
                            scatter(sts[:, 0:1], OYO, ov_d[l])
                            pool.wait_ge(ov_d[l], landed)
                            pool.sem_inc(ov_free[l], 1)
                        pool.nop()
                pool.sem_inc(moe_done[l], 1)

                pool.wait_ge(lnp_loaded, 32 * LNP[l, 2])
                for i in range(NT + 1):
                    if i < NT:
                        add_ln_bias(LN[l, 2], lambda i: X[:, i, :], LNB[:], [i])
                    for n in range(NB) if i else ():
                        pool.wait_ge(job_v, jobs["pp", l, i - 1, n].nth)
                        xs = X[:, i - 1, n * BANK:(n + 1) * BANK]
                        g.tensor_tensor(xs, xs, GT[((l * NT + i - 1) * NB + n) % 4], ALU.add).then_inc(ple_done, 1)
                if l == 0:
                    pool.wait_ge(ln_done, LN[l, 2] + NT)
                    load_ln(ln1_g[1], ln1_b[1])

        @block.scalar
        def _(act):
            s = nc.scalar

            for dst, src in ((BINV, a_b_in[0, D:2 * D]), (BINU, a_b_in[0, 0:D]), (VNG, a_vn_g[0]), (VNB, a_vn_b[0])):
                act.dma_start(dst, src.partition_broadcast(P)).then_inc(gm_loaded, 16)
            act.dma_start(WS, a_w_s[0].rearrange("g t s -> t g s")).then_inc(gm_loaded, 16)
            act.dma_start(BS, a_b_s[0].rearrange("g t -> t g"), allow_slow_non_contiguous=True).then_inc(gm_loaded, 16)

            def load_router(l):
                act.dma_start(rw[:, :, 0:NG], r_wg[l].rearrange(FLAT, p=P), allow_slow_non_contiguous=True).then_inc(rw_loaded, 16)
                act.dma_start(rw[:, :, NG:], r_we[l].rearrange(FLAT, p=P)).then_inc(rw_loaded, 16)
                act.dma_start(rb[:, 0:NG], r_bg[l].partition_broadcast(P)).then_inc(rw_loaded, 16)
                act.dma_start(rb[:, NG:], r_be[l].partition_broadcast(P)).then_inc(rw_loaded, 16)

            load_router(0)

            def take(job):
                act.wait_ge(job_done, job.n + 1)
                return ps[:, job.bank, :]

            def copy_job(dst, *name, scale=None):
                job = jobs[name]
                src = take(job)
                if len(dst.shape) == 3:
                    src = src.rearrange("p (a b) -> p a b", a=dst.shape[1])
                if scale is None:
                    s.activation(dst, src, ACT.Copy).then_inc(job_a, 1)
                else:
                    s.activation(dst, src, ACT.Copy, scale=scale).then_inc(job_a, 1)

            def take_transposed(name, i, dst):
                n = TR[name, i]
                act.wait_ge(tr_ps, 2 * n + 1)
                src = ps[:, 2 * (n % 2), :].rearrange("p (a b) -> p a b", a=4)
                s.activation(dst[:, 0:4, i * P:(i + 1) * P], src, ACT.Copy).then_inc(tr_a, 1)

            for i in range(NT):
                take_transposed("x0", i, XTv)
            for q in range(2):
                copy_job(WCT[:, 4 * q:4 * q + 4, :], "ws", q)
            for w in range(4):
                area, n = (V, U)[w // 2], w % 2
                for i in range(NT):
                    act.wait_ge(job_v, jobs["in", w, i].nth)
                    z = area[:, i, n * BANK:(n + 1) * BANK]
                    s.activation(z, z, ACT.Gelu).then_inc(z_done, 1)
            for i in range(NT):
                take_transposed("gated", i, AT)

            for l in range(DEPTH):
                if l == 1:
                    act.dma_start(KVG, b_kv_g[0].partition_broadcast(P)).then_inc(kvg_loaded, 16)
                    for q in range(4):
                        copy_job(UKT[:, 2 * q:2 * q + 2, :], "uk", q)
                    copy_job(KIT, "ki")
                    for i in range(NT):
                        job = jobs["ck", i]
                        src = take(job)
                        s.activation(JUNK[:, i, :], src[:, 0:LAT], ACT.Square, accum_out=ss[:, i:i + 1]).then_inc(var_ready, 1)
                    for b in range(4):
                        copy_job(QIT[:, b, :], "qi", b)
                    n = 0
                    for qt in range(1, NT):
                        for h in range(IH):
                            nk = (qt + 1) * P
                            src = take(jobs["ix", qt, h])
                            if n >= 2:
                                act.wait_ge(rl_used, n - 1)
                            s.activation(RL[:, n % 2, 0:nk], src[:, 0:nk], ACT.Relu).then_inc(job_a, 1)
                            n += 1
                    for cc in range(2):
                        copy_job(CKT[:, cc, :], "ct", cc)
                    for h in range(HEADS):
                        copy_job(AT[:, h, :], "q", h)
                    act.wait_ge(rl_used, n)
                    for h in range(HEADS):
                        for cc in range(2):
                            copy_job(QL[h][:, cc, :], "ql", h, cc, scale=float(HD) ** -0.5)
                    for u, (qt, hg) in enumerate(UNITS):
                        nk = (qt + 1) * P
                        for j in range(4):
                            act.wait_ge(lg_max, u + 1)
                            s.activation(PR[:, j, 0:nk], PR[:, j, 0:nk], ACT.Exp, bias=nmx[:, j:j + 1],
                                         accum_out=rs[:, j:j + 1]).then_inc(p_exp, 1)
                        for kt in range(1, qt + 1, 2):
                            copy_job(PT[:, kt, :], "tr", u, kt)
                        copy_job(OL[:, 0, :], "pv", u, 0)
                        copy_job(AT[:, 4 * hg:4 * hg + 4, qt * P:(qt + 1) * P], "uv", u)

                for i in range(NT):
                    act.wait_ge(ln_done, LN[l, 1] + i + 1)
                    act.dma_start(x_rows[i * P:(i + 1) * P, :], X[:, i, :]).then_inc(rows_stored, 16)
                    take_transposed("x1a" if l == 0 else "x1b", i, XTv)
                act.dma_start(PIN, p[l, 0].rearrange("(i p) n -> p i n", p=P)).then_inc(ple_in, 16)
                act.dma_start(GBB, ple_gb[l].partition_broadcast(P)).then_inc(ple_in, 16)
                act.wait_ge(gate_in, l + 1)
                s.activation(gexp, gexp, ACT.Exp).then_inc(gate_exp, 1)
                s.activation(dexp, dexp, ACT.Exp).then_inc(gate_exp, 1)

                def transposed(turn, k):
                    act.wait_ge(xg_used[l], turn)
                    s.activation(XGT[k], ps[:, k, :].rearrange("p (a b) -> p a b", a=KD), ACT.Copy).then_inc(xgt_ready[l], 1)

                def copy_hidden(k):
                    return s.activation(HS[k], ps[:, 2 + k, 0:FF], ACT.Copy)

                def silu(k):
                    return s.activation(SA[k], ps[:, 2 + k, FF:2 * FF].rearrange("p (a b) -> p a b", a=2)[:, :, 0:BLK], ACT.Silu)

                def halves(turn, k, slot, scattered):
                    act.wait_ge(wb_used, turn)
                    if scattered is not None:
                        act.wait_ge(sc_done[slot], scattered)
                    s.activation(YO[slot][0:BLK, 0:BANK], ps[0:BLK, 4 + 2 * k, :], ACT.Copy).then_inc(yo_a[l], 1)

                def blocks(it):
                    static = isinstance(it, int)
                    num = (lambda v: v) if static else act.snap
                    for j in range(RING):
                        first = static and it == 0
                        last = static and it == NE // RING - 1 and j == RING - 1
                        k = j % 2
                        product = num(it * RING + (l * NE + j + 1))
                        turned = num(it * RING + (j + 1))
                        nxt = num(it * RING + (j + 2))
                        wb_turn = num(it * RING + (l * NE + j))
                        scattered = None if first else num(it * 16 + 16 * (l * NE // RING - (j == 0)))
                        act.wait_ge(wa_used, product)
                        copy_hidden(k).then_inc(hs_ready[l], 1)
                        if not last:
                            transposed(nxt, 1 - k)
                        act.wait_ge(hs_ps[l], turned)
                        silu(k).then_inc(sa_ready[l], 1)
                        if not (first and j == 0):
                            halves(wb_turn, 1 - k, (j - 1) % RING, scattered)

                transposed(1, 0)
                blocks(0)
                with act.Fori(1, NE // RING - 1) as it:
                    blocks(it)
                blocks(NE // RING - 1)
                halves((l + 1) * NE, 1, RING - 1, 16 * ((l + 1) * NE // RING - 1))

                further = act.value_load(meta[0:1, NOV:NOV + 1], min_val=0, max_val=NOV)
                with act.If(further > 0):
                    with act.Fori(0, NOV) as u:
                        with act.If(u < further):
                            turn = act.snap(u + 1)
                            turned = act.snap(u + (NE + 1))
                            act.wait_ge(ov_t[l], turn)
                            s.activation(XGT[0], ps[:, 0, :].rearrange("p (a b) -> p a b", a=KD), ACT.Copy).then_inc(ov_x[l], 1)
                            act.wait_ge(ov_h[l], turn)
                            copy_hidden(0).then_inc(hs_ready[l], 1)
                            act.wait_ge(hs_ps[l], turned)
                            silu(0).then_inc(ov_s[l], 1)
                            act.wait_ge(ov_y[l], turn)
                            for n in range(NB):
                                s.activation(OYO[0:BLK, n * BANK:(n + 1) * BANK], ps[n * BLK:(n + 1) * BLK, 4 + n, :],
                                             ACT.Copy).then_inc(ov_e[l], 1)
                        act.nop()

                act.wait_ge(moe_done[l], 1)
                y_view = y_rows.rearrange("(k t) d -> t k d", k=2)

                def load_rr(i):
                    n = l * NT + i
                    if i >= 2:
                        act.wait_ge(rr_used, n - 1)
                    act.dma_start(RR[i % 2], y_view[i * P:(i + 1) * P]).then_inc(rr_full[i % 2], 16)

                def scale_rr(i):
                    act.wait_ge(rr_full[i % 2], 16 * (l * NT // 2 + i // 2 + 1))
                    r1 = RR[i % 2][:, 0, :]
                    s.activation(r1, r1, ACT.Copy, scale=gates[:, 0, i:i + 1]).then_inc(rr_scaled, 1)

                load_rr(0)
                load_rr(1)
                for cc in range(2):
                    copy_job(PTT[:, cc, :], "pt", l, cc)
                scale_rr(0)
                scale_rr(1)
                for i in range(NT):
                    take_transposed("x2a" if l == 0 else "x2b", i, XTv)
                    for n in range(NB):
                        q = (l * NT + i) * NB + n
                        act.wait_ge(job_v, jobs["g", l, i, n].nth)
                        s.activation(GT[q % 4], GT[q % 4], ACT.Sigmoid).then_inc(g_sig, 1)
                    if i + 2 < NT:
                        load_rr(i + 2)
                        scale_rr(i + 2)
                    if l == 0 and i:
                        take_transposed("x3a", i - 1, XTv)
                if l == 0:
                    take_transposed("x3a", NT - 1, XTv)
                    load_router(1)

        def attention(pe, open_job, need_wa, need_wb, product, need_xt):
            mm = nc.tensor.matmul
            need_wb(WB_UK)
            flat = wbh[WB_UK % RING]
            for q in range(4):
                bank = open_job("uk", q)
                for b in range(4):
                    last = nc.tensor.transpose(bank[:, b * P:(b + 1) * P], flat[:, 4 * q + b, :], ident[:])
                last.then_inc(job_done, 1)
            for i in range(NT):
                need_xt("x3a", i)
            tile = need_wa(WA_HEAD[1])
            product(open_job("ki"), lambda k: tile[:, k, LAT:LAT + 2 * ID], lambda k: XTv[:, k, :], T).then_inc(job_done, 1)
            for i in range(NT):
                bank = open_job("ck", i)
                product(bank, lambda k: XTv[:, k, i * P:(i + 1) * P], lambda k: tile[:, k, 0:LAT], LAT)
                product(bank[:, LAT:LAT + IH], lambda k: XTv[:, k, i * P:(i + 1) * P],
                        lambda k: tile[:, k, LAT + 2 * ID:LAT + 2 * ID + IH], IH).then_inc(job_done, 1)
            tile = need_wa(WA_HEAD[1] + 1)
            for b in range(4):
                product(open_job("qi", b), lambda k: tile[:, k, b * P:(b + 1) * P], lambda k: XTv[:, k, :], T).then_inc(job_done, 1)
            drained(pe, jobs["qi", 3])
            for qt in range(1, NT):
                nk = (qt + 1) * P
                for h in range(IH):
                    o = ID * (h % 2)
                    mm(open_job("ix", qt, h)[:, 0:nk], QIT[o:o + ID, h // 2, qt * P:(qt + 1) * P],
                       KIT[o:o + ID, 0:nk], start=True, stop=True).then_inc(job_done, 1)
            drained(pe, jobs["ck", NT - 1])
            for cc in range(2):
                bank = open_job("ct", cc)
                for i in range(NT):
                    last = nc.tensor.transpose(bank[:, i * P:(i + 1) * P], CK[:, i, cc * P:(cc + 1) * P], ident[:])
                last.then_inc(job_done, 1)
            for h in range(HEADS):
                tile = need_wa(WA_HEAD[1] + 2 + h // 4)
                product(open_job("q", h), lambda k: tile[:, k, (h % 4) * HD:(h % 4 + 1) * HD],
                        lambda k: XTv[:, k, :], T).then_inc(job_done, 1)
            for h in range(HEADS):
                drained(pe, jobs["q", h])
                for cc in range(2):
                    mm(open_job("ql", h, cc), UKT[:, h, cc * P:(cc + 1) * P], AT[:, h, :],
                       start=True, stop=True).then_inc(job_done, 1)
            drained(pe, jobs["ql", HEADS - 1, 1])

            def logits(u):
                qt, hg = UNITS[u]
                nk = (qt + 1) * P
                for j in range(4):
                    if u:
                        pe.wait_ge(lg_read, 4 * (u - 1) + j + 1)
                    for cc in range(2):
                        last = mm(ps[:, j, 0:nk], QL[4 * hg + j][:, cc, qt * P:(qt + 1) * P], CKT[:, cc, 0:nk],
                                  start=(cc == 0), stop=(cc == 1))
                    last.then_inc(lg_ps, 1)

            need_wb(WB_UV)
            uv = wbh[WB_UV % RING]
            logits(0)
            for u, (qt, hg) in enumerate(UNITS):
                if u + 1 < len(UNITS):
                    logits(u + 1)
                pe.wait_ge(p_norm, 4 * (u + 1))
                for kt in range(qt + 1):
                    bank = open_job("tr", u, kt)
                    for j in range(4):
                        last = nc.tensor.transpose(bank[:, j * P:(j + 1) * P], PR[:, j, kt * P:(kt + 1) * P], ident[:])
                    last.then_inc(job_done, 1)
                for cc in range(2):
                    bank = open_job("pv", u, cc)
                    for kt in range(qt + 1):
                        if cc == 0:
                            drained(pe, jobs["tr", u, kt])
                        last = mm(bank, CK[:, kt, cc * P:(cc + 1) * P], PT[:, kt, :], start=(kt == 0), stop=(kt == qt))
                    last.then_inc(job_done, 1)
                bank = open_job("uv", u)
                for cc in range(2):
                    drained(pe, jobs["pv", u, cc])
                for j in range(4):
                    for cc in range(2):
                        last = mm(bank[:, j * P:(j + 1) * P], uv[:, 2 * (4 * hg + j) + cc, :], OL[:, cc, j * P:(j + 1) * P],
                                  start=(cc == 0), stop=(cc == 1))
                last.then_inc(job_done, 1)
            drained(pe, jobs["uv", len(UNITS) - 1])

        @block.tensor
        def _(pe):
            mm = nc.tensor.matmul

            def open_job(*name):
                job = jobs[name]
                if job.n >= 4:
                    drained(pe, jobs.order[job.n - 4])
                return ps[:, job.bank, :]

            def transpose_tile(name, i, src):
                n = TR[name, i]
                if n >= 2:
                    pe.wait_ge(tr_a, n - 1)
                    pe.wait_ge(tr_v, n - 1)
                for h in range(2):
                    for b in range(4):
                        k = 4 * h + b
                        last = nc.tensor.transpose(ps[:, 2 * (n % 2) + h, b * P:(b + 1) * P],
                                                   src[:, k * P:(k + 1) * P], ident[:])
                    last.then_inc(tr_ps, 1)

            def need_wa(n):
                pe.wait_ge(wa_full[n % RING], wa_turn(n))
                return wa[n % RING]

            def need_wb(n):
                pe.wait_ge(wb_full[n % RING], 16 * (n // RING + 1))
                return wb[n % RING]

            def product(bank, left, right, w):
                for k in range(KD):
                    last = mm(bank[:, 0:w], left(k), right(k), start=(k == 0), stop=(k == KD - 1))
                return last

            def need_xt(name, i):
                pe.wait_ge(tr_a, TR[name, i] + 1)
                pe.wait_ge(tr_v, TR[name, i] + 1)

            pe.wait_ge(consts_ready, 1)
            pe.wait_ge(x_loaded, 16 * NT)
            for i in range(NT):
                transpose_tile("x0", i, X[:, i, :])
            pe.wait_ge(gm_loaded, 16 * 6)
            for q in range(2):
                bank = open_job("ws", q)
                for b in range(4):
                    last = nc.tensor.transpose(bank[:, b * P:(b + 1) * P], WS[:, 4 * q + b, :], ident[:])
                last.then_inc(job_done, 1)
            for w in range(4):
                tile = need_wa(w)
                for i in range(NT):
                    if w == 0:
                        need_xt("x0", i)
                    bank = open_job("in", w, i)
                    product(bank, lambda k: XTv[:, k, i * P:(i + 1) * P], lambda k: tile[:, k, :], BANK).then_inc(job_done, 1)
            pe.wait_ge(ln_done, NT)
            pe.wait_ge(wct_ready, 1)
            for g in range(8):
                bank = open_job("sp", g)
                mm(bank.rearrange("p (c d) -> p c d", c=NT), WCT[:, g, :], V[:, :, g * P:(g + 1) * P],
                   start=True, stop=True).then_inc(job_done, 1)
            drained(pe, jobs["sp", 7])
            for i in range(NT):
                transpose_tile("gated", i, U[:, i, :])

            for l in range(DEPTH):
                if l == 1:
                    attention(pe, open_job, need_wa, need_wb, product, need_xt)
                else:
                    for i in range(NT):
                        need_xt("gated", i)

                tiles = [need_wa(WA_HEAD[l] + 4 + n) for n in range(NB)]
                pe.wait_ge(rw_loaded, 64 * (l + 1))
                name = "x1a" if l == 0 else "x1b"
                for step in range(NT + 1):
                    if step < NT:
                        for n in range(NB):
                            bank = open_job("out", l, step, n)
                            product(bank, lambda k: AT[:, k, step * P:(step + 1) * P],
                                    lambda k: tiles[n][:, k, :], BANK).then_inc(job_done, 1)
                    if step:
                        i = step - 1
                        pe.wait_ge(ln_done, LN[l, 1] + i + 1)
                        transpose_tile(name, i, X[:, i, :])
                        need_xt(name, i)
                        bank = open_job("rt", l, i)
                        product(bank, lambda k: XTv[:, k, i * P:(i + 1) * P], lambda k: rw[:, k, :], NG + NE).then_inc(job_done, 1)

                drained(pe, jobs["rt", l, NT - 1])
                pe.wait_ge(picks, l + 1)
                cum, cnt = ps[:, 4, 0:NT * NE], ps[:, 5, 0:NE]
                for i in range(NT):
                    for j in range(i):
                        mm(cum[:, i * NE:(i + 1) * NE], ones[:], MB[:, j, :], start=(j == 0), stop=False)
                    mm(cum[:, i * NE:(i + 1) * NE], strict[:], MB[:, i, :], start=(i == 0), stop=True)
                for j in range(NT):
                    last = mm(cnt, ones[:], MB[:, j, :], start=(j == 0), stop=(j == NT - 1))
                last.then_inc(ranked, 1)
                pe.wait_ge(coded, l + 1)
                for q in range(2 * NT):
                    last = mm(ps[0:BLK, 6, 0:NU], RSH[:, q, :], UVH[:, q, :], start=(q == 0), stop=(q == 2 * NT - 1))
                last.then_inc(unit_ps, 1)

                def transposes(slot, k):
                    for b in range(KD):
                        n = P if b == 0 else BLK
                        last = nc.tensor.transpose(ps[:, k, b * BLK:b * BLK + n], XG[slot][0:n, b * P:(b + 1) * P],
                                                   ident[0:n, 0:n])
                    return last

                def products_in(k, tile):
                    for c in range(KD):
                        for n in range(2):
                            last = mm(ps[n * BLK:(n + 1) * BLK, 2 + k, 0:FF], XGT[k][:, c, :], tile[:, c, n * FF:(n + 1) * FF],
                                      start=(c == 0), stop=(c == KD - 1))
                    return last

                def turn_hidden(k):
                    for c in range(2):
                        last = nc.tensor.transpose(ps[:, 2 + k, FF + c * P:FF + (c + 1) * P], HS[k][:, c * P:(c + 1) * P], ident[:])
                    return last

                def products_out(k, tile):
                    for c in range(2):
                        for n in range(NB):
                            last = mm(ps[n * BLK:(n + 1) * BLK, 4 + 2 * k + n, :], HT[k][:, c, :],
                                      tile[:, c, n * BANK:(n + 1) * BANK], start=(c == 0), stop=(c == 1))
                    return last

                def out_block(b, k, s):
                    ht, full, free = b
                    pe.wait_ge(wb_full[s], full)
                    if free is not None:
                        pe.wait_ge(yo_a[l], free)
                        pe.wait_ge(yo_v[l], free)
                    pe.wait_ge(ht_ready[l], ht)
                    products_out(k, wb[s]).then_inc(wb_used, 1)

                def blocks(it):
                    static = isinstance(it, int)
                    num = (lambda v: v) if static else pe.snap
                    for j in range(RING):
                        first = static and it == 0
                        last = static and it == NE // RING - 1 and j == RING - 1
                        k = j % 2
                        na, nb = WA_E[l] + j, WB_E[l] + j - 1
                        full_a = num(it * 16 + wa_turn(na))
                        full_b = num(it * 16 + 16 * (nb // RING + 1))
                        e1 = num(it * RING + (j + 1))
                        e0 = None if first and j == 0 else num(it * RING + j)
                        em = None if first and j < 2 else num(it * RING + (j - 1))
                        emm = None if first and j < 3 else num(it * RING + (j - 2))
                        rows = num(it * 16 + 16 * (l * NE // RING + (j + 1) // RING + 1))
                        pe.wait_ge(wa_full[na % RING], full_a)
                        if em is not None:
                            pe.wait_ge(ht_ready[l], em)
                        pe.wait_ge(xgt_ready[l], e1)
                        products_in(k, wa[na % RING]).then_inc(wa_used, 1)
                        if not last:
                            pe.wait_ge(xg_full[(j + 1) % RING], rows)
                            transposes((j + 1) % RING, 1 - k).then_inc(xg_used[l], 1)
                        pe.wait_ge(hs_ready[l], e1)
                        turn_hidden(k).then_inc(hs_ps[l], 1)
                        if e0 is not None:
                            out_block((e0, full_b, emm), 1 - k, nb % RING)

                pe.wait_ge(xg_full[0], 16 * (l * NE // RING + 1))
                transposes(0, 0).then_inc(xg_used[l], 1)
                blocks(0)
                with pe.Fori(1, NE // RING - 1) as it:
                    blocks(it)
                blocks(NE // RING - 1)
                nb = WB_E[l] + NE - 1
                out_block((NE, 16 * (nb // RING + 1), NE - 2), 1, nb % RING)

                further = pe.value_load(meta[0:1, NOV:NOV + 1], min_val=0, max_val=NOV)
                with pe.If(further > 0):
                    with pe.Fori(0, NOV) as u:
                        with pe.If(u < further):
                            turn = pe.snap(u + 1)
                            copied = pe.snap(u + (NE + 1))
                            rows = pe.snap(u * 16 + 16)
                            weights = pe.snap(u * 32 + 32)
                            pe.wait_ge(ov_g[l], rows)
                            transposes(0, 0).then_inc(ov_t[l], 1)
                            pe.wait_ge(ov_w[l], weights)
                            pe.wait_ge(ov_x[l], turn)
                            products_in(0, OWA).then_inc(ov_h[l], 1)
                            pe.wait_ge(hs_ready[l], copied)
                            turn_hidden(0).then_inc(hs_ps[l], 1)
                            pe.wait_ge(ov_m[l], turn)
                            products_out(0, OWB).then_inc(ov_y[l], 1)
                        pe.nop()
                pe.wait_ge(moe_done[l], 1)

                pe.wait_ge(ple_in, 32 * (l + 1))
                for cc in range(2):
                    bank = open_job("pt", l, cc)
                    for i in range(NT):
                        last = nc.tensor.transpose(bank[:, i * P:(i + 1) * P], PIN[:, i, cc * P:(cc + 1) * P], ident[:])
                    last.then_inc(job_done, 1)
                tiles = [need_wa(WA_GW[l] + n) for n in range(NB)]
                ple_tile = need_wb(WB_PLE[l])
                drained(pe, jobs["pt", l, 1])
                name = "x2a" if l == 0 else "x2b"

                def next_layer(i):
                    pe.wait_ge(ple_done, NB * (i + 1))
                    transpose_tile("x3a", i, X[:, i, :])

                for i in range(NT):
                    pe.wait_ge(ln_done, LN[l, 2] + i + 1)
                    transpose_tile(name, i, X[:, i, :])
                    need_xt(name, i)
                    for n in range(NB):
                        bank = open_job("g", l, i, n)
                        product(bank, lambda k: XTv[:, k, i * P:(i + 1) * P], lambda k: tiles[n][:, k, :], BANK).then_inc(job_done, 1)
                    for n in range(NB):
                        bank = open_job("pp", l, i, n)
                        for c in range(2):
                            last = mm(bank, PTT[:, c, i * P:(i + 1) * P], ple_tile[:, c, n * BANK:(n + 1) * BANK],
                                      start=(c == 0), stop=(c == 1))
                        last.then_inc(job_done, 1)
                    if l == 0 and i:
                        next_layer(i - 1)
                if l == 0:
                    next_layer(NT - 1)

        def attention_v(dve, v, link, take):
            dve.wait_ge(kvg_loaded, 16)
            for i in range(NT):
                src = take("ck", i)
                norms[0] += 1
                dve.wait_ge(rstd_ready, norms[0])
                v.tensor_scalar(WI[:, i, :], src[:, LAT:LAT + IH], float(IH * ID) ** -0.5, None, ALU.mult)
                v.scalar_tensor_tensor(CK[:, i, :], src[:, 0:LAT], ss[:, i:i + 1], KVG, ALU.mult, ALU.mult).then_inc(job_v, 1)
            dve.wait_ge(job_v, jobs["ck", NT - 1].nth)
            n = 0
            for qt in range(1, NT):
                for h in range(IH):
                    dve.wait_ge(job_a, jobs["ix", qt, h].nth)
                    r, w = RL[:, n % 2, 0:(qt + 1) * P], WI[:, qt, h:h + 1]
                    if h == 0:
                        last = v.tensor_scalar(SEL[qt], r, w, None, ALU.mult)
                    else:
                        last = v.scalar_tensor_tensor(SEL[qt], r, w, SEL[qt], ALU.mult, ALU.add)
                    last.then_inc(rl_used, 1)
                    n += 1
                    dve.wait_ge(rl_used, n)
            for qt in range(1, NT):
                dve.wait_ge(sel_mask, qt + 1)
                for _ in range(TOPK // 8):
                    link(v.max(m8[:], SEL[qt]))
                    link(v.match_replace(SEL[qt], m8[:], SEL[qt], TAKEN))
                link(v.tensor_scalar(SEL[qt], SEL[qt], TAKEN / 10, -BIG, ALU.is_gt, ALU.mult))
            for u, (qt, hg) in enumerate(UNITS):
                nk = (qt + 1) * P
                if u:
                    dve.wait_ge(job_done, jobs["tr", u - 1, UNITS[u - 1][0]].n + 1)
                for j in range(4):
                    dve.wait_ge(lg_ps, 4 * u + j + 1)
                    v.tensor_tensor_reduce(PR[:, j, 0:nk], ps[:, j, 0:nk], SEL[qt], 1.0, TAKEN, ALU.add, ALU.max,
                                           mx[:, j:j + 1]).then_inc(lg_read, 1)
                dve.wait_ge(lg_read, 4 * (u + 1))
                v.tensor_scalar(nmx[:], mx[:], -1.0, None, ALU.mult).then_inc(lg_max, 1)
                dve.wait_ge(p_exp, 4 * (u + 1))
                link(v.reciprocal(rc[:], rs[:]))
                for j in range(4):
                    v.tensor_scalar(PR[:, j, 0:nk], PR[:, j, 0:nk], rc[:, j:j + 1], None, ALU.mult).then_inc(p_norm, 1)
                for kt in range(0, qt + 1, 2):
                    v.tensor_copy(PT[:, kt, :], take("tr", u, kt)).then_inc(job_v, 1)
                v.tensor_copy(OL[:, 1, :], take("pv", u, 1)).then_inc(job_v, 1)

        def route(dve, v, link, l):
            tt, ts, red = v.tensor_tensor, v.tensor_scalar, v.tensor_reduce

            def over(a, n):
                return a.unsqueeze(len(a.shape)).broadcast_to(list(a.shape) + [n])

            def pick(dst, vals, top, work, rank_of, n):
                link(tt(work, vals, over(top, n), ALU.is_equal))
                link(tt(work, work, rank_of.unsqueeze(1).broadcast_to([P, NT, n]), ALU.mult))
                link(red(key, work, AX.X, ALU.max))
                link(tt(dst, work, over(key, n), ALU.is_equal))

            g, e = LG[:, :, 0:NG], LG[:, :, NG:]
            link(red(gmax, g, AX.X, ALU.max))
            pick(gsel, g, gmax, geq, rev[:, NE - NG:], NG)
            tt(gexp, g, over(gmax, NG), ALU.subtract)
            link(ts(pen, gsel, BIG, -BIG, ALU.mult, ALU.add))
            grouped = em.rearrange("p t (g e) -> p t g e", g=NG)
            for i in range(NT):
                tt(grouped[:, i], e[:, i].rearrange("p (g e) -> p g e", g=NG), over(gsel[:, i], EPG), ALU.mult).then_inc(chain_v, 1)
                links_v[0] += 1
            dve.wait_ge(chain_v, links_v[0])
            for i in range(NT):
                tt(grouped[:, i], grouped[:, i], over(pen[:, i], EPG), ALU.add).then_inc(chain_v, 1)
                links_v[0] += 1
            dve.wait_ge(chain_v, links_v[0])
            link(red(m1, em, AX.X, ALU.max))
            pick(EK[:, 0], em, m1, eq, rev[:], NE)
            link(v.scalar_tensor_tensor(em, EK[:, 0], -BIG, em, ALU.mult, ALU.add))
            link(red(m2, em, AX.X, ALU.max))
            pick(EK[:, 1], em, m2, eq, rev[:], NE)
            tt(MB, EK[:, 0], EK[:, 1], ALU.add).then_inc(picks, 1)
            tt(dexp, m2, m1, ALU.subtract).then_inc(gate_in, 1)
            ek = EK.rearrange("p k t e -> p (k t) e")
            ew = EW.rearrange("p k t e -> p (k t) e")

            def spread(row, n):
                return row.unsqueeze(1).broadcast_to([P, 2 * NT, n])

            link(tt(ew, ek, spread(iota[:, 0:NE], NE), ALU.mult))
            link(red(eidx, ew, AX.X, ALU.add))
            link(v.memset(one, 1.0))
            dve.wait_ge(ranked, l + 1)
            link(ts(intc, ps[:, 5, 0:NE], -1.0, 0.0, ALU.add, ALU.max))
            link(ts(intc, intc, 6, None, ALU.logical_shift_right))
            link(v.tensor_copy(extra, intc))
            link(v.tensor_tensor_scan(cin, one, extra, 0.0, ALU.mult, ALU.add))
            link(tt(cex, cin, extra, ALU.subtract))
            link(tt(ew, ek, spread(cex, NE), ALU.mult))
            link(red(base, ew, AX.X, ALU.add))
            flat = EK.rearrange("p k t e -> p k (t e)")
            link(tt(EW.rearrange("p k t e -> p k (t e)"), flat,
                    ps[:, 4, 0:NT * NE].unsqueeze(1).broadcast_to([P, 2, NT * NE]), ALU.mult))
            link(red(rank, ew, AX.X, ALU.add))
            link(v.tensor_copy(ints, rank))
            link(ts(inti, ints, 6, None, ALU.logical_shift_right))
            link(v.tensor_copy(blk, inti))
            link(ts(ints, ints, BLK - 1, None, ALU.bitwise_and))
            link(v.tensor_copy(slot, ints))
            link(tt(unit, base, blk, ALU.add))
            link(v.scalar_tensor_tensor(unit, unit, float(NE - 1), eidx, ALU.add, ALU.subtract))
            link(ts(further_blk, blk, 0.0, None, ALU.is_gt))
            link(tt(unit, unit, further_blk, ALU.mult))
            link(tt(unit, unit, eidx, ALU.add))
            link(tt(UVH, spread(iota[:, 0:NU], NU), over(unit, NU), ALU.is_equal))
            link(tt(RSH, spread(iota[:], BLK), over(slot, BLK), ALU.is_equal))
            tt(UVH, UVH, over(val[:], NU), ALU.mult).then_inc(coded, 1)
            link(tt(whose[0:1], cin[0:1].unsqueeze(1).broadcast_to([1, NOV, NE]),
                    iota[0:1, 0:NOV].unsqueeze(2).broadcast_to([1, NOV, NE]), ALU.is_le))
            link(red(owner[0:1], whose[0:1], AX.X, ALU.add))
            link(ts(meta[0:1, 0:NOV], owner[0:1], float(NE - 1), None, ALU.min))
            link(v.tensor_copy(meta[0:1, NOV:NOV + 1], cin[0:1, NE - 1:NE]))
            dve.wait_ge(gate_exp, 2 * (l + 1))
            link(red(gsum, gexp, AX.X, ALU.add))
            link(ts(den, dexp, 1.0, None, ALU.add))
            link(tt(den, den, gsum, ALU.mult))
            link(v.reciprocal(gates[:, 0, :], den))
            link(tt(gates[:, 1, :], gates[:, 0, :], dexp, ALU.mult))
            dve.wait_ge(unit_ps, l + 1)
            rows, off = rowf[0:BLK], offs[0:BLK]
            link(ts(rows, ps[0:BLK, 6, 0:NU], float(NONE), None, ALU.add))
            link(v.tensor_copy(idx_row[:], rows))
            link(ts(off, rows, float(T), -float(T), ALU.is_ge, ALU.mult))
            tt(idx_tok[:], rows, off, ALU.add).then_inc(units_ready, 1)

        @block.vector
        def _(dve):
            v = nc.vector

            def link(ins):
                links_v[0] += 1
                ins.then_inc(chain_v, 1)
                dve.wait_ge(chain_v, links_v[0])

            def take(*name):
                job = jobs[name]
                dve.wait_ge(job_done, job.n + 1)
                return ps[:, job.bank, :]

            def take_transposed(name, i, dst):
                n = TR[name, i]
                dve.wait_ge(tr_ps, 2 * n + 2)
                src = ps[:, 2 * (n % 2) + 1, :].rearrange("p (a b) -> p a b", a=4)
                v.tensor_copy(dst[:, 4:8, i * P:(i + 1) * P], src).then_inc(tr_v, 1)

            def normalize(t, gain):
                for n in range(NB):
                    last = v.bn_stats(bn[:, n, :], t[:, n * BANK:(n + 1) * BANK])
                link(last)
                v.bn_aggr(mv[:], bn[:]).then_inc(var_ready, 1)
                norms[0] += 1
                dve.wait_ge(var_ready, norms[0])
                dve.wait_ge(rstd_ready, norms[0])
                link(v.tensor_scalar(t, t, mv[:, 0:1], rstd[:], ALU.subtract, ALU.mult))
                v.tensor_tensor(t, t, gain, ALU.mult).then_inc(ln_pre, 1)

            for i in range(NT):
                take_transposed("x0", i, XTv)
            dve.wait_ge(gm_loaded, 16 * 6)

            def norm_v(i):
                dve.wait_ge(z_done, NT + i + 1)
                normalize(V[:, i, :], VNG)

            for w in range(4):
                area, bias, n = ((V, BINV), (U, BINU))[w // 2] + (w % 2,)
                cols = slice(n * BANK, (n + 1) * BANK)
                for i in range(NT):
                    v.tensor_tensor(area[:, i, cols], take("in", w, i), bias[:, cols], ALU.add).then_inc(job_v, 1)
                    if w == 1 and i:
                        norm_v(i - 1)
                    if w == 2 and i == 0:
                        norm_v(NT - 1)
            dve.wait_ge(z_done, 4 * NT)
            for g in range(8):
                us = U[:, :, g * P:(g + 1) * P]
                src = take("sp", g).rearrange("p (c d) -> p c d", c=NT)
                v.scalar_tensor_tensor(us, src, BS[:, g:g + 1], us, ALU.add, ALU.mult).then_inc(job_v, 1)
            for i in range(NT):
                take_transposed("gated", i, AT)

            for l in range(DEPTH):
                if l == 1:
                    attention_v(dve, v, link, take)
                name = "x1a" if l == 0 else "x1b"
                for step in range(NT + 1):
                    if step < NT:
                        for n in range(NB):
                            xs = X[:, step, n * BANK:(n + 1) * BANK]
                            last = v.scalar_tensor_tensor(xs, xs, ALPHA, take("out", l, step, n), ALU.mult, ALU.add)
                            last.then_inc(job_v, 1)
                        dve.wait_ge(job_v, jobs["out", l, step, NB - 1].nth)
                        if step == 0:
                            dve.wait_ge(lnp_loaded, 32 * LNP[l, 1])
                        normalize(X[:, step, :], LNG[:])
                    if step:
                        i = step - 1
                        take_transposed(name, i, XTv)
                        if i == 0:
                            dve.wait_ge(rw_loaded, 64 * (l + 1))
                        v.tensor_tensor(LG[:, i, :], take("rt", l, i)[:, 0:NG + NE], rb[:], ALU.add).then_inc(job_v, 1)
                dve.wait_ge(job_v, jobs["rt", l, NT - 1].nth)
                route(dve, v, link, l)

                def hidden(k):
                    values = ps[:, 2 + k, FF:2 * FF].rearrange("p (a b) -> p a b", a=2)[:, :, BLK:2 * BLK]
                    return v.tensor_tensor(HT[k], SA[k], values, ALU.mult)

                def half_out(k, slot):
                    return v.tensor_copy(YO[slot][0:BLK, BANK:], ps[BLK:2 * BLK, 5 + 2 * k, :])

                def blocks(it):
                    static = isinstance(it, int)
                    num = (lambda a: a) if static else dve.snap
                    for j in range(RING):
                        first = static and it == 0
                        k = j % 2
                        e1 = num(it * RING + (j + 1))
                        wb_0 = num(it * RING + (l * NE + j))
                        scattered = None if first else num(it * 16 + 16 * (l * NE // RING - (j == 0)))
                        dve.wait_ge(sa_ready[l], e1)
                        hidden(k).then_inc(ht_ready[l], 1)
                        if not (first and j == 0):
                            if scattered is not None:
                                dve.wait_ge(sc_done[(j - 1) % RING], scattered)
                            dve.wait_ge(wb_used, wb_0)
                            half_out(1 - k, (j - 1) % RING).then_inc(yo_v[l], 1)

                blocks(0)
                with dve.Fori(1, NE // RING - 1) as it:
                    blocks(it)
                blocks(NE // RING - 1)
                dve.wait_ge(sc_done[RING - 1], 16 * ((l + 1) * NE // RING - 1))
                dve.wait_ge(wb_used, (l + 1) * NE)
                half_out(1, RING - 1).then_inc(yo_v[l], 1)
                further = dve.value_load(meta[0:1, NOV:NOV + 1], min_val=0, max_val=NOV)
                with dve.If(further > 0):
                    with dve.Fori(0, NOV) as u:
                        with dve.If(u < further):
                            turn = dve.snap(u + 1)
                            dve.wait_ge(ov_s[l], turn)
                            hidden(0).then_inc(ov_m[l], 1)
                        dve.nop()

                def combine(i):
                    n = l * NT + i
                    r, t = RR[i % 2], X[:, i, :]
                    dve.wait_ge(rr_scaled, n + 1)
                    link(v.scalar_tensor_tensor(t, t, ALPHA, r[:, 0, :], ALU.mult, ALU.add))
                    last = v.scalar_tensor_tensor(t, r[:, 1, :], gates[:, 1, i:i + 1], t, ALU.mult, ALU.add)
                    last.then_inc(rr_used, 1)
                    dve.wait_ge(rr_used, n + 1)
                    if i == 0:
                        dve.wait_ge(lnp_loaded, 32 * LNP[l, 2])
                    normalize(t, LNG[:])

                combine(0)
                for i in range(NT):
                    if i + 1 < NT:
                        combine(i + 1)
                    take_transposed("x2a" if l == 0 else "x2b", i, XTv)
                    if i == 0:
                        dve.wait_ge(ple_in, 32 * (l + 1))
                    for n in range(NB):
                        q = (l * NT + i) * NB + n
                        if q >= 4:
                            dve.wait_ge(ple_done, q - 3)
                        v.tensor_tensor(GT[q % 4], take("g", l, i, n), GBB[:, n * BANK:(n + 1) * BANK], ALU.add).then_inc(job_v, 1)
                    for n in range(NB):
                        q = (l * NT + i) * NB + n
                        dve.wait_ge(g_sig, q + 1)
                        v.tensor_tensor(GT[q % 4], GT[q % 4], take("pp", l, i, n), ALU.mult).then_inc(job_v, 1)
                    if l == 0 and i:
                        take_transposed("x3a", i - 1, XTv)
                if l == 0:
                    take_transposed("x3a", NT - 1, XTv)


_INS = ["x", "p", "a_w_in", "a_b_in", "a_vn_g", "a_vn_b", "a_w_s", "a_b_s", "a_w_out", "b_w_in", "b_kv_g", "b_w_uk",
        "b_w_uv", "b_w_out", "ln1_g", "ln1_b", "ln2_g", "ln2_b", "r_wg", "r_bg", "r_we", "r_be", "e_w_in", "e_w_out",
        "ple_w", "ple_gw", "ple_gb"]


def kernel(**inputs):
    import concourse.bacc as bacc
    from concourse.bass_utils import run_bass_kernel_spmd

    nc = bacc.Bacc("TRN2", target_bir_lowering=False, num_devices=1)
    arrays, aps = {}, {}
    for name in _INS:
        a = np.ascontiguousarray(inputs[name])
        arrays[f"in_{name}"] = a
        aps[name] = nc.dram_tensor(f"in_{name}", a.shape, mybir.dt.from_np(a.dtype), kind="ExternalInput").ap()
    aps["out"] = nc.dram_tensor("out_x", (1, T, D), F32, kind="ExternalOutput").ap()
    trunk(nc, **aps)
    r = run_bass_kernel_spmd(nc, [arrays], core_ids=[0])
    return r.results[0]["out_x"]
```

```python
from contextlib import ExitStack

import numpy as np

import concourse.bass as bass
from concourse import mybir

F32 = mybir.dt.float32
BF16 = mybir.dt.bfloat16
I32 = mybir.dt.int32
U32 = mybir.dt.uint32
ALU = mybir.AluOpType
ACT = mybir.ActivationFunctionType
AX = mybir.AxisListType

P = 128
DEPTH = 2
ALPHA = (2 * DEPTH) ** 0.25
LN_EPS, RMS_EPS = 1e-5, 1e-6
BIG = 1e30
TAKEN = -3e38

T, D = 512, 1024
NT, KD, BANK = T // P, D // P, 512
NB = D // BANK
HEADS, HD, LAT = 8, 128, 256
IH, ID = 8, 64
TOPK = min(256, T // 4)
NG, EPG = 4, 8
NE = NG * EPG
ASIDE = NE - 4
STREAMED = NE - 1
FF = 256
PLE = 256
BLK = 64
NCH = T // BLK - 1
NOV = 2 * T // BLK - 1
NU = 48
NONE = 4096
GATES_AT, UNITS_AT = 2, 6
RING = 4


class Job:

    def __init__(self, n, engine, nth):
        self.n, self.bank, self.engine, self.nth = n, 4 + n % 4, engine, nth


class Jobs:

    def __init__(self):
        self.order, self.by, self.count = [], {}, {"act": 0, "dve": 0}

    def add(self, engine, *name):
        self.count[engine] += 1
        job = Job(len(self.order), engine, self.count[engine])
        self.order.append(job)
        self.by[name] = job

    def __getitem__(self, name):
        return self.by[name]


UNITS = [(qt, hg) for qt in range(NT) for hg in range(2)]


def plan_jobs():
    jobs = Jobs()
    for w in range(4):
        for i in range(NT):
            jobs.add("dve", "in", w, i)
        for q in range(2) if w == 0 else ():
            jobs.add("act", "ws", q)
    for g in range(8):
        jobs.add("dve", "sp", g)
    for l in range(DEPTH):
        if l == 1:
            for q in range(4):
                jobs.add("act", "uk", q)
            jobs.add("act", "ki")
            for i in range(NT):
                jobs.add("dve", "ck", i)
            for b in range(4):
                jobs.add("act", "qi", b)
            for qt in range(1, NT):
                for h in range(IH):
                    jobs.add("act", "ix", qt, h)
            for cc in range(2):
                jobs.add("act", "ct", cc)
            for h in range(HEADS):
                jobs.add("act", "q", h)
            for h in range(HEADS):
                for cc in range(2):
                    jobs.add("act", "ql", h, cc)
            for u, (qt, hg) in enumerate(UNITS):
                for kt in range(qt + 1):
                    jobs.add("act" if kt % 2 else "dve", "tr", u, kt)
                for cc in range(2):
                    jobs.add("dve" if cc else "act", "pv", u, cc)
                jobs.add("act", "uv", u)
        for step in range(NT + 1):
            if step < NT:
                for n in range(NB):
                    jobs.add("dve", "out", l, step, n)
            if step:
                jobs.add("dve", "rt", l, step - 1)
        for cc in range(2):
            jobs.add("act", "pt", l, cc)
        for i in range(NT):
            for n in range(NB):
                jobs.add("act", "pp", l, i, n)
        for i in range(NT):
            for n in range(NB):
                jobs.add("dve", "g", l, i, n)
    return jobs


def trunk(nc, x, p, a_w_in, a_b_in, a_vn_g, a_vn_b, a_w_s, a_b_s, a_w_out,
          b_w_in, b_kv_g, b_w_uk, b_w_uv, b_w_out, ln1_g, ln1_b, ln2_g, ln2_b,
          r_wg, r_bg, r_we, r_be, e_w_in, e_w_out, ple_w, ple_gw, ple_gb, out):
    jobs = plan_jobs()
    x_rows = nc.dram_tensor("x_rows", [T, D], F32, kind="Internal").ap()
    y_rows = nc.dram_tensor("y_rows", [2 * T, D], F32, kind="Internal").ap()

    Q0, K0, I0, KI0 = 0, HEADS * HD, HEADS * HD + LAT, HEADS * HD + LAT + IH * ID
    half = lambda w, n: [(w[:, n * BANK:(n + 1) * BANK], 0, BANK)]
    misc = [(b_w_in[0][:, K0:K0 + LAT], 0, LAT),
            (b_w_in[0][:, KI0:KI0 + ID], LAT, ID),
            (b_w_in[0][:, KI0:KI0 + ID + IH], LAT + ID, ID + IH)]
    wa_head = [
        [half(a_w_in[0], 2), half(a_w_in[0], 3), half(a_w_in[0], 0), half(a_w_in[0], 1),
         half(a_w_out[0], 0), half(a_w_out[0], 1)],
        [misc, [(b_w_in[0][:, I0:I0 + BANK], 0, BANK)], half(b_w_in[0], 0), half(b_w_in[0], 1),
         half(b_w_out[0], 0), half(b_w_out[0], 1)],
    ]
    WA_E = [6, 6 + STREAMED + 2 + 6]
    WB_E = [1, STREAMED + 4]
    WA_HEAD = [0, 6 + STREAMED + 2]
    WA_GW = [WA_E[0] + STREAMED, WA_E[1] + STREAMED]
    WB_PLE = [WB_E[0] - 1, WB_E[1] - 1]
    WB_UK, WB_UV = STREAMED + 1, STREAMED + 2
    FLAT = "(a p) n -> p a n"

    wa_last, wb_last = {}, {WB_UK: ("uk", 3), WB_UV: ("uv", len(UNITS) - 1)}
    for w in range(4):
        wa_last[w] = ("in", w, NT - 1)
    for n, name in enumerate([("ck", NT - 1), ("qi", 3), ("q", 3), ("q", 7)]):
        wa_last[WA_HEAD[1] + n] = name
    for l in range(DEPTH):
        for n in range(NB):
            wa_last[WA_HEAD[l] + 4 + n] = ("out", l, NT - 1, n)
            wa_last[WA_GW[l] + n] = ("g", l, NT - 1, n)
        wb_last[WB_PLE[l]] = ("pp", l, NT - 1, NB - 1)
    MISC = WA_HEAD[1]

    def tile_of(e):
        return e - (e > ASIDE)

    def wa_turn(n):
        extra = len(misc) - 1 if n >= MISC and n % RING == MISC % RING else 0
        return 16 * (n // RING + 1 + extra)

    ctx = ExitStack()
    with ctx:
        def sb(name, shape, dt=F32):
            return ctx.enter_context(nc.sbuf_tensor(name, shape, dt))

        def sem(name):
            return ctx.enter_context(nc.semaphore(name))

        ps = ctx.enter_context(nc.psum_tensor("ps", [P, 8, BANK], F32))
        wa = [sb(f"wa{r}", [P, KD, BANK]) for r in range(RING)]
        wb = [sb(f"wb{r}", [P, 2, D]) for r in range(RING)]
        wbh = [w[:].rearrange("p a (h d) -> p (a h) d", d=HD) for w in wb]
        X = sb("X", [P, NT, D])
        XT = sb("XT", [P, KD * T])
        A = sb("A", [P, KD * T])
        B = sb("B", [P, KD * T])
        C = sb("C", [P, 9216])
        LNG, LNB = sb("LNG", [P, D]), sb("LNB", [P, D])

        def cut(area, at, *dims):
            n = int(np.prod(dims))
            v = area[:, at:at + n]
            if len(dims) == 2:
                v = v.rearrange("p (a b) -> p a b", a=dims[0])
            if len(dims) == 3:
                v = v.rearrange("p (a b c) -> p a b c", a=dims[0], b=dims[1])
            if len(dims) == 4:
                v = v.rearrange("p (a b c d) -> p a b c d", a=dims[0], b=dims[1], c=dims[2])
            return v

        XTv, AT = cut(XT, 0, KD, T), cut(A, 0, KD, T)
        V, U = cut(A, 0, NT, D), cut(B, 0, NT, D)
        BINV, BINU, VNG, VNB = (C[:, D * n:D * (n + 1)] for n in range(4))
        WS, WCT, BS = cut(C, 4096, 8, P), cut(C, 5120, 8, P), C[:, 6144:6152]
        QIT, KIT, CK, CKT = cut(C, 0, 4, T), C[:, 2048:2560], cut(C, 2560, NT, LAT), cut(C, 3584, 2, T)
        UKT, SELS, OL, KVG = cut(C, 4608, HEADS, LAT), C[:, 6656:7936], cut(C, 7936, 2, BANK), C[:, 8960:9216]
        SEL = [SELS[:, P * (q * (q + 1) // 2):][:, :P * (q + 1)] for q in range(NT)]
        PR, PT = cut(C, 0, 4, BANK), cut(C, 4608, NT, BANK)
        RL = cut(B, 0, 2, BANK)
        JUNK = cut(B, 1024, NT, LAT)
        QL = [cut(B if h < 4 else XT, (h % 4) * 2 * T, 2, T) for h in range(HEADS)]
        LG = cut(C, 8192, NT, NG + NE)
        at = [0]

        def tmp(*dims, area=XT):
            v = cut(area, at[0], *dims)
            at[0] += int(np.prod(dims))
            return v

        gmax, gkey, gsum, m1, m2, key, dexp, den = (tmp(NT) for _ in range(8))
        geq, gsel, gexp, pen = (tmp(NT, NG) for _ in range(4))
        em, eq = tmp(NT, NE), tmp(NT, NE)
        EK, EW = tmp(2, NT, NE), tmp(2, NT, NE)
        MB = cut(XT, at[0], NT * NE // 2).bitcast(BF16).rearrange("p (a b) -> p a b", a=NT)
        at[0] += NT * NE // 2
        cex, cin, extra, one, c0 = (tmp(NE) for _ in range(5))
        rank, base, eidx, blk, slot, unit, further_blk = (tmp(2 * NT) for _ in range(7))
        ints, inti, intc = (tmp(n).bitcast(I32) for n in (2 * NT, 2 * NT, NE))
        RSH = tmp(2 * NT, BLK)
        at[0] = 7168
        UVH, whose, owner = tmp(2 * NT, NU, area=C), tmp(NOV, NE, area=C), tmp(NOV, area=C)
        rowf, offs = tmp(NU, area=C), tmp(NU, area=C)
        XG, YO = ([B[h * BLK:(h + 1) * BLK, D * s:D * (s + 1)] for s in range(RING)] for h in range(2))
        XGT = [cut(XT, 512 * s, KD, BLK) for s in range(2)]
        SA = [cut(XT, 1024 + 128 * s, 2, BLK) for s in range(2)]
        HT = [cut(XT, 1280 + 128 * s, 2, BLK) for s in range(2)]
        HS = [cut(XT, 1536 + FF * s, FF) for s in range(2)]
        OWA, OWB = cut(A, 0, KD, BANK), cut(XT, 2048, 2, D)
        RR = [[cut(wa[(WA_GW[l] + NB + i // 2) % RING][:].rearrange("p a b -> p (a b)"), (i % 2) * 2 * D, 2, D)
               for i in range(NT)] for l in range(DEPTH)]
        PIN, PTT, GBB, PP = cut(C, 0, NT, PLE), cut(C, 1024, 2, T), C[:, 2048:3072], cut(C, 3072, NT, D)
        GT = [B[:, 512 * s:512 * (s + 1)] for s in range(4)]

        ident = sb("ident", [P, P])
        strict = sb("strict", [P, P], BF16)
        ones = sb("ones", [P, P], BF16)
        iota = sb("iota", [P, BLK])
        rev = sb("rev", [P, NE])
        val = sb("val", [P, 2 * NT])
        rw = sb("rw", [P, KD, NG + NE])
        rb = sb("rb", [P, NG + NE])
        idx_tok = sb("idx_tok", [BLK, NU], U32)
        idx_row = sb("idx_row", [BLK, NU], U32)
        meta = sb("meta", [1, NOV + 1], I32)
        stg = sb("stg", [BLK, 4], U32)
        sts = sb("sts", [BLK, 4], U32)
        gates = sb("gates", [P, 2, NT])
        WI = sb("WI", [P, NT, IH])
        bn = sb("bn", [P, 2, 6])
        mv = sb("mv", [P, 2])
        rstd = sb("rstd", [P, 1])
        minus_half = sb("minus_half", [P, 1])
        m8 = sb("m8", [P, 8])
        ss = sb("ss", [P, NT])
        mx, nmx, rs, rc = (sb(n, [P, 4]) for n in ("mx", "nmx", "rs", "rc"))

        consts_ready, x_loaded, gm_loaded = sem("consts_ready"), sem("x_loaded"), sem("gm_loaded")
        wa_full = [sem(f"wa_full{r}") for r in range(RING)]
        wb_full = [sem(f"wb_full{r}") for r in range(RING)]
        wa_used, wb_used, aside_full = sem("wa_used"), sem("wb_used"), sem("aside_full")
        tr_ps, tr_a, tr_v = sem("tr_ps"), sem("tr_a"), sem("tr_v")
        job_done, job_a, job_v = sem("job_done"), sem("job_a"), sem("job_v")
        z_done = sem("z_done")
        ln_done, lnp_loaded = sem("ln_done"), sem("lnp_loaded")
        chain_v, chain_p = sem("chain_v"), sem("chain_p")
        wct_ready = sem("wct_ready")
        rw_loaded, ple_in, kvg_loaded = sem("rw_loaded"), sem("ple_in"), sem("kvg_loaded")
        rows_stored = sem("rows_stored")
        gate_in, gate_exp = sem("gate_in"), sem("gate_exp")
        picks, ranked, coded, unit_ps, units_ready = (sem(n) for n in ("picks", "ranked", "coded", "unit_ps", "units_ready"))
        xg_zero = sem("xg_zero")
        staged = [sem(f"staged{l}") for l in range(DEPTH)]
        xg_full = [sem(f"xg_full{s}") for s in range(RING)]
        sc_done = [sem(f"sc_done{s}") for s in range(RING)]
        xg_used, xgt_ready, hs_ready, hs_ps, sa_ready, ht_ready, yo_a, yo_v = (
            [sem(f"{n}{l}") for l in range(DEPTH)]
            for n in ("xg_used", "xgt_ready", "hs_ready", "hs_ps", "sa_ready", "ht_ready", "yo_a", "yo_v"))
        ov_free, ov_w, ov_g, ov_t, ov_x, ov_h, ov_s, ov_m, ov_y, ov_e, ov_d, moe_done = (
            [sem(f"{n}{l}") for l in range(DEPTH)]
            for n in ("ov_free", "ov_w", "ov_g", "ov_t", "ov_x", "ov_h", "ov_s", "ov_m", "ov_y", "ov_e", "ov_d", "moe_done"))
        rr_full = [sem(f"rr_full{i}") for i in range(NT)]
        rr_used, x_scaled = sem("rr_used"), sem("x_scaled")
        g_sig, gated, ple_done = sem("g_sig"), sem("gated"), sem("ple_done")
        var_ready, rstd_ready, rl_used, sel_mask = (sem(n) for n in ("var_ready", "rstd_ready", "rl_used", "sel_mask"))
        lg_ps, lg_read, lg_max, p_exp, p_norm = (sem(n) for n in ("lg_ps", "lg_read", "lg_max", "p_exp", "p_norm"))
        out_done = sem("out_done")
        pe_passed = sem("pe_passed")
        passed = sem("passed")

        TR = {}
        for s, name in enumerate(["x0", "gated", "x1a", "x2a", "x3a", "x1b", "x2b"]):
            for i in range(NT):
                TR[name, i] = None
        order = [("x0", i) for i in range(NT)] + [("gated", i) for i in range(NT)] + [("x1a", i) for i in range(NT)]
        ple_order = []
        ple_order.append(("x2a", 0))
        for i in range(NT):
            if i + 1 < NT:
                ple_order.append(("x2a", i + 1))
            if i:
                ple_order.append(("x3a", i - 1))
        ple_order.append(("x3a", NT - 1))
        order += ple_order + [("x1b", i) for i in range(NT)] + [("x2b", i) for i in range(NT)]
        for n, tile_name in enumerate(order):
            TR[tile_name] = n
        LN = {"v": 0, (0, 1): NT, (0, 2): 2 * NT, (1, 1): 3 * NT, (1, 2): 4 * NT}
        LNP = {(0, 1): 1, (0, 2): 2, (1, 1): 3, (1, 2): 4}

        def drained(eng, job):
            eng.wait_ge(job_a if job.engine == "act" else job_v, job.nth)

        links_v, norms, rstds = [0], [0], [0]
        block = ctx.enter_context(nc.Block())

        @block.sync
        def _(sp):
            def slot_free(n, last, used, first_expert):
                if n < 0:
                    return
                if n in last:
                    sp.wait_ge(job_done, jobs[last[n]].n + 1)
                else:
                    l = 1 if n >= first_expert[1] else 0
                    e = n - first_expert[l]
                    sp.wait_ge(used, l * NE + e + (e >= ASIDE) + 1)

            def load_wa(n, parts):
                slot_free(n - RING, wa_last, wa_used, WA_E)
                s = n % RING
                for src, at, w in parts:
                    sp.dma_start(wa[s][:, :, at:at + w], src.rearrange(FLAT, p=P)).then_inc(wa_full[s], 16)

            def load_wb(n, dst, src):
                slot_free(n - RING, wb_last, wb_used, WB_E)
                sp.dma_start(dst, src).then_inc(wb_full[n % RING], 16)

            def load_experts(l, it):
                for j in range(RING):
                    e = sp.snap(it * RING + j)
                    before = sp.snap(it * RING + (l * NE + j + 1 - RING))
                    sa, sb_ = (WA_E[l] + j) % RING, (WB_E[l] + j) % RING
                    sp.wait_ge(wa_used, before)
                    sp.dma_start(wa[sa][:], e_w_in[l, bass.ds(e, 1)].rearrange("o (a p) f -> p (o a) f", p=P)).then_inc(wa_full[sa], 16)
                    sp.wait_ge(wb_used, before)
                    sp.dma_start(wb[sb_][:], e_w_out[l, bass.ds(e, 1)].rearrange("o (a p) f -> p (o a) f", p=P)).then_inc(wb_full[sb_], 16)

            for i in range(NT):
                sp.dma_start(X[:, i, :], x[0, i * P:(i + 1) * P, :]).then_inc(x_loaded, 16)
            for l in range(DEPTH):
                if l == 1:
                    sp.wait_ge(rr_used, NT)
                for n, parts in enumerate(wa_head[l]):
                    load_wa(WA_HEAD[l] + n, parts)
                    if l == 0 and n == 0:
                        for dst, src in ((BINV, a_b_in[0, D:2 * D]), (VNG, a_vn_g[0]), (VNB, a_vn_b[0]), (BINU, a_b_in[0, 0:D])):
                            sp.dma_start(dst, src.partition_broadcast(P)).then_inc(gm_loaded, 16)
                        sp.dma_start(WS, a_w_s[0].rearrange("g t s -> t g s")).then_inc(gm_loaded, 16)
                        sp.dma_start(BS, a_b_s[0].rearrange("g t -> t g"), allow_slow_non_contiguous=True).then_inc(gm_loaded, 16)
                    if l == 1 and n == 1:
                        load_wb(WB_UK, wbh[WB_UK % RING], b_w_uk[0].rearrange("h (a p) d -> p (h a) d", p=P))
                    if l == 1 and n == 3:
                        load_wb(WB_UV, wbh[WB_UV % RING], b_w_uv[0].rearrange("h (a p) d -> p (h a) d", p=P))
                load_wb(WB_PLE[l], wb[WB_PLE[l] % RING][:], ple_w[l].rearrange(FLAT, p=P))
                for e in range(RING):
                    load_wa(WA_E[l] + e, [(e_w_in[l, e], 0, BANK)])
                    if e < RING - 1:
                        load_wb(WB_E[l] + e, wb[(WB_E[l] + e) % RING][:], e_w_out[l, e].rearrange(FLAT, p=P))
                sp.wait_ge(job_done, jobs["out", l, NT - 1, NB - 1].n + 1)
                sp.dma_start(OWA, e_w_in[l, ASIDE].rearrange(FLAT, p=P)).then_inc(aside_full, 16)
                sp.wait_ge(job_done, jobs["rt", l, NT - 1].n + 1)
                sp.dma_start(OWB, e_w_out[l, ASIDE].rearrange(FLAT, p=P)).then_inc(aside_full, 16)
                load_wb(WB_E[l] + RING - 1, wb[(WB_E[l] + RING - 1) % RING][:], e_w_out[l, RING - 1].rearrange(FLAT, p=P))
                with sp.Fori(1, NE // RING - 1) as it:
                    load_experts(l, it)
                for e in range(ASIDE + 1, NE):
                    na, nb = WA_E[l] + tile_of(e), WB_E[l] + tile_of(e)
                    load_wa(na, [(e_w_in[l, e], 0, BANK)])
                    load_wb(nb, wb[nb % RING][:], e_w_out[l, e].rearrange(FLAT, p=P))
                sp.wait_ge(units_ready, l + 1)
                further = sp.value_load(meta[0:1, NOV:NOV + 1], min_val=0, max_val=NOV)
                with sp.If(further > 0):
                    with sp.Fori(0, NOV) as u:
                        with sp.If(u < further):
                            e = sp.value_load(meta[0:1, bass.ds(u, 1)], min_val=0, max_val=NE - 1)
                            turn = sp.snap(u + 1)
                            sp.wait_ge(ov_free[l], turn)
                            sp.dma_start(OWA, e_w_in[l, bass.ds(e, 1)].rearrange("o (a p) f -> p (o a) f", p=P)).then_inc(ov_w[l], 16)
                            sp.dma_start(OWB, e_w_out[l, bass.ds(e, 1)].rearrange("o (a p) f -> p (o a) f", p=P)).then_inc(ov_w[l], 16)
                        sp.nop()
                for n in range(NB):
                    load_wa(WA_GW[l] + n, half(ple_gw[l], n))
                    if n == 0:
                        sp.wait_ge(rr_full[0], 16 * (l + 1))
            for i in range(NT):
                sp.wait_ge(ple_done, NB * (NT + i + 1))
                sp.dma_start(out[0, i * P:(i + 1) * P, :], X[:, i, :]).then_inc(out_done, 16)
            sp.wait_ge(out_done, 16 * NT)

        @block.gpsimd
        def _(pool):
            links = [0]

            def link(ins):
                links[0] += 1
                ins.then_inc(chain_p, 1)
                pool.wait_ge(chain_p, links[0])

            g = nc.gpsimd
            last_tok, last_row = pool.to_reg(T - 1), pool.to_reg(2 * T - 1)
            link(g.memset(ident[:], 0.0))
            link(g.affine_select(out=ident[:], in_=ident[:], compare_op=ALU.not_equal, fill=1.0, base=0,
                                 pattern=[[-1, P]], channel_multiplier=1))
            link(g.memset(minus_half[:], -0.5))
            link(g.memset(ones[:], 1.0))
            link(g.affine_select(out=strict[:], in_=ones[:], compare_op=ALU.is_gt, fill=0.0, base=0,
                                 pattern=[[1, P]], channel_multiplier=-1))
            link(g.iota(iota[:], pattern=[[1, BLK]], base=0, channel_multiplier=0, allow_small_or_imprecise_dtypes=True))
            link(g.iota(rev[:], pattern=[[-1, NE]], base=NE, channel_multiplier=0, allow_small_or_imprecise_dtypes=True))
            link(g.iota(val[:], pattern=[[T, 2], [P, NT]], base=-NONE, channel_multiplier=1,
                        allow_small_or_imprecise_dtypes=True))
            g.sem_inc(consts_ready, 1)

            def load_ln(gain, bias):
                for dst, src in ((LNG, gain), (LNB, bias)):
                    pool.dma_start(dst[:], src.partition_broadcast(P)).then_inc(lnp_loaded, 16)

            def rstd_of_tiles(n):
                for _ in range(n):
                    rstds[0] += 1
                    pool.wait_ge(var_ready, rstds[0])
                    link(g.tensor_scalar(rstd[:], mv[:, 1:2], LN_EPS, None, ALU.add))
                    g.tensor_tensor(rstd[:], rstd[:], minus_half[:], ALU.pow).then_inc(rstd_ready, 1)

            pool.wait_ge(gm_loaded, 16 * 6)
            load_ln(ln1_g[0], ln1_b[0])
            drained(pool, jobs["ws", 1])
            g.affine_select(out=WCT, in_=WCT, compare_op=ALU.is_ge, fill=0.0, base=0,
                            pattern=[[0, 8], [1, P]], channel_multiplier=-1).then_inc(wct_ready, 1)
            rstd_of_tiles(NT)

            for l in range(DEPTH):
                if l == 1:
                    for i in range(NT):
                        rstds[0] += 1
                        pool.wait_ge(var_ready, rstds[0])
                        link(g.tensor_scalar(ss[:, i:i + 1], ss[:, i:i + 1], 1.0 / LAT, RMS_EPS, ALU.mult, ALU.add))
                        g.tensor_tensor(ss[:, i:i + 1], ss[:, i:i + 1], minus_half[:], ALU.pow).then_inc(rstd_ready, 1)
                    g.memset(SEL[0], 0.0).then_inc(chain_p, 1)
                    links[0] += 1
                    pool.wait_ge(chain_p, links[0])
                    g.affine_select(out=SEL[0], in_=SEL[0], compare_op=ALU.is_ge, fill=-BIG, base=0,
                                    pattern=[[-1, P]], channel_multiplier=1).then_inc(sel_mask, 1)
                    for qt in range(1, NT):
                        pool.wait_ge(rl_used, IH * qt)
                        own = SEL[qt][:, qt * P:]
                        g.affine_select(out=own, in_=own, compare_op=ALU.is_ge, fill=-BIG, base=0,
                                        pattern=[[-1, P]], channel_multiplier=1).then_inc(sel_mask, 1)
                rstd_of_tiles(NT)
                pool.wait_ge(ln_done, LN[l, 1] + NT)
                load_ln(ln2_g[l], ln2_b[l])
                for s in range(RING):
                    g.memset(XG[s], 0.0).then_inc(xg_zero, 1)
                pool.wait_ge(xg_zero, RING * (l + 1))
                pool.wait_ge(rows_stored, 16 * NT * (l + 1))
                pool.wait_ge(units_ready, l + 1)

                def gather(col, s, done):
                    pool.indirect_dma_start(XG[s], None, x_rows,
                                            bass.IndirectOffsetOnAxis(ap=col, axis=0),
                                            bounds_check=last_tok, oob_is_err=False).then_inc(done, 16)

                def scatter(col, src, done):
                    pool.indirect_dma_start(y_rows, bass.IndirectOffsetOnAxis(ap=col, axis=0),
                                            src, None,
                                            bounds_check=last_row, oob_is_err=False).then_inc(done, 16)

                for s in range(RING):
                    gather(idx_tok[:, s:s + 1], s, xg_full[s])

                def blocks(it, last):
                    static = isinstance(it, int)
                    num = (lambda a: a) if static else pool.snap
                    for j in range(RING):
                        first = static and it == 0 and j < 2
                        copies = j - 1 if first else it * (2 * RING) + (j - 2 if last else 2 * j - 2)
                        column = (lambda e: slice(e, e + 1)) if static else (lambda e: bass.ds(e, 1))
                        if not last:
                            copies = copies + (2 if first else 1)
                            pool.wait_ge(xg_used[l], num(it * RING + (j + 1)))
                            pool.sem_inc(passed, 1)
                            g.tensor_copy(stg[:, j:j + 1], idx_tok[:, column(num(it * RING + (RING + j)))]).then_inc(staged[l], 1)
                            pool.wait_ge(staged[l], num(copies))
                            pool.sem_inc(passed, 1)
                            gather(stg[:, j:j + 1], j, xg_full[j])
                        if not first:
                            store_block(num, column, it * RING + (j - 2), (j - 2) % RING, copies + 1)

                def store_block(num, column, e, s, copies):
                    pool.wait_ge(yo_a[l], num(e + 1))
                    pool.wait_ge(yo_v[l], num(e + 1))
                    pool.sem_inc(passed, 1)
                    g.tensor_copy(sts[:, s:s + 1], idx_row[:, column(num(e))]).then_inc(staged[l], 1)
                    pool.wait_ge(staged[l], num(copies))
                    pool.sem_inc(passed, 1)
                    scatter(sts[:, s:s + 1], YO[s], sc_done[s])

                blocks(0, False)
                with pool.Fori(1, NE // RING - 1) as it:
                    blocks(it, False)
                blocks(NE // RING - 1, True)
                for e in range(NE - 2, NE):
                    store_block(int, lambda e: slice(e, e + 1), e, e % RING, 2 * NE - RING - (NE - 1 - e))
                for s in range(RING):
                    pool.wait_ge(sc_done[s], 16 * NE // RING * (l + 1))
                further = pool.value_load(meta[0:1, NOV:NOV + 1], min_val=0, max_val=NOV)
                with pool.If(further > 0):
                    pool.sem_inc(ov_free[l], 1)
                    with pool.Fori(0, NOV) as u:
                        with pool.If(u < further):
                            turn = pool.snap(u + 1)
                            landed = pool.snap(u * 16 + 16)
                            outputs = pool.snap(u * 2 + 2)
                            staged_n = pool.snap(u * 2 + (2 * NE - RING + 2))
                            g.tensor_copy(stg[:, 0:1], idx_tok[:, bass.ds(u + NE, 1)]).then_inc(staged[l], 1)
                            g.tensor_copy(sts[:, 0:1], idx_row[:, bass.ds(u + NE, 1)]).then_inc(staged[l], 1)
                            pool.wait_ge(staged[l], staged_n)
                            pool.sem_inc(passed, 1)
                            gather(stg[:, 0:1], 0, ov_g[l])
                            pool.wait_ge(ov_e[l], outputs)
                            pool.sem_inc(passed, 1)
                            scatter(sts[:, 0:1], YO[0], ov_d[l])
                            pool.wait_ge(ov_d[l], landed)
                            pool.sem_inc(ov_free[l], 1)
                        pool.nop()
                pool.sem_inc(moe_done[l], 1)

                rstd_of_tiles(2)
                for i in range(NT):
                    if i + 2 < NT:
                        rstd_of_tiles(1)
                    for n in range(NB):
                        q = (l * NT + i) * NB + n
                        pool.wait_ge(gated, q + 1)
                        xs = X[:, i, n * BANK:(n + 1) * BANK]
                        g.tensor_tensor(xs, xs, GT[q % 4], ALU.add).then_inc(ple_done, 1)
                if l == 0:
                    pool.wait_ge(ln_done, LN[l, 2] + NT)
                    load_ln(ln1_g[1], ln1_b[1])

        @block.scalar
        def _(act):
            s = nc.scalar

            def load_router(l):
                act.dma_start(rw[:, :, 0:NG], r_wg[l].rearrange(FLAT, p=P), allow_slow_non_contiguous=True).then_inc(rw_loaded, 16)
                act.dma_start(rw[:, :, NG:], r_we[l].rearrange(FLAT, p=P)).then_inc(rw_loaded, 16)
                act.dma_start(rb[:, 0:NG], r_bg[l].partition_broadcast(P)).then_inc(rw_loaded, 16)
                act.dma_start(rb[:, NG:], r_be[l].partition_broadcast(P)).then_inc(rw_loaded, 16)

            def take(job):
                act.wait_ge(job_done, job.n + 1)
                return ps[:, job.bank, :]

            def copy_job(dst, *name, scale=None):
                job = jobs[name]
                src = take(job)
                if len(dst.shape) == 3:
                    src = src.rearrange("p (a b) -> p a b", a=dst.shape[1])
                if scale is None:
                    s.activation(dst, src, ACT.Copy).then_inc(job_a, 1)
                else:
                    s.activation(dst, src, ACT.Copy, scale=scale).then_inc(job_a, 1)

            def take_transposed(name, i, dst):
                n = TR[name, i]
                act.wait_ge(tr_ps, 2 * n + 1)
                src = ps[:, 2 * (n % 2), :].rearrange("p (a b) -> p a b", a=4)
                s.activation(dst[:, 0:4, i * P:(i + 1) * P], src, ACT.Copy).then_inc(tr_a, 1)

            for i in range(NT):
                take_transposed("x0", i, XTv)
            act.wait_ge(gm_loaded, 16 * 6)
            load_router(0)
            for w in range(4):
                area, n = (V, U)[w // 2], w % 2
                for i in range(NT):
                    act.wait_ge(job_v, jobs["in", w, i].nth)
                    z = area[:, i, n * BANK:(n + 1) * BANK]
                    s.activation(z, z, ACT.Gelu).then_inc(z_done, 1)
                for q in range(2) if w == 0 else ():
                    copy_job(WCT[:, 4 * q:4 * q + 4, :], "ws", q)
            for i in range(NT):
                take_transposed("gated", i, AT)

            for l in range(DEPTH):
                if l == 1:
                    act.dma_start(KVG, b_kv_g[0].partition_broadcast(P)).then_inc(kvg_loaded, 16)
                    for q in range(4):
                        copy_job(UKT[:, 2 * q:2 * q + 2, :], "uk", q)
                    copy_job(KIT, "ki")
                    for i in range(NT):
                        job = jobs["ck", i]
                        src = take(job)
                        s.activation(JUNK[:, i, :], src[:, 0:LAT], ACT.Square, accum_out=ss[:, i:i + 1]).then_inc(var_ready, 1)
                    for b in range(4):
                        copy_job(QIT[:, b, :], "qi", b)
                    n = 0
                    for qt in range(1, NT):
                        for h in range(IH):
                            nk = (qt + 1) * P
                            src = take(jobs["ix", qt, h])
                            if n >= 2:
                                act.wait_ge(rl_used, n - 1)
                            s.activation(RL[:, n % 2, 0:nk], src[:, 0:nk], ACT.Relu).then_inc(job_a, 1)
                            n += 1
                    for cc in range(2):
                        copy_job(CKT[:, cc, :], "ct", cc)
                    for h in range(HEADS):
                        copy_job(AT[:, h, :], "q", h)
                    act.wait_ge(rl_used, n)
                    for h in range(HEADS):
                        for cc in range(2):
                            copy_job(QL[h][:, cc, :], "ql", h, cc, scale=float(HD) ** -0.5)
                    for u, (qt, hg) in enumerate(UNITS):
                        nk = (qt + 1) * P
                        for j in range(4):
                            act.wait_ge(lg_max, u + 1)
                            s.activation(PR[:, j, 0:nk], PR[:, j, 0:nk], ACT.Exp, bias=nmx[:, j:j + 1],
                                         accum_out=rs[:, j:j + 1]).then_inc(p_exp, 1)
                        for kt in range(1, qt + 1, 2):
                            copy_job(PT[:, kt, :], "tr", u, kt)
                        copy_job(OL[:, 0, :], "pv", u, 0)
                        copy_job(AT[:, 4 * hg:4 * hg + 4, qt * P:(qt + 1) * P], "uv", u)

                act.dma_start(PIN, p[l, 0].rearrange("(i p) n -> p i n", p=P)).then_inc(ple_in, 16)
                act.dma_start(GBB, ple_gb[l].partition_broadcast(P)).then_inc(ple_in, 16)
                for i in range(NT):
                    act.wait_ge(ln_done, LN[l, 1] + i + 1)
                    act.dma_start(x_rows[i * P:(i + 1) * P, :], X[:, i, :]).then_inc(rows_stored, 16)
                    take_transposed("x1a" if l == 0 else "x1b", i, XTv)
                for cc in range(2):
                    copy_job(PTT[:, cc, :], "pt", l, cc)
                for q in range(NT * NB):
                    if q == GATES_AT:
                        act.wait_ge(gate_in, l + 1)
                        s.activation(gexp, gexp, ACT.Exp).then_inc(gate_exp, 1)
                        s.activation(dexp, dexp, ACT.Exp).then_inc(gate_exp, 1)
                    i, n = q // NB, q % NB
                    copy_job(PP[:, i, n * BANK:(n + 1) * BANK], "pp", l, i, n)

                def transposed(turn, k):
                    act.wait_ge(xg_used[l], turn)
                    s.activation(XGT[k], ps[:, k, :].rearrange("p (a b) -> p a b", a=KD), ACT.Copy).then_inc(xgt_ready[l], 1)

                def copy_hidden(k):
                    return s.activation(HS[k], ps[:, 2 + k, 0:FF], ACT.Copy)

                def silu(k):
                    return s.activation(SA[k], ps[:, 2 + k, FF:2 * FF].rearrange("p (a b) -> p a b", a=2)[:, :, 0:BLK], ACT.Silu)

                def halves(turn, k, slot, scattered):
                    act.wait_ge(wb_used, turn)
                    if scattered is not None:
                        act.wait_ge(sc_done[slot], scattered)
                    s.activation(YO[slot][:, 0:BANK], ps[0:BLK, 4 + 2 * k, :], ACT.Copy).then_inc(yo_a[l], 1)

                def blocks(it):
                    static = isinstance(it, int)
                    num = (lambda v: v) if static else act.snap
                    for j in range(RING):
                        first = static and it == 0
                        last = static and it == NE // RING - 1 and j == RING - 1
                        k = j % 2
                        product = num(it * RING + (l * NE + j + 1))
                        turned = num(it * RING + (j + 1))
                        nxt = num(it * RING + (j + 2))
                        wb_turn = num(it * RING + (l * NE + j))
                        scattered = None if first else num(it * 16 + 16 * (l * NE // RING - (j == 0)))
                        act.wait_ge(wa_used, product)
                        copy_hidden(k).then_inc(hs_ready[l], 1)
                        if not last:
                            transposed(nxt, 1 - k)
                        act.wait_ge(hs_ps[l], turned)
                        silu(k).then_inc(sa_ready[l], 1)
                        if not (first and j == 0):
                            halves(wb_turn, 1 - k, (j - 1) % RING, scattered)

                transposed(1, 0)
                blocks(0)
                with act.Fori(1, NE // RING - 1) as it:
                    blocks(it)
                blocks(NE // RING - 1)
                halves((l + 1) * NE, 1, RING - 1, 16 * ((l + 1) * NE // RING - 1))

                further = act.value_load(meta[0:1, NOV:NOV + 1], min_val=0, max_val=NOV)
                with act.If(further > 0):
                    with act.Fori(0, NOV) as u:
                        with act.If(u < further):
                            turn = act.snap(u + 1)
                            turned = act.snap(u + (NE + 1))
                            act.wait_ge(ov_t[l], turn)
                            s.activation(XGT[0], ps[:, 0, :].rearrange("p (a b) -> p a b", a=KD), ACT.Copy).then_inc(ov_x[l], 1)
                            act.wait_ge(ov_h[l], turn)
                            copy_hidden(0).then_inc(hs_ready[l], 1)
                            act.wait_ge(hs_ps[l], turned)
                            silu(0).then_inc(ov_s[l], 1)
                            act.wait_ge(ov_y[l], turn)
                            for n in range(NB):
                                s.activation(YO[0][:, n * BANK:(n + 1) * BANK], ps[n * BLK:(n + 1) * BLK, 4 + n, :],
                                             ACT.Copy).then_inc(ov_e[l], 1)
                        act.nop()

                act.wait_ge(moe_done[l], 1)
                y_view = y_rows.rearrange("(k t) d -> t k d", k=2)

                for i in range(NT):
                    act.dma_start(RR[l][i], y_view[i * P:(i + 1) * P]).then_inc(rr_full[i], 16)
                name = "x2a" if l == 0 else "x2b"
                take_transposed(name, 0, XTv)
                for i in range(NT):
                    for n in range(NB):
                        q = (l * NT + i) * NB + n
                        act.wait_ge(job_v, jobs["g", l, i, n].nth)
                        s.activation(GT[q % 4], GT[q % 4], ACT.Sigmoid).then_inc(g_sig, 1)
                        if n == 0 and i + 1 < NT:
                            take_transposed(name, i + 1, XTv)
                    if l == 0 and i:
                        take_transposed("x3a", i - 1, XTv)
                if l == 0:
                    take_transposed("x3a", NT - 1, XTv)
                    load_router(1)

        def attention(pe, open_job, need_wa, need_wb, product, need_xt):
            mm = nc.tensor.matmul
            need_wb(WB_UK)
            flat = wbh[WB_UK % RING]
            for q in range(4):
                bank = open_job("uk", q)
                for b in range(4):
                    last = nc.tensor.transpose(bank[:, b * P:(b + 1) * P], flat[:, 4 * q + b, :], ident[:])
                last.then_inc(job_done, 1)
            for i in range(NT):
                need_xt("x3a", i)
            tile = need_wa(WA_HEAD[1])
            product(open_job("ki"), lambda k: tile[:, k, LAT:LAT + 2 * ID], lambda k: XTv[:, k, :], T).then_inc(job_done, 1)
            for i in range(NT):
                bank = open_job("ck", i)
                product(bank, lambda k: XTv[:, k, i * P:(i + 1) * P], lambda k: tile[:, k, 0:LAT], LAT)
                product(bank[:, LAT:LAT + IH], lambda k: XTv[:, k, i * P:(i + 1) * P],
                        lambda k: tile[:, k, LAT + 2 * ID:LAT + 2 * ID + IH], IH).then_inc(job_done, 1)
            tile = need_wa(WA_HEAD[1] + 1)
            for b in range(4):
                product(open_job("qi", b), lambda k: tile[:, k, b * P:(b + 1) * P], lambda k: XTv[:, k, :], T).then_inc(job_done, 1)
            drained(pe, jobs["qi", 3])
            for qt in range(1, NT):
                nk = (qt + 1) * P
                for h in range(IH):
                    o = ID * (h % 2)
                    mm(open_job("ix", qt, h)[:, 0:nk], QIT[o:o + ID, h // 2, qt * P:(qt + 1) * P],
                       KIT[o:o + ID, 0:nk], start=True, stop=True).then_inc(job_done, 1)
            drained(pe, jobs["ck", NT - 1])
            for cc in range(2):
                bank = open_job("ct", cc)
                for i in range(NT):
                    last = nc.tensor.transpose(bank[:, i * P:(i + 1) * P], CK[:, i, cc * P:(cc + 1) * P], ident[:])
                last.then_inc(job_done, 1)
            for h in range(HEADS):
                tile = need_wa(WA_HEAD[1] + 2 + h // 4)
                product(open_job("q", h), lambda k: tile[:, k, (h % 4) * HD:(h % 4 + 1) * HD],
                        lambda k: XTv[:, k, :], T).then_inc(job_done, 1)
            for h in range(HEADS):
                drained(pe, jobs["q", h])
                for cc in range(2):
                    mm(open_job("ql", h, cc), UKT[:, h, cc * P:(cc + 1) * P], AT[:, h, :],
                       start=True, stop=True).then_inc(job_done, 1)
            drained(pe, jobs["ql", HEADS - 1, 1])

            def logits(u):
                qt, hg = UNITS[u]
                nk = (qt + 1) * P
                for j in range(4):
                    if u:
                        pe.wait_ge(lg_read, 4 * (u - 1) + j + 1)
                    for cc in range(2):
                        last = mm(ps[:, j, 0:nk], QL[4 * hg + j][:, cc, qt * P:(qt + 1) * P], CKT[:, cc, 0:nk],
                                  start=(cc == 0), stop=(cc == 1))
                    last.then_inc(lg_ps, 1)

            need_wb(WB_UV)
            uv = wbh[WB_UV % RING]
            logits(0)
            for u, (qt, hg) in enumerate(UNITS):
                if u + 1 < len(UNITS):
                    logits(u + 1)
                pe.wait_ge(p_norm, 4 * (u + 1))
                for kt in range(qt + 1):
                    bank = open_job("tr", u, kt)
                    for j in range(4):
                        last = nc.tensor.transpose(bank[:, j * P:(j + 1) * P], PR[:, j, kt * P:(kt + 1) * P], ident[:])
                    last.then_inc(job_done, 1)
                for cc in range(2):
                    bank = open_job("pv", u, cc)
                    for kt in range(qt + 1):
                        if cc == 0:
                            drained(pe, jobs["tr", u, kt])
                        last = mm(bank, CK[:, kt, cc * P:(cc + 1) * P], PT[:, kt, :], start=(kt == 0), stop=(kt == qt))
                    last.then_inc(job_done, 1)
                bank = open_job("uv", u)
                for cc in range(2):
                    drained(pe, jobs["pv", u, cc])
                for j in range(4):
                    for cc in range(2):
                        last = mm(bank[:, j * P:(j + 1) * P], uv[:, 2 * (4 * hg + j) + cc, :], OL[:, cc, j * P:(j + 1) * P],
                                  start=(cc == 0), stop=(cc == 1))
                last.then_inc(job_done, 1)
            drained(pe, jobs["uv", len(UNITS) - 1])

        @block.tensor
        def _(pe):
            mm = nc.tensor.matmul

            def open_job(*name):
                job = jobs[name]
                if job.n >= 4:
                    drained(pe, jobs.order[job.n - 4])
                return ps[:, job.bank, :]

            def transpose_tile(name, i, src):
                n = TR[name, i]
                if n >= 2:
                    pe.wait_ge(tr_a, n - 1)
                    pe.wait_ge(tr_v, n - 1)
                for h in range(2):
                    for b in range(4):
                        k = 4 * h + b
                        last = nc.tensor.transpose(ps[:, 2 * (n % 2) + h, b * P:(b + 1) * P],
                                                   src[:, k * P:(k + 1) * P], ident[:])
                    last.then_inc(tr_ps, 1)

            def need_wa(n):
                pe.wait_ge(wa_full[n % RING], wa_turn(n))
                return wa[n % RING]

            def need_wb(n):
                pe.wait_ge(wb_full[n % RING], 16 * (n // RING + 1))
                return wb[n % RING]

            def product(bank, left, right, w):
                for k in range(KD):
                    last = mm(bank[:, 0:w], left(k), right(k), start=(k == 0), stop=(k == KD - 1))
                return last

            def need_xt(name, i):
                pe.wait_ge(tr_a, TR[name, i] + 1)
                pe.wait_ge(tr_v, TR[name, i] + 1)

            pe.wait_ge(consts_ready, 1)
            pe.wait_ge(x_loaded, 16 * NT)
            for i in range(NT):
                transpose_tile("x0", i, X[:, i, :])
            for w in range(4):
                tile = need_wa(w)
                for i in range(NT):
                    if w == 0:
                        need_xt("x0", i)
                    bank = open_job("in", w, i)
                    product(bank, lambda k: XTv[:, k, i * P:(i + 1) * P], lambda k: tile[:, k, :], BANK).then_inc(job_done, 1)
                if w == 0:
                    pe.wait_ge(gm_loaded, 16 * 6)
                for q in range(2) if w == 0 else ():
                    bank = open_job("ws", q)
                    for b in range(4):
                        last = nc.tensor.transpose(bank[:, b * P:(b + 1) * P], WS[:, 4 * q + b, :], ident[:])
                    last.then_inc(job_done, 1)
            pe.wait_ge(ln_done, NT)
            pe.wait_ge(wct_ready, 1)
            for g in range(8):
                bank = open_job("sp", g)
                mm(bank.rearrange("p (c d) -> p c d", c=NT), WCT[:, g, :], V[:, :, g * P:(g + 1) * P],
                   start=True, stop=True).then_inc(job_done, 1)
            drained(pe, jobs["sp", 7])
            for i in range(NT):
                transpose_tile("gated", i, U[:, i, :])

            for l in range(DEPTH):
                if l == 1:
                    attention(pe, open_job, need_wa, need_wb, product, need_xt)
                else:
                    for i in range(NT):
                        need_xt("gated", i)

                tiles = [need_wa(WA_HEAD[l] + 4 + n) for n in range(NB)]
                pe.wait_ge(rw_loaded, 64 * (l + 1))
                name = "x1a" if l == 0 else "x1b"
                for step in range(NT + 1):
                    for n in range(NB):
                        if step < NT:
                            bank = open_job("out", l, step, n)
                            product(bank, lambda k: AT[:, k, step * P:(step + 1) * P],
                                    lambda k: tiles[n][:, k, :], BANK).then_inc(job_done, 1)
                        if step and n == 0:
                            pe.wait_ge(ln_done, LN[l, 1] + step)
                            transpose_tile(name, step - 1, X[:, step - 1, :])
                    if step:
                        i = step - 1
                        need_xt(name, i)
                        bank = open_job("rt", l, i)
                        product(bank, lambda k: XTv[:, k, i * P:(i + 1) * P], lambda k: rw[:, k, :], NG + NE).then_inc(job_done, 1)

                pe.wait_ge(ple_in, 32 * (l + 1))
                for cc in range(2):
                    bank = open_job("pt", l, cc)
                    for i in range(NT):
                        last = nc.tensor.transpose(bank[:, i * P:(i + 1) * P], PIN[:, i, cc * P:(cc + 1) * P], ident[:])
                    last.then_inc(job_done, 1)
                ple_tile = need_wb(WB_PLE[l])
                drained(pe, jobs["pt", l, 1])
                for q in range(NT * NB):
                    if q == GATES_AT:
                        pe.wait_ge(picks, l + 1)
                        cum, cnt = ps[:, 0, 0:NT * NE], ps[:, 1, 0:NE]
                        for i in range(NT):
                            for j in range(i):
                                mm(cum[:, i * NE:(i + 1) * NE], ones[:], MB[:, j, :], start=(j == 0), stop=False)
                            mm(cum[:, i * NE:(i + 1) * NE], strict[:], MB[:, i, :], start=(i == 0), stop=True)
                        for j in range(NT):
                            last = mm(cnt, ones[:], MB[:, j, :], start=(j == 0), stop=(j == NT - 1))
                        last.then_inc(ranked, 1)
                    if q == UNITS_AT:
                        pe.wait_ge(coded, l + 1)
                        for c in range(2 * NT):
                            last = mm(ps[0:BLK, 2, 0:NU], RSH[:, c, :], UVH[:, c, :], start=(c == 0), stop=(c == 2 * NT - 1))
                        last.then_inc(unit_ps, 1)
                    i, n = q // NB, q % NB
                    bank = open_job("pp", l, i, n)
                    for c in range(2):
                        last = mm(bank, PTT[:, c, i * P:(i + 1) * P], ple_tile[:, c, n * BANK:(n + 1) * BANK],
                                  start=(c == 0), stop=(c == 1))
                    last.then_inc(job_done, 1)

                def transposes(slot, k):
                    pe.sem_inc(pe_passed, 1)
                    for b in range(KD):
                        last = nc.tensor.transpose(ps[:, k, b * BLK:(b + 1) * BLK], XG[slot][:, b * P:(b + 1) * P],
                                                   ident[0:BLK, 0:BLK])
                    return last

                def products_in(k, tile):
                    for c in range(KD):
                        for n in range(2):
                            last = mm(ps[n * BLK:(n + 1) * BLK, 2 + k, 0:FF], XGT[k][:, c, :], tile[:, c, n * FF:(n + 1) * FF],
                                      start=(c == 0), stop=(c == KD - 1))
                    return last

                def turn_hidden(k):
                    for c in range(2):
                        last = nc.tensor.transpose(ps[:, 2 + k, FF + c * P:FF + (c + 1) * P], HS[k][:, c * P:(c + 1) * P], ident[:])
                    return last

                def products_out(k, tile):
                    for c in range(2):
                        for n in range(NB):
                            last = mm(ps[n * BLK:(n + 1) * BLK, 4 + 2 * k + n, :], HT[k][:, c, :],
                                      tile[:, c, n * BANK:(n + 1) * BANK], start=(c == 0), stop=(c == 1))
                    return last

                def out_block(b, k, s):
                    ht, full, free = b
                    if full is not None:
                        pe.wait_ge(wb_full[s], full)
                    if free is not None:
                        pe.wait_ge(yo_a[l], free)
                        pe.wait_ge(yo_v[l], free)
                    pe.wait_ge(ht_ready[l], ht)
                    products_out(k, OWB if full is None else wb[s]).then_inc(wb_used, 1)

                def blocks(it):
                    static = isinstance(it, int)
                    num = (lambda v: v) if static else pe.snap
                    for j in range(RING):
                        first = static and it == 0
                        last = static and it == NE // RING - 1 and j == RING - 1
                        aside = static and it * RING + j == ASIDE
                        aside_before = static and it * RING + j - 1 == ASIDE
                        k = j % 2
                        na, nb = WA_E[l] + j, WB_E[l] + j - 1
                        if static and it * RING > ASIDE - RING:
                            na = WA_E[l] + tile_of(it * RING + j) - it * RING
                            nb = WB_E[l] + tile_of(it * RING + j - 1) - it * RING
                        full_a = num(it * 16 + wa_turn(na))
                        full_b = num(it * 16 + 16 * (nb // RING + 1))
                        e1 = num(it * RING + (j + 1))
                        e0 = None if first and j == 0 else num(it * RING + j)
                        em = None if first and j < 2 else num(it * RING + (j - 1))
                        emm = None if first and j < 3 else num(it * RING + (j - 2))
                        rows = num(it * 16 + 16 * (l * NE // RING + (j + 1) // RING + 1))
                        if aside:
                            pe.wait_ge(aside_full, 32 * (l + 1))
                        else:
                            pe.wait_ge(wa_full[na % RING], full_a)
                        if em is not None:
                            pe.wait_ge(ht_ready[l], em)
                        pe.wait_ge(xgt_ready[l], e1)
                        products_in(k, OWA if aside else wa[na % RING]).then_inc(wa_used, 1)
                        if not last:
                            pe.wait_ge(xg_full[(j + 1) % RING], rows)
                            transposes((j + 1) % RING, 1 - k).then_inc(xg_used[l], 1)
                        pe.wait_ge(hs_ready[l], e1)
                        turn_hidden(k).then_inc(hs_ps[l], 1)
                        if e0 is not None:
                            out_block((e0, None if aside_before else full_b, emm), 1 - k, nb % RING)

                pe.wait_ge(xg_full[0], 16 * (l * NE // RING + 1))
                transposes(0, 0).then_inc(xg_used[l], 1)
                blocks(0)
                with pe.Fori(1, NE // RING - 1) as it:
                    blocks(it)
                blocks(NE // RING - 1)
                nb = WB_E[l] + STREAMED - 1
                out_block((NE, 16 * (nb // RING + 1), NE - 2), 1, nb % RING)

                further = pe.value_load(meta[0:1, NOV:NOV + 1], min_val=0, max_val=NOV)
                with pe.If(further > 0):
                    with pe.Fori(0, NOV) as u:
                        with pe.If(u < further):
                            turn = pe.snap(u + 1)
                            copied = pe.snap(u + (NE + 1))
                            rows = pe.snap(u * 16 + 16)
                            weights = pe.snap(u * 32 + 32)
                            pe.wait_ge(ov_g[l], rows)
                            transposes(0, 0).then_inc(ov_t[l], 1)
                            pe.wait_ge(ov_w[l], weights)
                            pe.wait_ge(ov_x[l], turn)
                            products_in(0, OWA).then_inc(ov_h[l], 1)
                            pe.wait_ge(hs_ready[l], copied)
                            turn_hidden(0).then_inc(hs_ps[l], 1)
                            pe.wait_ge(ov_m[l], turn)
                            products_out(0, OWB).then_inc(ov_y[l], 1)
                        pe.nop()
                pe.wait_ge(moe_done[l], 1)

                name = "x2a" if l == 0 else "x2b"

                def normalized(i):
                    pe.wait_ge(ln_done, LN[l, 2] + i + 1)
                    transpose_tile(name, i, X[:, i, :])

                def next_layer(i):
                    pe.wait_ge(ple_done, NB * (i + 1))
                    transpose_tile("x3a", i, X[:, i, :])

                normalized(0)
                for i in range(NT):
                    need_xt(name, i)
                    for n in range(NB):
                        tile = need_wa(WA_GW[l] + n)
                        bank = open_job("g", l, i, n)
                        product(bank, lambda k: XTv[:, k, i * P:(i + 1) * P], lambda k: tile[:, k, :], BANK).then_inc(job_done, 1)
                        if n == 0 and i + 1 < NT:
                            normalized(i + 1)
                    if l == 0 and i:
                        next_layer(i - 1)
                if l == 0:
                    next_layer(NT - 1)

        def attention_v(dve, v, link, take):
            dve.wait_ge(kvg_loaded, 16)
            for i in range(NT):
                src = take("ck", i)
                norms[0] += 1
                dve.wait_ge(rstd_ready, norms[0])
                v.tensor_scalar(WI[:, i, :], src[:, LAT:LAT + IH], float(IH * ID) ** -0.5, None, ALU.mult)
                v.scalar_tensor_tensor(CK[:, i, :], src[:, 0:LAT], ss[:, i:i + 1], KVG, ALU.mult, ALU.mult).then_inc(job_v, 1)
            dve.wait_ge(job_v, jobs["ck", NT - 1].nth)
            n = 0
            for qt in range(1, NT):
                for h in range(IH):
                    dve.wait_ge(job_a, jobs["ix", qt, h].nth)
                    r, w = RL[:, n % 2, 0:(qt + 1) * P], WI[:, qt, h:h + 1]
                    if h == 0:
                        last = v.tensor_scalar(SEL[qt], r, w, None, ALU.mult)
                    else:
                        last = v.scalar_tensor_tensor(SEL[qt], r, w, SEL[qt], ALU.mult, ALU.add)
                    last.then_inc(rl_used, 1)
                    n += 1
                    dve.wait_ge(rl_used, n)
            for qt in range(1, NT):
                dve.wait_ge(sel_mask, qt + 1)
                for _ in range(TOPK // 8):
                    link(v.max(m8[:], SEL[qt]))
                    link(v.match_replace(SEL[qt], m8[:], SEL[qt], TAKEN))
                link(v.tensor_scalar(SEL[qt], SEL[qt], TAKEN / 10, -BIG, ALU.is_gt, ALU.mult))
            for u, (qt, hg) in enumerate(UNITS):
                nk = (qt + 1) * P
                if u:
                    dve.wait_ge(job_done, jobs["tr", u - 1, UNITS[u - 1][0]].n + 1)
                for j in range(4):
                    dve.wait_ge(lg_ps, 4 * u + j + 1)
                    v.tensor_tensor_reduce(PR[:, j, 0:nk], ps[:, j, 0:nk], SEL[qt], 1.0, TAKEN, ALU.add, ALU.max,
                                           mx[:, j:j + 1]).then_inc(lg_read, 1)
                dve.wait_ge(lg_read, 4 * (u + 1))
                v.tensor_scalar(nmx[:], mx[:], -1.0, None, ALU.mult).then_inc(lg_max, 1)
                dve.wait_ge(p_exp, 4 * (u + 1))
                link(v.reciprocal(rc[:], rs[:]))
                for j in range(4):
                    v.tensor_scalar(PR[:, j, 0:nk], PR[:, j, 0:nk], rc[:, j:j + 1], None, ALU.mult).then_inc(p_norm, 1)
                for kt in range(0, qt + 1, 2):
                    v.tensor_copy(PT[:, kt, :], take("tr", u, kt)).then_inc(job_v, 1)
                v.tensor_copy(OL[:, 1, :], take("pv", u, 1)).then_inc(job_v, 1)

        def route(dve, v, link, l):
            tt, ts, red = v.tensor_tensor, v.tensor_scalar, v.tensor_reduce

            def over(a, n):
                return a.unsqueeze(len(a.shape)).broadcast_to(list(a.shape) + [n])

            def pick(dst, vals, top, work, rank_of, n):
                link(tt(work, vals, over(top, n), ALU.is_equal))
                link(tt(work, work, rank_of.unsqueeze(1).broadcast_to([P, NT, n]), ALU.mult))
                link(red(key, work, AX.X, ALU.max))
                link(tt(dst, work, over(key, n), ALU.is_equal))

            g, e = LG[:, :, 0:NG], LG[:, :, NG:]
            link(red(gmax, g, AX.X, ALU.max))
            pick(gsel, g, gmax, geq, rev[:, NE - NG:], NG)
            tt(gexp, g, over(gmax, NG), ALU.subtract)
            link(ts(pen, gsel, BIG, -BIG, ALU.mult, ALU.add))
            grouped = em.rearrange("p t (g e) -> p t g e", g=NG)
            for i in range(NT):
                last = tt(grouped[:, i], e[:, i].rearrange("p (g e) -> p g e", g=NG), over(pen[:, i], EPG), ALU.add)
            link(last)
            link(red(m1, em, AX.X, ALU.max))
            pick(EK[:, 0], em, m1, eq, rev[:], NE)
            link(v.scalar_tensor_tensor(em, EK[:, 0], -BIG, em, ALU.mult, ALU.add))
            link(red(m2, em, AX.X, ALU.max))
            pick(EK[:, 1], em, m2, eq, rev[:], NE)
            tt(MB, EK[:, 0], EK[:, 1], ALU.add).then_inc(picks, 1)
            tt(dexp, m2, m1, ALU.subtract).then_inc(gate_in, 1)
            ek = EK.rearrange("p k t e -> p (k t) e")
            ew = EW.rearrange("p k t e -> p (k t) e")

            def spread(row, n):
                return row.unsqueeze(1).broadcast_to([P, 2 * NT, n])

            link(tt(ew, ek, spread(iota[:, 0:NE], NE), ALU.mult))
            link(red(eidx, ew, AX.X, ALU.add))
            link(v.memset(one, 1.0))
            dve.wait_ge(ranked, l + 1)
            link(ts(intc, ps[:, 1, 0:NE], -1.0, 0.0, ALU.add, ALU.max))
            link(ts(intc, intc, 6, None, ALU.logical_shift_right))
            link(v.tensor_copy(extra, intc))
            link(v.tensor_tensor_scan(cin, one, extra, 0.0, ALU.mult, ALU.add))
            link(tt(cex, cin, extra, ALU.subtract))
            link(tt(ew, ek, spread(cex, NE), ALU.mult))
            link(red(base, ew, AX.X, ALU.add))
            flat = EK.rearrange("p k t e -> p k (t e)")
            link(tt(EW.rearrange("p k t e -> p k (t e)"), flat,
                    ps[:, 0, 0:NT * NE].unsqueeze(1).broadcast_to([P, 2, NT * NE]), ALU.mult))
            link(red(rank, ew, AX.X, ALU.add))
            link(v.tensor_copy(ints, rank))
            link(ts(inti, ints, 6, None, ALU.logical_shift_right))
            link(v.tensor_copy(blk, inti))
            link(ts(ints, ints, BLK - 1, None, ALU.bitwise_and))
            link(v.tensor_copy(slot, ints))
            link(tt(unit, base, blk, ALU.add))
            link(v.scalar_tensor_tensor(unit, unit, float(NE - 1), eidx, ALU.add, ALU.subtract))
            link(ts(further_blk, blk, 0.0, None, ALU.is_gt))
            link(tt(unit, unit, further_blk, ALU.mult))
            link(tt(unit, unit, eidx, ALU.add))
            link(tt(UVH, spread(iota[:, 0:NU], NU), over(unit, NU), ALU.is_equal))
            link(tt(RSH, spread(iota[:], BLK), over(slot, BLK), ALU.is_equal))
            tt(UVH, UVH, over(val[:], NU), ALU.mult).then_inc(coded, 1)
            link(tt(whose[0:1], cin[0:1].unsqueeze(1).broadcast_to([1, NOV, NE]),
                    iota[0:1, 0:NOV].unsqueeze(2).broadcast_to([1, NOV, NE]), ALU.is_le))
            link(red(owner[0:1], whose[0:1], AX.X, ALU.add))
            link(ts(meta[0:1, 0:NOV], owner[0:1], float(NE - 1), None, ALU.min))
            link(v.tensor_copy(meta[0:1, NOV:NOV + 1], cin[0:1, NE - 1:NE]))
            dve.wait_ge(gate_exp, 2 * (l + 1))
            link(red(gsum, gexp, AX.X, ALU.add))
            link(ts(den, dexp, 1.0, None, ALU.add))
            link(tt(den, den, gsum, ALU.mult))
            link(v.reciprocal(gates[:, 0, :], den))
            link(tt(gates[:, 1, :], gates[:, 0, :], dexp, ALU.mult))
            dve.wait_ge(unit_ps, l + 1)
            rows, off = rowf[0:BLK], offs[0:BLK]
            link(ts(rows, ps[0:BLK, 2, 0:NU], float(NONE), None, ALU.add))
            link(v.tensor_copy(idx_row[:], rows))
            link(ts(off, rows, float(T), -float(T), ALU.is_ge, ALU.mult))
            tt(idx_tok[:], rows, off, ALU.add).then_inc(units_ready, 1)

        @block.vector
        def _(dve):
            v = nc.vector

            def link(ins):
                links_v[0] += 1
                ins.then_inc(chain_v, 1)
                dve.wait_ge(chain_v, links_v[0])

            def take(*name):
                job = jobs[name]
                dve.wait_ge(job_done, job.n + 1)
                return ps[:, job.bank, :]

            def take_transposed(name, i, dst):
                n = TR[name, i]
                dve.wait_ge(tr_ps, 2 * n + 2)
                src = ps[:, 2 * (n % 2) + 1, :].rearrange("p (a b) -> p a b", a=4)
                v.tensor_copy(dst[:, 4:8, i * P:(i + 1) * P], src).then_inc(tr_v, 1)

            def normalize(t, gain, bias):
                for n in range(NB):
                    last = v.bn_stats(bn[:, n, :], t[:, n * BANK:(n + 1) * BANK])
                link(last)
                v.bn_aggr(mv[:], bn[:]).then_inc(var_ready, 1)
                norms[0] += 1
                dve.wait_ge(var_ready, norms[0])
                link(v.scalar_tensor_tensor(t, t, mv[:, 0:1], gain, ALU.subtract, ALU.mult))
                dve.wait_ge(rstd_ready, norms[0])
                v.scalar_tensor_tensor(t, t, rstd[:], bias, ALU.mult, ALU.add).then_inc(ln_done, 1)

            for i in range(NT):
                take_transposed("x0", i, XTv)
            dve.wait_ge(gm_loaded, 16 * 6)

            def norm_v(i):
                dve.wait_ge(z_done, NT + i + 1)
                normalize(V[:, i, :], VNG, VNB)

            for w in range(4):
                area, bias, n = ((V, BINV), (U, BINU))[w // 2] + (w % 2,)
                cols = slice(n * BANK, (n + 1) * BANK)
                for i in range(NT):
                    v.tensor_tensor(area[:, i, cols], take("in", w, i), bias[:, cols], ALU.add).then_inc(job_v, 1)
                    if w == 1 and i:
                        norm_v(i - 1)
                    if w == 2 and i == 0:
                        norm_v(NT - 1)
            dve.wait_ge(z_done, 4 * NT)
            for g in range(8):
                us = U[:, :, g * P:(g + 1) * P]
                src = take("sp", g).rearrange("p (c d) -> p c d", c=NT)
                v.scalar_tensor_tensor(us, src, BS[:, g:g + 1], us, ALU.add, ALU.mult).then_inc(job_v, 1)
            for i in range(NT):
                take_transposed("gated", i, AT)

            for l in range(DEPTH):
                if l == 1:
                    attention_v(dve, v, link, take)
                name = "x1a" if l == 0 else "x1b"
                for step in range(NT + 1):
                    for n in range(NB):
                        if step < NT:
                            xs = X[:, step, n * BANK:(n + 1) * BANK]
                            last = v.scalar_tensor_tensor(xs, xs, ALPHA, take("out", l, step, n), ALU.mult, ALU.add)
                            last.then_inc(job_v, 1)
                        if step and n == 0:
                            take_transposed(name, step - 1, XTv)
                    if step < NT:
                        dve.wait_ge(job_v, jobs["out", l, step, NB - 1].nth)
                        if step == 0:
                            dve.wait_ge(lnp_loaded, 32 * LNP[l, 1])
                        normalize(X[:, step, :], LNG[:], LNB[:])
                    if step:
                        i = step - 1
                        if i == 0:
                            dve.wait_ge(rw_loaded, 64 * (l + 1))
                        v.tensor_tensor(LG[:, i, :], take("rt", l, i)[:, 0:NG + NE], rb[:], ALU.add).then_inc(job_v, 1)
                dve.wait_ge(job_v, jobs["rt", l, NT - 1].nth)
                route(dve, v, link, l)

                def hidden(k):
                    values = ps[:, 2 + k, FF:2 * FF].rearrange("p (a b) -> p a b", a=2)[:, :, BLK:2 * BLK]
                    return v.tensor_tensor(HT[k], SA[k], values, ALU.mult)

                def half_out(k, slot):
                    return v.tensor_copy(YO[slot][:, BANK:], ps[BLK:2 * BLK, 5 + 2 * k, :])

                def blocks(it):
                    static = isinstance(it, int)
                    num = (lambda a: a) if static else dve.snap
                    for j in range(RING):
                        first = static and it == 0
                        k = j % 2
                        e1 = num(it * RING + (j + 1))
                        wb_0 = num(it * RING + (l * NE + j))
                        scattered = None if first else num(it * 16 + 16 * (l * NE // RING - (j == 0)))
                        dve.wait_ge(sa_ready[l], e1)
                        hidden(k).then_inc(ht_ready[l], 1)
                        if not (first and j == 0):
                            if scattered is not None:
                                dve.wait_ge(sc_done[(j - 1) % RING], scattered)
                            dve.wait_ge(wb_used, wb_0)
                            half_out(1 - k, (j - 1) % RING).then_inc(yo_v[l], 1)

                blocks(0)
                dve.wait_ge(rows_stored, 16 * NT * (l + 1))
                v.tensor_scalar(X[:], X[:], ALPHA, None, ALU.mult).then_inc(x_scaled, 1)
                with dve.Fori(1, NE // RING - 1) as it:
                    blocks(it)
                blocks(NE // RING - 1)
                dve.wait_ge(sc_done[RING - 1], 16 * ((l + 1) * NE // RING - 1))
                dve.wait_ge(wb_used, (l + 1) * NE)
                half_out(1, RING - 1).then_inc(yo_v[l], 1)
                further = dve.value_load(meta[0:1, NOV:NOV + 1], min_val=0, max_val=NOV)
                with dve.If(further > 0):
                    with dve.Fori(0, NOV) as u:
                        with dve.If(u < further):
                            turn = dve.snap(u + 1)
                            dve.wait_ge(ov_s[l], turn)
                            hidden(0).then_inc(ov_m[l], 1)
                        dve.nop()

                def combine(i):
                    r, t = RR[l][i], X[:, i, :]
                    dve.wait_ge(rr_full[i], 16 * (l + 1))
                    link(v.scalar_tensor_tensor(t, r[:, 0, :], gates[:, 0, i:i + 1], t, ALU.mult, ALU.add))
                    v.scalar_tensor_tensor(t, r[:, 1, :], gates[:, 1, i:i + 1], t, ALU.mult, ALU.add).then_inc(rr_used, 1)
                    dve.wait_ge(rr_used, l * NT + i + 1)
                    if i == 0:
                        dve.wait_ge(lnp_loaded, 32 * LNP[l, 2])
                    normalize(t, LNG[:], LNB[:])

                name = "x2a" if l == 0 else "x2b"
                dve.wait_ge(x_scaled, l + 1)
                combine(0)
                take_transposed(name, 0, XTv)
                combine(1)
                dve.wait_ge(ple_in, 32 * (l + 1))
                for i in range(NT):
                    for n in range(NB):
                        q = (l * NT + i) * NB + n
                        if q >= 4:
                            dve.wait_ge(ple_done, q - 3)
                        v.tensor_tensor(GT[q % 4], take("g", l, i, n), GBB[:, n * BANK:(n + 1) * BANK], ALU.add).then_inc(job_v, 1)
                        if n == 0 and i + 1 < NT:
                            take_transposed(name, i + 1, XTv)
                    for n in range(NB):
                        q = (l * NT + i) * NB + n
                        dve.wait_ge(g_sig, q + 1)
                        v.tensor_tensor(GT[q % 4], GT[q % 4], PP[:, i, n * BANK:(n + 1) * BANK], ALU.mult).then_inc(gated, 1)
                    if l == 0 and i:
                        take_transposed("x3a", i - 1, XTv)
                    if i + 2 < NT:
                        combine(i + 2)
                if l == 0:
                    take_transposed("x3a", NT - 1, XTv)


_INS = ["x", "p", "a_w_in", "a_b_in", "a_vn_g", "a_vn_b", "a_w_s", "a_b_s", "a_w_out", "b_w_in", "b_kv_g", "b_w_uk",
        "b_w_uv", "b_w_out", "ln1_g", "ln1_b", "ln2_g", "ln2_b", "r_wg", "r_bg", "r_we", "r_be", "e_w_in", "e_w_out",
        "ple_w", "ple_gw", "ple_gb"]


def kernel(**inputs):
    import concourse.bacc as bacc
    from concourse.bass_utils import run_bass_kernel_spmd

    nc = bacc.Bacc("TRN2", target_bir_lowering=False, num_devices=1)
    arrays, aps = {}, {}
    for name in _INS:
        a = np.ascontiguousarray(inputs[name])
        arrays[f"in_{name}"] = a
        aps[name] = nc.dram_tensor(f"in_{name}", a.shape, mybir.dt.from_np(a.dtype), kind="ExternalInput").ap()
    aps["out"] = nc.dram_tensor("out_x", (1, T, D), F32, kind="ExternalOutput").ap()
    trunk(nc, **aps)
    r = run_bass_kernel_spmd(nc, [arrays], core_ids=[0])
    return r.results[0]["out_x"]
```

```python
from contextlib import ExitStack

import numpy as np

import concourse.bass as bass
from concourse import mybir

F32 = mybir.dt.float32
BF16 = mybir.dt.bfloat16
I32 = mybir.dt.int32
F32R = mybir.dt.float32r
U32 = mybir.dt.uint32
ALU = mybir.AluOpType
ACT = mybir.ActivationFunctionType
AX = mybir.AxisListType

P = 128
DEPTH = 2
ALPHA = (2 * DEPTH) ** 0.25
LN_EPS, RMS_EPS = 1e-5, 1e-6
BIG = 1e30
TAKEN = -3e38

T, D = 512, 1024
NT, KD, BANK = T // P, D // P, 512
NB = D // BANK
HEADS, HD, LAT = 8, 128, 256
IH, ID = 8, 64
TOPK = min(256, T // 4)
NG, EPG = 4, 8
NE = NG * EPG
ASIDE = NE - 4
STREAMED = NE - 1
FF = 256
PLE = 256
BLK = 64
NOV = 2 * T // BLK - 1
NU = 48
NONE = 4096
GATES_AT, UNITS_AT = 2, 6
RING = 4


class Job:

    def __init__(self, n, engine, nth):
        self.n, self.bank, self.engine, self.nth = n, 4 + n % 4, engine, nth


class Jobs:

    def __init__(self):
        self.order, self.by, self.count = [], {}, {"act": 0, "dve": 0}

    def add(self, engine, *name):
        self.count[engine] += 1
        job = Job(len(self.order), engine, self.count[engine])
        self.order.append(job)
        self.by[name] = job

    def __getitem__(self, name):
        return self.by[name]


WEIGHTS = [("in", 0, w) for w in range(4)]
WEIGHTS += [job for l in range(DEPTH) for job in (("out", l, 0), ("out", l, 1), ("g", l, 0))]
ROWS = [("in", 0, i) for i in range(NT)]
ROWS += [(kind, l, i) for l in range(DEPTH) for kind in ("out", "g") for i in range(NT)]
PARTS = 4
HIGH = -(1 << 12)

UNITS = [(qt, hg) for qt in range(NT) for hg in range(2)]


def plan_jobs():
    jobs = Jobs()
    for w in range(4):
        for i in range(NT):
            jobs.add("dve", "in", w, i)
        for q in range(2) if w == 0 else ():
            jobs.add("act", "ws", q)
    for g in range(8):
        jobs.add("dve", "sp", g)
    for l in range(DEPTH):
        if l == 1:
            for q in range(4):
                jobs.add("act", "uk", q)
            jobs.add("act", "ki")
            for i in range(NT):
                jobs.add("dve", "ck", i)
            for b in range(4):
                jobs.add("act", "qi", b)
            for qt in range(1, NT):
                for h in range(IH):
                    jobs.add("act", "ix", qt, h)
            for cc in range(2):
                jobs.add("act", "ct", cc)
            for h in range(HEADS):
                jobs.add("act", "q", h)
            for h in range(HEADS):
                for cc in range(2):
                    jobs.add("act", "ql", h, cc)
            for u, (qt, hg) in enumerate(UNITS):
                for kt in range(qt + 1):
                    jobs.add("act" if kt % 2 else "dve", "tr", u, kt)
                for cc in range(2):
                    jobs.add("dve" if cc else "act", "pv", u, cc)
                jobs.add("act", "uv", u)
        for step in range(NT + 1):
            if step < NT:
                for n in range(NB):
                    jobs.add("dve", "out", l, step, n)
            if step:
                jobs.add("dve", "rt", l, step - 1)
        for cc in range(2):
            jobs.add("act", "pt", l, cc)
        for i in range(NT):
            for n in range(NB):
                jobs.add("act", "pp", l, i, n)
        for i in range(NT):
            for n in range(NB):
                jobs.add("dve", "g", l, i, n)
    return jobs


def trunk(nc, x, p, a_w_in, a_b_in, a_vn_g, a_vn_b, a_w_s, a_b_s, a_w_out,
          b_w_in, b_kv_g, b_w_uk, b_w_uv, b_w_out, ln1_g, ln1_b, ln2_g, ln2_b,
          r_wg, r_bg, r_we, r_be, e_w_in, e_w_out, ple_w, ple_gw, ple_gb, out):
    jobs = plan_jobs()
    x_rows = nc.dram_tensor("x_rows", [T, D], F32, kind="Internal").ap()
    y_rows = nc.dram_tensor("y_rows", [2 * T, D], F32, kind="Internal").ap()

    Q0, K0, I0, KI0 = 0, HEADS * HD, HEADS * HD + LAT, HEADS * HD + LAT + IH * ID
    half = lambda w, n: [(w[:, n * BANK:(n + 1) * BANK], 0, BANK)]
    misc = [(b_w_in[0][:, K0:K0 + LAT], 0, LAT),
            (b_w_in[0][:, KI0:KI0 + ID], LAT, ID),
            (b_w_in[0][:, KI0:KI0 + ID + IH], LAT + ID, ID + IH)]
    wa_head = [
        [half(a_w_in[0], 2), half(a_w_in[0], 3), half(a_w_in[0], 0), half(a_w_in[0], 1),
         half(a_w_out[0], 0), half(a_w_out[0], 1)],
        [misc, [(b_w_in[0][:, I0:I0 + BANK], 0, BANK)], half(b_w_in[0], 0), half(b_w_in[0], 1),
         half(b_w_out[0], 0), half(b_w_out[0], 1)],
    ]
    WA_E = [6, 6 + STREAMED + 2 + 6]
    WB_E = [1, STREAMED + 4]
    WA_HEAD = [0, 6 + STREAMED + 2]
    WA_GW = [WA_E[0] + STREAMED, WA_E[1] + STREAMED]
    WB_PLE = [WB_E[0] - 1, WB_E[1] - 1]
    WB_UK, WB_UV = STREAMED + 1, STREAMED + 2
    FLAT = "(a p) n -> p a n"

    wa_last, wb_last = {}, {WB_UK: ("uk", 3), WB_UV: ("uv", len(UNITS) - 1)}
    for w in range(4):
        wa_last[w] = ("in", w, NT - 1)
    for n, name in enumerate([("ck", NT - 1), ("qi", 3), ("q", 3), ("q", 7)]):
        wa_last[WA_HEAD[1] + n] = name
    for l in range(DEPTH):
        for n in range(NB):
            wa_last[WA_HEAD[l] + 4 + n] = ("out", l, NT - 1, n)
            wa_last[WA_GW[l] + n] = ("g", l, NT - 1, n)
        wb_last[WB_PLE[l]] = ("pp", l, NT - 1, NB - 1)
    MISC = WA_HEAD[1]

    def tile_of(e):
        return e - (e > ASIDE)

    def wa_turn(n):
        extra = len(misc) - 1 if n >= MISC and n % RING == MISC % RING else 0
        return 16 * (n // RING + 1 + extra)

    ctx = ExitStack()
    with ctx:
        def sb(name, shape, dt=F32):
            return ctx.enter_context(nc.sbuf_tensor(name, shape, dt))

        twins = {}

        def sb_twin(name, shape):
            with nc.sbuf_tensor(name, shape, F32) as plain:
                pass
            twins[name] = sb(name + "_r", shape, F32R)
            return plain

        def rounded(view):
            return bass.AP(twins[view.tensor.name], view.offset, view.ap)

        def sem(name):
            return ctx.enter_context(nc.semaphore(name))

        ps = ctx.enter_context(nc.psum_tensor("ps", [P, 8, BANK], F32))
        wa = [sb_twin(f"wa{r}", [P, KD, BANK]) for r in range(RING)]
        wb = [sb_twin(f"wb{r}", [P, 2, D]) for r in range(RING)]
        wbh = [w[:].rearrange("p a (h d) -> p (a h) d", d=HD) for w in wb]
        X = sb("X", [P, NT, D])
        XT = sb_twin("XT", [P, KD * T])
        A = sb_twin("A", [P, KD * T])
        B = sb_twin("B", [P, KD * T])
        C = sb_twin("C", [P, 9216])
        LNG, LNB = sb("LNG", [P, D]), sb("LNB", [P, D])

        def cut(area, at, *dims):
            n = int(np.prod(dims))
            v = area[:, at:at + n]
            if len(dims) == 2:
                v = v.rearrange("p (a b) -> p a b", a=dims[0])
            if len(dims) == 3:
                v = v.rearrange("p (a b c) -> p a b c", a=dims[0], b=dims[1])
            if len(dims) == 4:
                v = v.rearrange("p (a b c d) -> p a b c d", a=dims[0], b=dims[1], c=dims[2])
            return v

        XTv, AT = cut(XT, 0, KD, T), cut(A, 0, KD, T)
        V, U = cut(A, 0, NT, D), cut(B, 0, NT, D)
        BINV, BINU, VNG, VNB = C[:, 0:D], C[:, D:2 * D], LNG[:], LNB[:]
        WCT, BS, WS, XHI = cut(C, 2048, 8, P), C[:, 3072:3080], cut(C, 4096, 8, P), cut(C, 5120, KD, T)
        QIT, KIT, CK, CKT = cut(C, 0, 4, T), C[:, 2048:2560], cut(C, 2560, NT, LAT), cut(C, 3584, 2, T)
        UKT, SELS, OL, KVG = cut(C, 4608, HEADS, LAT), C[:, 6656:7936], cut(C, 7936, 2, BANK), C[:, 8960:9216]
        SEL = [SELS[:, P * (q * (q + 1) // 2):][:, :P * (q + 1)] for q in range(NT)]
        PR, PT = cut(C, 0, 4, BANK), cut(C, 4608, NT, BANK)
        RL = cut(B, 0, 2, BANK)
        JUNK = cut(B, 1024, NT, LAT)
        QL = [cut(B if h < 4 else XT, (h % 4) * 2 * T, 2, T) for h in range(HEADS)]
        LG = cut(C, 8192, NT, NG + NE)
        at = [0]

        def tmp(*dims, area=XT):
            v = cut(area, at[0], *dims)
            at[0] += int(np.prod(dims))
            return v

        gmax, gkey, gsum, m1, m2, key, dexp, den = (tmp(NT) for _ in range(8))
        geq, gsel, gexp, pen = (tmp(NT, NG) for _ in range(4))
        em, eq = tmp(NT, NE), tmp(NT, NE)
        EK, EW = tmp(2, NT, NE), tmp(2, NT, NE)
        MB = cut(XT, at[0], NT * NE // 2).bitcast(BF16).rearrange("p (a b) -> p a b", a=NT)
        at[0] += NT * NE // 2
        cex, cin, extra, one = (tmp(NE) for _ in range(4))
        rank, base, eidx, blk, slot, unit, further_blk = (tmp(2 * NT) for _ in range(7))
        ints, inti, intc = (tmp(n).bitcast(I32) for n in (2 * NT, 2 * NT, NE))
        RSH = tmp(2 * NT, BLK)
        at[0] = 7168
        UVH, whose, owner = tmp(2 * NT, NU, area=C), tmp(NOV, NE, area=C), tmp(NOV, area=C)
        rowf, offs = tmp(NU, area=C), tmp(NU, area=C)
        XG, YO = ([B[h * BLK:(h + 1) * BLK, D * s:D * (s + 1)] for s in range(RING)] for h in range(2))
        XGT = [cut(XT, 512 * s, KD, BLK) for s in range(2)]
        SA = [cut(XT, 1024 + 128 * s, 2, BLK) for s in range(2)]
        HT = [cut(XT, 1280 + 128 * s, 2, BLK) for s in range(2)]
        HS = [cut(XT, 1536 + FF * s, FF) for s in range(2)]
        OWA, OWB = cut(A, 0, KD, BANK), cut(XT, 2048, 2, D)
        RR = [[cut(wa[(WA_GW[l] + NB + i // 2) % RING][:].rearrange("p a b -> p (a b)"), (i % 2) * 2 * D, 2, D)
               for i in range(NT)] for l in range(DEPTH)]
        def halves_of(*areas):
            return [a.rearrange("p a (b n) -> p (a b) n", b=2) if a.shape[2] == D else a for a in areas]

        HI = {(kind, 0, n): halves_of(wb[2 * (n % 2)][:], wb[2 * (n % 2) + 1][:])
              for kind, n in [("in", w) for w in range(4)] + [("out", n) for n in range(NB)]}
        HI |= {
            ("out", 1, 0): halves_of(wb[2][:], wb[3][:]),
            ("out", 1, 1): halves_of(cut(B, 0, 4, BANK), cut(B, 2048, 4, BANK))}
        for l in range(DEPTH):
            HI["g", l, 0] = halves_of(cut(A, 0, 4, BANK), cut(A, 2048, 4, BANK))
            HI["g", l, 1] = halves_of(wb[2][:], wb[3][:])
        XH = [cut(B, 2048 + 1024 * s, KD, P) for s in range(2)]
        PIN, PTT, GBB, PP = cut(C, 0, NT, PLE), cut(C, 1024, 2, T), C[:, 2048:3072], cut(C, 3072, NT, D)
        GT = [B[:, 512 * s:512 * (s + 1)] for s in range(4)]

        ident = sb("ident", [P, P])
        strict = sb("strict", [P, P], BF16)
        ones = sb("ones", [P, P], BF16)
        iota = sb("iota", [P, BLK])
        rev = sb("rev", [P, NE])
        val = sb("val", [P, 2 * NT])
        rw = sb("rw", [P, KD, NG + NE])
        rb = sb("rb", [P, NG + NE])
        idx_tok = sb("idx_tok", [BLK, NU], U32)
        idx_row = sb("idx_row", [BLK, NU], U32)
        meta = sb("meta", [1, NOV + 1], I32)
        stg = sb("stg", [BLK, 4], U32)
        sts = sb("sts", [BLK, 4], U32)
        gates = sb("gates", [P, 2, NT])
        WI = sb("WI", [P, NT, IH])
        bn = sb("bn", [P, 2, 6])
        mv = sb("mv", [P, 2])
        rstd = sb("rstd", [P, 1])
        minus_half = sb("minus_half", [P, 1])
        m8 = sb("m8", [P, 8])
        ss = sb("ss", [P, NT])
        mx, nmx, rs, rc = (sb(n, [P, 4]) for n in ("mx", "nmx", "rs", "rc"))

        consts_ready, x_loaded, gm_loaded = sem("consts_ready"), sem("x_loaded"), sem("gm_loaded")
        wa_full = [sem(f"wa_full{r}") for r in range(RING)]
        wb_full = [sem(f"wb_full{r}") for r in range(RING)]
        wa_used, wb_used, aside_full = sem("wa_used"), sem("wb_used"), sem("aside_full")
        tr_ps, tr_a, tr_v = sem("tr_ps"), sem("tr_a"), sem("tr_v")
        job_done, job_a, job_v = sem("job_done"), sem("job_a"), sem("job_v")
        z_done = sem("z_done")
        ln_done, lnp_loaded = sem("ln_done"), sem("lnp_loaded")
        chain_v, chain_p = sem("chain_v"), sem("chain_p")
        wct_ready = sem("wct_ready")
        rw_loaded, ple_in, kvg_loaded = sem("rw_loaded"), sem("ple_in"), sem("kvg_loaded")
        rows_stored = sem("rows_stored")
        gate_in, gate_exp = sem("gate_in"), sem("gate_exp")
        picks, ranked, coded, unit_ps, units_ready = (sem(n) for n in ("picks", "ranked", "coded", "unit_ps", "units_ready"))
        xg_zero = sem("xg_zero")
        staged = [sem(f"staged{l}") for l in range(DEPTH)]
        xg_full = [sem(f"xg_full{s}") for s in range(RING)]
        sc_done = [sem(f"sc_done{s}") for s in range(RING)]
        xg_used, xgt_ready, hs_ready, hs_ps, sa_ready, ht_ready, yo_a, yo_v = (
            [sem(f"{n}{l}") for l in range(DEPTH)]
            for n in ("xg_used", "xgt_ready", "hs_ready", "hs_ps", "sa_ready", "ht_ready", "yo_a", "yo_v"))
        ov_free, ov_w, ov_g, ov_t, ov_x, ov_h, ov_s, ov_m, ov_y, ov_e, ov_d, moe_done = (
            [sem(f"{n}{l}") for l in range(DEPTH)]
            for n in ("ov_free", "ov_w", "ov_g", "ov_t", "ov_x", "ov_h", "ov_s", "ov_m", "ov_y", "ov_e", "ov_d", "moe_done"))
        rr_full = [sem(f"rr_full{i}") for i in range(NT)]
        rr_used, x_scaled = sem("rr_used"), sem("x_scaled")
        g_sig, ple_done = sem("g_sig"), sem("ple_done")
        var_ready, rstd_ready, rl_used, sel_mask = (sem(n) for n in ("var_ready", "rstd_ready", "rl_used", "sel_mask"))
        lg_ps, lg_read, lg_max, p_exp, p_norm = (sem(n) for n in ("lg_ps", "lg_read", "lg_max", "p_exp", "p_norm"))
        out_done = sem("out_done")
        first_half, last_added = sem("first_half"), sem("last_added")
        pe_passed = sem("pe_passed")
        w_split, x_split, gw_rest, high_done, gw_low, w_ready, xs_ready, gw_ready = (sem(n) for n in (
            "w_split", "x_split", "gw_rest", "high_done", "gw_low", "w_ready", "xs_ready", "gw_ready"))
        passed = sem("passed")

        TR = {}
        for s, name in enumerate(["x0", "gated", "x1a", "x2a", "x3a", "x1b", "x2b"]):
            for i in range(NT):
                TR[name, i] = None
        order = [("x0", i) for i in range(NT)] + [("gated", i) for i in range(NT)] + [("x1a", i) for i in range(NT)]
        ple_order = []
        ple_order.append(("x2a", 0))
        for i in range(NT):
            if i + 1 < NT:
                ple_order.append(("x2a", i + 1))
            if i:
                ple_order.append(("x3a", i - 1))
        ple_order.append(("x3a", NT - 1))
        order += ple_order + [("x1b", i) for i in range(NT)] + [("x2b", i) for i in range(NT)]
        for n, tile_name in enumerate(order):
            TR[tile_name] = n
        LN = {"v": 0, (0, 1): NT, (0, 2): 2 * NT, (1, 1): 3 * NT, (1, 2): 4 * NT}
        LNP = {(0, 1): 1, (0, 2): 2, (1, 1): 3, (1, 2): 4}

        def weight_part(kind, l, n, tile_n, q):
            return HI[kind, l, n][q // 2][:, 2 * (q % 2):2 * (q % 2) + 2, :], wa[tile_n % RING][:, 2 * q:2 * q + 2, :]

        def row_halves(kind, l, i):
            cols = slice(i * P, (i + 1) * P)
            return {"in": (XHI[:, :, cols], XTv[:, :, cols]), "out": (XTv[:, :, cols], AT[:, :, cols]),
                    "g": (XH[i % 2], XTv[:, :, cols])}[kind]

        def drained(eng, job):
            eng.wait_ge(job_a if job.engine == "act" else job_v, job.nth)

        links_v, norms, rstds = [0], [0], [0]
        block = ctx.enter_context(nc.Block())

        @block.sync
        def _(sp):
            def slot_free(n, last, used, first_expert):
                if n < 0:
                    return
                if n in last:
                    sp.wait_ge(job_done, jobs[last[n]].n + 1)
                else:
                    l = 1 if n >= first_expert[1] else 0
                    e = n - first_expert[l]
                    sp.wait_ge(used, l * NE + e + (e >= ASIDE) + 1)

            def load_wa(n, parts):
                slot_free(n - RING, wa_last, wa_used, WA_E)
                s = n % RING
                if n == 0:
                    src = parts[0][0].rearrange(FLAT, p=P)
                    sp.dma_start(wa[0][:, 0:KD // 2, :], src[:, 0:KD // 2]).then_inc(first_half, 16)
                    sp.dma_start(wa[0][:, KD // 2:, :], src[:, KD // 2:]).then_inc(wa_full[0], 16)
                    return
                for src, at, w in parts:
                    sp.dma_start(wa[s][:, :, at:at + w], src.rearrange(FLAT, p=P)).then_inc(wa_full[s], 16)

            def load_wb(n, dst, src):
                slot_free(n - RING, wb_last, wb_used, WB_E)
                sp.dma_start(dst, src).then_inc(wb_full[n % RING], 16)

            def load_experts(l, it):
                for j in range(RING):
                    e = sp.snap(it * RING + j)
                    before = sp.snap(it * RING + (l * NE + j + 1 - RING))
                    sa, sb_ = (WA_E[l] + j) % RING, (WB_E[l] + j) % RING
                    sp.wait_ge(wa_used, before)
                    sp.dma_start(wa[sa][:], e_w_in[l, bass.ds(e, 1)].rearrange("o (a p) f -> p (o a) f", p=P)).then_inc(wa_full[sa], 16)
                    sp.wait_ge(wb_used, before)
                    sp.dma_start(wb[sb_][:], e_w_out[l, bass.ds(e, 1)].rearrange("o (a p) f -> p (o a) f", p=P)).then_inc(wb_full[sb_], 16)

            for i in range(NT):
                sp.dma_start(X[:, i, :], x[0, i * P:(i + 1) * P, :]).then_inc(x_loaded, 16)
            for l in range(DEPTH):
                if l == 1:
                    sp.wait_ge(rr_used, NT)
                for n, parts in enumerate(wa_head[l]):
                    load_wa(WA_HEAD[l] + n, parts)
                    if l == 0 and n == 0:
                        for dst, src in ((BINV, a_b_in[0, D:2 * D]), (VNG, a_vn_g[0]), (VNB, a_vn_b[0]), (BINU, a_b_in[0, 0:D])):
                            sp.dma_start(dst, src.partition_broadcast(P)).then_inc(gm_loaded, 16)
                        sp.dma_start(WS, a_w_s[0].rearrange("g t s -> t g s")).then_inc(gm_loaded, 16)
                        sp.dma_start(BS, a_b_s[0].rearrange("g t -> t g"), allow_slow_non_contiguous=True).then_inc(gm_loaded, 16)
                    if l == 1 and n == 1:
                        load_wb(WB_UK, wbh[WB_UK % RING], b_w_uk[0].rearrange("h (a p) d -> p (h a) d", p=P))
                    if l == 1 and n == 3:
                        load_wb(WB_UV, wbh[WB_UV % RING], b_w_uv[0].rearrange("h (a p) d -> p (h a) d", p=P))
                for e in range(2):
                    load_wa(WA_E[l] + e, [(e_w_in[l, e], 0, BANK)])
                sp.wait_ge(job_done, jobs["out", l, NT - 1, NB - 1].n + 1)
                load_wb(WB_PLE[l], wb[WB_PLE[l] % RING][:], ple_w[l].rearrange(FLAT, p=P))
                for e in range(RING):
                    if e >= 2:
                        load_wa(WA_E[l] + e, [(e_w_in[l, e], 0, BANK)])
                    if e < RING - 1:
                        load_wb(WB_E[l] + e, wb[(WB_E[l] + e) % RING][:], e_w_out[l, e].rearrange(FLAT, p=P))
                load_wb(WB_E[l] + RING - 1, wb[(WB_E[l] + RING - 1) % RING][:], e_w_out[l, RING - 1].rearrange(FLAT, p=P))
                sp.wait_ge(xg_full[RING - 1], 16 * (l * NE // RING + 1))
                sp.dma_start(OWA, e_w_in[l, ASIDE].rearrange(FLAT, p=P)).then_inc(aside_full, 16)
                sp.dma_start(OWB, e_w_out[l, ASIDE].rearrange(FLAT, p=P)).then_inc(aside_full, 16)
                with sp.Fori(1, NE // RING - 1) as it:
                    load_experts(l, it)
                for e in range(ASIDE + 1, NE):
                    na, nb = WA_E[l] + tile_of(e), WB_E[l] + tile_of(e)
                    load_wa(na, [(e_w_in[l, e], 0, BANK)])
                    load_wb(nb, wb[nb % RING][:], e_w_out[l, e].rearrange(FLAT, p=P))
                sp.wait_ge(units_ready, l + 1)
                further = sp.value_load(meta[0:1, NOV:NOV + 1], min_val=0, max_val=NOV)
                with sp.If(further > 0):
                    with sp.Fori(0, NOV) as u:
                        with sp.If(u < further):
                            e = sp.value_load(meta[0:1, bass.ds(u, 1)], min_val=0, max_val=NE - 1)
                            turn = sp.snap(u + 1)
                            sp.wait_ge(ov_free[l], turn)
                            sp.dma_start(OWA, e_w_in[l, bass.ds(e, 1)].rearrange("o (a p) f -> p (o a) f", p=P)).then_inc(ov_w[l], 16)
                            sp.dma_start(OWB, e_w_out[l, bass.ds(e, 1)].rearrange("o (a p) f -> p (o a) f", p=P)).then_inc(ov_w[l], 16)
                        sp.nop()
                load_wa(WA_GW[l], half(ple_gw[l], 0))
                n = WA_GW[l] + 1
                slot_free(n - RING, wa_last, wa_used, WA_E)
                for k in (0, KD // 2):
                    if k:
                        sp.wait_ge(rr_full[0], 16 * (l + 1))
                    sp.dma_start(wa[n % RING][:, k:k + KD // 2, :],
                                 ple_gw[l][:, BANK:].rearrange(FLAT, p=P)[:, k:k + KD // 2]).then_inc(
                                     gw_rest if k else wa_full[n % RING], 16)
            for i in range(NT - 1):
                sp.wait_ge(ple_done, NB * (NT + i + 1))
                sp.dma_start(out[0, i * P:(i + 1) * P, :], X[:, i, :]).then_inc(out_done, 16)
            for n, (added, count) in enumerate(((ple_done, DEPTH * NT * NB - 1), (last_added, 1))):
                sp.wait_ge(added, count)
                cols = slice(n * BANK, (n + 1) * BANK)
                sp.dma_start(out[0, (NT - 1) * P:, cols], X[:, NT - 1, cols]).then_inc(out_done, 16)
            sp.wait_ge(out_done, 16 * (NT + 1))

        @block.gpsimd
        def _(pool):
            links = [0]

            def link(ins):
                links[0] += 1
                ins.then_inc(chain_p, 1)
                pool.wait_ge(chain_p, links[0])

            g = nc.gpsimd
            last_tok, last_row = pool.to_reg(T - 1), pool.to_reg(2 * T - 1)
            link(g.memset(ident[:], 0.0))
            link(g.affine_select(out=ident[:], in_=ident[:], compare_op=ALU.not_equal, fill=1.0, base=0,
                                 pattern=[[-1, P]], channel_multiplier=1))
            link(g.memset(minus_half[:], -0.5))
            link(g.memset(ones[:], 1.0))
            link(g.affine_select(out=strict[:], in_=ones[:], compare_op=ALU.is_gt, fill=0.0, base=0,
                                 pattern=[[1, P]], channel_multiplier=-1))
            link(g.iota(iota[:], pattern=[[1, BLK]], base=0, channel_multiplier=0, allow_small_or_imprecise_dtypes=True))
            link(g.iota(rev[:], pattern=[[-1, NE]], base=NE, channel_multiplier=0, allow_small_or_imprecise_dtypes=True))
            link(g.iota(val[:], pattern=[[T, 2], [P, NT]], base=-NONE, channel_multiplier=1,
                        allow_small_or_imprecise_dtypes=True))
            g.sem_inc(consts_ready, 1)

            def load_ln(gain, bias):
                for dst, src in ((LNG, gain), (LNB, bias)):
                    pool.dma_start(dst[:], src.partition_broadcast(P)).then_inc(lnp_loaded, 16)

            def rstd_of_tiles(n):
                for _ in range(n):
                    rstds[0] += 1
                    pool.wait_ge(var_ready, rstds[0])
                    link(g.tensor_scalar(rstd[:], mv[:, 1:2], LN_EPS, None, ALU.add))
                    g.tensor_tensor(rstd[:], rstd[:], minus_half[:], ALU.pow).then_inc(rstd_ready, 1)

            drained(pool, jobs["ws", 1])
            g.affine_select(out=WCT, in_=WCT, compare_op=ALU.is_ge, fill=0.0, base=0,
                            pattern=[[0, 8], [1, P]], channel_multiplier=-1).then_inc(wct_ready, 1)
            rstd_of_tiles(NT)
            pool.wait_ge(ln_done, NT)
            load_ln(ln1_g[0], ln1_b[0])

            for l in range(DEPTH):
                if l == 1:
                    for i in range(NT):
                        rstds[0] += 1
                        pool.wait_ge(var_ready, rstds[0])
                        link(g.tensor_scalar(ss[:, i:i + 1], ss[:, i:i + 1], 1.0 / LAT, RMS_EPS, ALU.mult, ALU.add))
                        g.tensor_tensor(ss[:, i:i + 1], ss[:, i:i + 1], minus_half[:], ALU.pow).then_inc(rstd_ready, 1)
                    g.memset(SEL[0], 0.0).then_inc(chain_p, 1)
                    links[0] += 1
                    pool.wait_ge(chain_p, links[0])
                    g.affine_select(out=SEL[0], in_=SEL[0], compare_op=ALU.is_ge, fill=-BIG, base=0,
                                    pattern=[[-1, P]], channel_multiplier=1).then_inc(sel_mask, 1)
                    for qt in range(1, NT):
                        pool.wait_ge(rl_used, IH * qt)
                        own = SEL[qt][:, qt * P:]
                        g.affine_select(out=own, in_=own, compare_op=ALU.is_ge, fill=-BIG, base=0,
                                        pattern=[[-1, P]], channel_multiplier=1).then_inc(sel_mask, 1)
                rstd_of_tiles(NT)
                pool.wait_ge(ln_done, LN[l, 1] + NT)
                load_ln(ln2_g[l], ln2_b[l])
                for s in range(RING):
                    g.memset(XG[s], 0.0).then_inc(xg_zero, 1)
                pool.wait_ge(xg_zero, RING * (l + 1))
                pool.wait_ge(rows_stored, 16 * NT * (l + 1))
                pool.wait_ge(units_ready, l + 1)

                def gather(col, s, done):
                    pool.indirect_dma_start(XG[s], None, x_rows,
                                            bass.IndirectOffsetOnAxis(ap=col, axis=0),
                                            bounds_check=last_tok, oob_is_err=False).then_inc(done, 16)

                def scatter(col, src, done):
                    pool.indirect_dma_start(y_rows, bass.IndirectOffsetOnAxis(ap=col, axis=0),
                                            src, None,
                                            bounds_check=last_row, oob_is_err=False).then_inc(done, 16)

                for s in range(RING):
                    gather(idx_tok[:, s:s + 1], s, xg_full[s])

                def blocks(it, last):
                    static = isinstance(it, int)
                    num = (lambda a: a) if static else pool.snap
                    for j in range(RING):
                        first = static and it == 0 and j < 2
                        copies = j - 1 if first else it * (2 * RING) + (j - 2 if last else 2 * j - 2)
                        column = (lambda e: slice(e, e + 1)) if static else (lambda e: bass.ds(e, 1))
                        if not last:
                            copies = copies + (2 if first else 1)
                            pool.wait_ge(xg_used[l], num(it * RING + (j + 1)))
                            pool.sem_inc(passed, 1)
                            g.tensor_copy(stg[:, j:j + 1], idx_tok[:, column(num(it * RING + (RING + j)))]).then_inc(staged[l], 1)
                            pool.wait_ge(staged[l], num(copies))
                            pool.sem_inc(passed, 1)
                            gather(stg[:, j:j + 1], j, xg_full[j])
                        if not first:
                            store_block(num, column, it * RING + (j - 2), (j - 2) % RING, copies + 1)

                def store_block(num, column, e, s, copies):
                    pool.wait_ge(yo_a[l], num(e + 1))
                    pool.wait_ge(yo_v[l], num(e + 1))
                    pool.sem_inc(passed, 1)
                    g.tensor_copy(sts[:, s:s + 1], idx_row[:, column(num(e))]).then_inc(staged[l], 1)
                    pool.wait_ge(staged[l], num(copies))
                    pool.sem_inc(passed, 1)
                    scatter(sts[:, s:s + 1], YO[s], sc_done[s])

                blocks(0, False)
                with pool.Fori(1, NE // RING - 1) as it:
                    blocks(it, False)
                blocks(NE // RING - 1, True)
                for e in range(NE - 2, NE):
                    pool.wait_ge(yo_a[l], e + 1)
                    pool.wait_ge(yo_v[l], e + 1)
                    pool.sem_inc(passed, 1)
                    scatter(idx_row[:, e:e + 1], YO[e % RING], sc_done[e % RING])
                for s in range(RING):
                    pool.wait_ge(sc_done[s], 16 * NE // RING * (l + 1))
                further = pool.value_load(meta[0:1, NOV:NOV + 1], min_val=0, max_val=NOV)
                with pool.If(further > 0):
                    pool.sem_inc(ov_free[l], 1)
                    with pool.Fori(0, NOV) as u:
                        with pool.If(u < further):
                            turn = pool.snap(u + 1)
                            landed = pool.snap(u * 16 + 16)
                            outputs = pool.snap(u * 2 + 2)
                            staged_n = pool.snap(u * 2 + (2 * NE - RING))
                            g.tensor_copy(stg[:, 0:1], idx_tok[:, bass.ds(u + NE, 1)]).then_inc(staged[l], 1)
                            g.tensor_copy(sts[:, 0:1], idx_row[:, bass.ds(u + NE, 1)]).then_inc(staged[l], 1)
                            pool.wait_ge(staged[l], staged_n)
                            pool.sem_inc(passed, 1)
                            gather(stg[:, 0:1], 0, ov_g[l])
                            pool.wait_ge(ov_e[l], outputs)
                            pool.sem_inc(passed, 1)
                            scatter(sts[:, 0:1], YO[0], ov_d[l])
                            pool.wait_ge(ov_d[l], landed)
                            pool.sem_inc(ov_free[l], 1)
                        pool.nop()
                pool.sem_inc(moe_done[l], 1)

                def low_parts(parts):
                    for q in parts:
                        pool.wait_ge(high_done, PARTS * l + q + 1)
                        high, values = weight_part("g", l, 1, WA_GW[l] + 1, q)
                        g.tensor_tensor(rounded(values), values, high, ALU.subtract).then_inc(gw_low, 1)

                low_parts(range(PARTS // 2))
                rstd_of_tiles(2)
                low_parts(range(PARTS // 2, PARTS))
                for i in range(NT):
                    if i + 2 < NT:
                        rstd_of_tiles(1)
                    for n in range(NB):
                        q = (l * NT + i) * NB + n
                        if q == DEPTH * NT * NB - 1:
                            break
                        pool.wait_ge(g_sig, q + 1)
                        link(g.tensor_tensor(GT[q % 4], GT[q % 4], PP[:, i, n * BANK:(n + 1) * BANK], ALU.mult))
                        xs = X[:, i, n * BANK:(n + 1) * BANK]
                        g.tensor_tensor(xs, xs, GT[q % 4], ALU.add).then_inc(ple_done, 1)
                if l == 0:
                    pool.wait_ge(ln_done, LN[l, 2] + NT)
                    load_ln(ln1_g[1], ln1_b[1])

        @block.scalar
        def _(act):
            s = nc.scalar

            def load_router(l):
                act.dma_start(rw[:, :, 0:NG], r_wg[l].rearrange(FLAT, p=P), allow_slow_non_contiguous=True).then_inc(rw_loaded, 16)
                act.dma_start(rw[:, :, NG:], r_we[l].rearrange(FLAT, p=P)).then_inc(rw_loaded, 16)
                act.dma_start(rb[:, 0:NG], r_bg[l].partition_broadcast(P)).then_inc(rw_loaded, 16)
                act.dma_start(rb[:, NG:], r_be[l].partition_broadcast(P)).then_inc(rw_loaded, 16)

            def take(job):
                act.wait_ge(job_done, job.n + 1)
                return ps[:, job.bank, :]

            def copy_job(dst, *name, scale=None):
                job = jobs[name]
                src = take(job)
                if len(dst.shape) == 3:
                    src = src.rearrange("p (a b) -> p a b", a=dst.shape[1])
                if scale is None:
                    s.activation(dst, src, ACT.Copy).then_inc(job_a, 1)
                else:
                    s.activation(dst, src, ACT.Copy, scale=scale).then_inc(job_a, 1)

            def take_transposed(name, i, dst):
                n = TR[name, i]
                act.wait_ge(tr_ps, 2 * n + 1)
                src = ps[:, 2 * (n % 2), :].rearrange("p (a b) -> p a b", a=4)
                s.activation(dst[:, 0:4, i * P:(i + 1) * P], src, ACT.Copy).then_inc(tr_a, 1)

            def hand_over(high, split_done, count, ready):
                act.wait_ge(split_done, count)
                s.activation(rounded(high), high, ACT.Copy).then_inc(ready, 1)

            def weights_ready(kind, l, n, parts=range(PARTS)):
                tile_n = {"in": 0, "out": WA_HEAD[l] + 4, "g": WA_GW[l]}[kind] + n
                for q in parts:
                    high = weight_part(kind, l, n, tile_n, q)[0]
                    if (kind, n) == ("g", 1):
                        hand_over(high, gw_low, PARTS * l + q + 1, gw_ready)
                    else:
                        hand_over(high, w_split, PARTS * WEIGHTS.index((kind, l, n)) + q + 1, w_ready)

            def rows_ready(kind, l, i):
                hand_over(row_halves(kind, l, i)[0], x_split, ROWS.index((kind, l, i)) + 1, xs_ready)

            for i in range(2):
                take_transposed("x0", i, XTv)
            for i in range(2):
                rows_ready("in", 0, i)
            weights_ready("in", 0, 0)
            for i in range(2, NT):
                take_transposed("x0", i, XTv)
            for i in range(2, NT):
                rows_ready("in", 0, i)
            act.wait_ge(gm_loaded, 16 * 6)
            load_router(0)
            for w in range(4):
                area, n = (V, U)[w // 2], w % 2
                for i in range(NT):
                    act.wait_ge(job_v, jobs["in", w, i].nth)
                    z = area[:, i, n * BANK:(n + 1) * BANK]
                    s.activation(z, z, ACT.Gelu).then_inc(z_done, 1)
                    weights_ready(*(("in", 0, w + 1) if w < 3 else ("out", 0, 0)), (i,))
                for q in range(2) if w == 0 else ():
                    copy_job(WCT[:, 4 * q:4 * q + 4, :], "ws", q)
            for i in range(NT):
                take_transposed("gated", i, AT)
                if i in (1, 3):
                    rows_ready("out", 0, i - 1)
                    rows_ready("out", 0, i)
                if i == 2:
                    weights_ready("out", 0, 1)

            for l in range(DEPTH):
                if l == 1:
                    act.dma_start(KVG, b_kv_g[0].partition_broadcast(P)).then_inc(kvg_loaded, 16)
                    for q in range(4):
                        copy_job(UKT[:, 2 * q:2 * q + 2, :], "uk", q)
                    copy_job(KIT, "ki")
                    for i in range(NT):
                        job = jobs["ck", i]
                        src = take(job)
                        s.activation(JUNK[:, i, :], src[:, 0:LAT], ACT.Square, accum_out=ss[:, i:i + 1]).then_inc(var_ready, 1)
                    for b in range(4):
                        copy_job(QIT[:, b, :], "qi", b)
                    n = 0
                    for qt in range(1, NT):
                        for h in range(IH):
                            nk = (qt + 1) * P
                            src = take(jobs["ix", qt, h])
                            if n >= 2:
                                act.wait_ge(rl_used, n - 1)
                            s.activation(RL[:, n % 2, 0:nk], src[:, 0:nk], ACT.Relu).then_inc(job_a, 1)
                            n += 1
                    for cc in range(2):
                        copy_job(CKT[:, cc, :], "ct", cc)
                    for h in range(HEADS):
                        copy_job(AT[:, h, :], "q", h)
                    act.wait_ge(rl_used, n)
                    for h in range(HEADS):
                        for cc in range(2):
                            copy_job(QL[h][:, cc, :], "ql", h, cc, scale=float(HD) ** -0.5)
                    for u, (qt, hg) in enumerate(UNITS):
                        nk = (qt + 1) * P
                        for j in range(4):
                            act.wait_ge(lg_max, u + 1)
                            s.activation(PR[:, j, 0:nk], PR[:, j, 0:nk], ACT.Exp, bias=nmx[:, j:j + 1],
                                         accum_out=rs[:, j:j + 1]).then_inc(p_exp, 1)
                        for kt in range(1, qt + 1, 2):
                            copy_job(PT[:, kt, :], "tr", u, kt)
                        copy_job(OL[:, 0, :], "pv", u, 0)
                        copy_job(AT[:, 4 * hg:4 * hg + 4, qt * P:(qt + 1) * P], "uv", u)
                        if u < PARTS:
                            weights_ready("out", 1, 0, (u,))
                    for i in range(NT):
                        rows_ready("out", 1, i)
                        if i == NT - 2:
                            weights_ready("out", 1, 1)

                act.dma_start(PIN, p[l, 0].rearrange("(i p) n -> p i n", p=P)).then_inc(ple_in, 16)
                act.dma_start(GBB, ple_gb[l].partition_broadcast(P)).then_inc(ple_in, 16)
                for i in range(NT):
                    act.wait_ge(ln_done, LN[l, 1] + i + 1)
                    act.dma_start(x_rows[i * P:(i + 1) * P, :], X[:, i, :]).then_inc(rows_stored, 16)
                    take_transposed("x1a" if l == 0 else "x1b", i, XTv)
                for cc in range(2):
                    copy_job(PTT[:, cc, :], "pt", l, cc)
                for q in range(NT * NB):
                    if q == GATES_AT:
                        act.wait_ge(gate_in, l + 1)
                        s.activation(gexp, gexp, ACT.Exp).then_inc(gate_exp, 1)
                        s.activation(dexp, dexp, ACT.Exp).then_inc(gate_exp, 1)
                    i, n = q // NB, q % NB
                    copy_job(PP[:, i, n * BANK:(n + 1) * BANK], "pp", l, i, n)

                def transposed(turn, k):
                    act.wait_ge(xg_used[l], turn)
                    s.activation(XGT[k], ps[:, k, :].rearrange("p (a b) -> p a b", a=KD), ACT.Copy).then_inc(xgt_ready[l], 1)

                def copy_hidden(k):
                    return s.activation(HS[k], ps[:, 2 + k, 0:FF], ACT.Copy)

                def silu(k):
                    return s.activation(SA[k], ps[:, 2 + k, FF:2 * FF].rearrange("p (a b) -> p a b", a=2)[:, :, 0:BLK], ACT.Silu)

                def halves(turn, k, slot, scattered):
                    act.wait_ge(wb_used, turn)
                    if scattered is not None:
                        act.wait_ge(sc_done[slot], scattered)
                    s.activation(YO[slot][:, 0:BANK], ps[0:BLK, 4 + 2 * k, :], ACT.Copy).then_inc(yo_a[l], 1)

                def blocks(it):
                    static = isinstance(it, int)
                    num = (lambda v: v) if static else act.snap
                    for j in range(RING):
                        first = static and it == 0
                        last = static and it == NE // RING - 1 and j == RING - 1
                        k = j % 2
                        product = num(it * RING + (l * NE + j + 1))
                        turned = num(it * RING + (j + 1))
                        nxt = num(it * RING + (j + 2))
                        wb_turn = num(it * RING + (l * NE + j))
                        scattered = None if first else num(it * 16 + 16 * (l * NE // RING - (j == 0)))
                        if static and scattered == 0:
                            scattered = None
                        act.wait_ge(wa_used, product)
                        copy_hidden(k).then_inc(hs_ready[l], 1)
                        if not last:
                            transposed(nxt, 1 - k)
                        act.wait_ge(hs_ps[l], turned)
                        silu(k).then_inc(sa_ready[l], 1)
                        if not (first and j == 0):
                            halves(wb_turn, 1 - k, (j - 1) % RING, scattered)

                transposed(1, 0)
                blocks(0)
                blocks(1)
                with act.Fori(2, NE // RING - 1) as it:
                    blocks(it)
                blocks(NE // RING - 1)
                halves((l + 1) * NE, 1, RING - 1, 16 * ((l + 1) * NE // RING - 1))

                further = act.value_load(meta[0:1, NOV:NOV + 1], min_val=0, max_val=NOV)
                with act.If(further > 0):
                    with act.Fori(0, NOV) as u:
                        with act.If(u < further):
                            turn = act.snap(u + 1)
                            turned = act.snap(u + (NE + 1))
                            act.wait_ge(ov_t[l], turn)
                            s.activation(XGT[0], ps[:, 0, :].rearrange("p (a b) -> p a b", a=KD), ACT.Copy).then_inc(ov_x[l], 1)
                            act.wait_ge(ov_h[l], turn)
                            copy_hidden(0).then_inc(hs_ready[l], 1)
                            act.wait_ge(hs_ps[l], turned)
                            silu(0).then_inc(ov_s[l], 1)
                            act.wait_ge(ov_y[l], turn)
                            for n in range(NB):
                                s.activation(YO[0][:, n * BANK:(n + 1) * BANK], ps[n * BLK:(n + 1) * BLK, 4 + n, :],
                                             ACT.Copy).then_inc(ov_e[l], 1)
                        act.nop()

                act.wait_ge(moe_done[l], 1)
                y_view = y_rows.rearrange("(k t) d -> t k d", k=2)

                for i in range(NT):
                    act.dma_start(RR[l][i], y_view[i * P:(i + 1) * P]).then_inc(rr_full[i], 16)
                name = "x2a" if l == 0 else "x2b"
                weights_ready("g", l, 0)
                weights_ready("g", l, 1, range(PARTS // 2))
                take_transposed(name, 0, XTv)
                rows_ready("g", l, 0)
                for i in range(NT):
                    for n in range(NB):
                        q = (l * NT + i) * NB + n
                        act.wait_ge(job_v, jobs["g", l, i, n].nth)
                        s.activation(GT[q % 4], GT[q % 4], ACT.Sigmoid).then_inc(g_sig, 1)
                        if n == 0 and i + 1 < NT:
                            take_transposed(name, i + 1, XTv)
                            if i == 0:
                                weights_ready("g", l, 1, range(PARTS // 2, PARTS))
                            rows_ready("g", l, i + 1)
                    if l == 0 and i:
                        take_transposed("x3a", i - 1, XTv)
                if l == 0:
                    take_transposed("x3a", NT - 1, XTv)
                    load_router(1)

        def attention(pe, open_job, need_wa, need_wb, product, need_xt):
            mm = nc.tensor.matmul
            need_wb(WB_UK)
            flat = wbh[WB_UK % RING]
            for q in range(4):
                bank = open_job("uk", q)
                for b in range(4):
                    last = nc.tensor.transpose(bank[:, b * P:(b + 1) * P], flat[:, 4 * q + b, :], ident[:])
                last.then_inc(job_done, 1)
            for i in range(NT):
                need_xt("x3a", i)
            tile = need_wa(WA_HEAD[1])
            product(open_job("ki"), lambda k: tile[:, k, LAT:LAT + 2 * ID], lambda k: XTv[:, k, :], T).then_inc(job_done, 1)
            for i in range(NT):
                bank = open_job("ck", i)
                product(bank, lambda k: XTv[:, k, i * P:(i + 1) * P], lambda k: tile[:, k, 0:LAT], LAT)
                product(bank[:, LAT:LAT + IH], lambda k: XTv[:, k, i * P:(i + 1) * P],
                        lambda k: tile[:, k, LAT + 2 * ID:LAT + 2 * ID + IH], IH).then_inc(job_done, 1)
            tile = need_wa(WA_HEAD[1] + 1)
            for b in range(4):
                product(open_job("qi", b), lambda k: tile[:, k, b * P:(b + 1) * P], lambda k: XTv[:, k, :], T).then_inc(job_done, 1)
            drained(pe, jobs["qi", 3])
            for qt in range(1, NT):
                nk = (qt + 1) * P
                for h in range(IH):
                    o = ID * (h % 2)
                    mm(open_job("ix", qt, h)[:, 0:nk], QIT[o:o + ID, h // 2, qt * P:(qt + 1) * P],
                       KIT[o:o + ID, 0:nk], start=True, stop=True).then_inc(job_done, 1)
            drained(pe, jobs["ck", NT - 1])
            for cc in range(2):
                bank = open_job("ct", cc)
                for i in range(NT):
                    last = nc.tensor.transpose(bank[:, i * P:(i + 1) * P], CK[:, i, cc * P:(cc + 1) * P], ident[:])
                last.then_inc(job_done, 1)
            for h in range(HEADS):
                tile = need_wa(WA_HEAD[1] + 2 + h // 4)
                product(open_job("q", h), lambda k: tile[:, k, (h % 4) * HD:(h % 4 + 1) * HD],
                        lambda k: XTv[:, k, :], T).then_inc(job_done, 1)
            for h in range(HEADS):
                drained(pe, jobs["q", h])
                for cc in range(2):
                    mm(open_job("ql", h, cc), UKT[:, h, cc * P:(cc + 1) * P], AT[:, h, :],
                       start=True, stop=True).then_inc(job_done, 1)
            drained(pe, jobs["ql", HEADS - 1, 1])

            def logits(u):
                qt, hg = UNITS[u]
                nk = (qt + 1) * P
                for j in range(4):
                    if u:
                        pe.wait_ge(lg_read, 4 * (u - 1) + j + 1)
                    for cc in range(2):
                        last = mm(ps[:, j, 0:nk], QL[4 * hg + j][:, cc, qt * P:(qt + 1) * P], CKT[:, cc, 0:nk],
                                  start=(cc == 0), stop=(cc == 1))
                    last.then_inc(lg_ps, 1)

            need_wb(WB_UV)
            uv = wbh[WB_UV % RING]
            logits(0)
            for u, (qt, hg) in enumerate(UNITS):
                if u + 1 < len(UNITS):
                    logits(u + 1)
                pe.wait_ge(p_norm, 4 * (u + 1))
                for kt in range(qt + 1):
                    bank = open_job("tr", u, kt)
                    for j in range(4):
                        last = nc.tensor.transpose(bank[:, j * P:(j + 1) * P], PR[:, j, kt * P:(kt + 1) * P], ident[:])
                    last.then_inc(job_done, 1)
                for cc in range(2):
                    bank = open_job("pv", u, cc)
                    for kt in range(qt + 1):
                        if cc == 0:
                            drained(pe, jobs["tr", u, kt])
                        last = mm(bank, CK[:, kt, cc * P:(cc + 1) * P], PT[:, kt, :], start=(kt == 0), stop=(kt == qt))
                    last.then_inc(job_done, 1)
                bank = open_job("uv", u)
                for cc in range(2):
                    drained(pe, jobs["pv", u, cc])
                for j in range(4):
                    for cc in range(2):
                        last = mm(bank[:, j * P:(j + 1) * P], uv[:, 2 * (4 * hg + j) + cc, :], OL[:, cc, j * P:(j + 1) * P],
                                  start=(cc == 0), stop=(cc == 1))
                last.then_inc(job_done, 1)
            drained(pe, jobs["uv", len(UNITS) - 1])

        @block.tensor
        def _(pe):
            mm = nc.tensor.matmul

            def open_job(*name):
                job = jobs[name]
                if job.n >= 4:
                    drained(pe, jobs.order[job.n - 4])
                return ps[:, job.bank, :]

            def transpose_tile(name, i, src):
                n = TR[name, i]
                if n >= 2:
                    pe.wait_ge(tr_a, n - 1)
                    pe.wait_ge(tr_v, n - 1)
                for h in range(2):
                    for b in range(4):
                        k = 4 * h + b
                        last = nc.tensor.transpose(ps[:, 2 * (n % 2) + h, b * P:(b + 1) * P],
                                                   src[:, k * P:(k + 1) * P], ident[:])
                    last.then_inc(tr_ps, 1)

            def need_wa(n):
                pe.wait_ge(wa_full[n % RING], wa_turn(n))
                return wa[n % RING]

            def need_wb(n):
                pe.wait_ge(wb_full[n % RING], 16 * (n // RING + 1))
                return wb[n % RING]

            def product(bank, left, right, w):
                for k in range(KD):
                    last = mm(bank[:, 0:w], left(k), right(k), start=(k == 0), stop=(k == KD - 1))
                return last

            first_use = set()

            def product3(bank, x_high, x_low, kind, l, n, tile):
                for k in range(KD):
                    part = (kind, l, n, k * PARTS // KD)
                    if part not in first_use:
                        first_use.add(part)
                        if (kind, n) == ("g", 1):
                            pe.wait_ge(gw_ready, PARTS * l + part[-1] + 1)
                        else:
                            pe.wait_ge(w_ready, PARTS * WEIGHTS.index((kind, l, n)) + part[-1] + 1)
                    w_high, w_low = rounded(HI[kind, l, n][k // 4][:, k % 4, :]), rounded(tile[:, k, :])
                    xh, xl = rounded(x_high(k)), rounded(x_low(k))
                    mm(bank, xh, w_high, start=(k == 0), stop=False)
                    mm(bank, xh, w_low, start=False, stop=False)
                    last = mm(bank, xl, w_high, start=False, stop=(k == KD - 1))
                return last

            def need_xt(name, i):
                pe.wait_ge(tr_a, TR[name, i] + 1)
                pe.wait_ge(tr_v, TR[name, i] + 1)

            pe.wait_ge(consts_ready, 1)
            pe.wait_ge(x_loaded, 16 * NT)
            for i in range(NT):
                transpose_tile("x0", i, X[:, i, :])
            for w in range(4):
                tile = wa[w]
                for i in range(NT):
                    if w == 0:
                        pe.wait_ge(xs_ready, ROWS.index(("in", 0, i)) + 1)
                    cols = slice(i * P, (i + 1) * P)
                    product3(open_job("in", w, i), lambda k: XHI[:, k, cols], lambda k: XTv[:, k, cols],
                             "in", 0, w, tile).then_inc(job_done, 1)
                if w == 0:
                    pe.wait_ge(gm_loaded, 16 * 6)
                for q in range(2) if w == 0 else ():
                    bank = open_job("ws", q)
                    for b in range(4):
                        last = nc.tensor.transpose(bank[:, b * P:(b + 1) * P], WS[:, 4 * q + b, :], ident[:])
                    last.then_inc(job_done, 1)
            pe.wait_ge(ln_done, NT)
            pe.wait_ge(wct_ready, 1)
            for g in range(8):
                bank = open_job("sp", g)
                mm(bank.rearrange("p (c d) -> p c d", c=NT), WCT[:, g, :], V[:, :, g * P:(g + 1) * P],
                   start=True, stop=True).then_inc(job_done, 1)
            drained(pe, jobs["sp", 7])
            for i in range(NT - 1):
                transpose_tile("gated", i, U[:, i, :])

            for l in range(DEPTH):
                if l == 1:
                    attention(pe, open_job, need_wa, need_wb, product, need_xt)

                tiles = [need_wa(WA_HEAD[l] + 4 + n) for n in range(NB)]
                pe.wait_ge(rw_loaded, 64 * (l + 1))
                name = "x1a" if l == 0 else "x1b"
                for step in range(NT + 1):
                    for n in range(NB):
                        if step < NT:
                            if n == 0:
                                pe.wait_ge(xs_ready, ROWS.index(("out", l, step)) + 1)
                            cols = slice(step * P, (step + 1) * P)
                            product3(open_job("out", l, step, n), lambda k: XTv[:, k, cols], lambda k: AT[:, k, cols],
                                     "out", l, n, tiles[n]).then_inc(job_done, 1)
                        if l == 0 and step == 0 and n == 0:
                            transpose_tile("gated", NT - 1, U[:, NT - 1, :])
                        if step and n == 0:
                            pe.wait_ge(ln_done, LN[l, 1] + step)
                            transpose_tile(name, step - 1, X[:, step - 1, :])
                    if step:
                        i = step - 1
                        need_xt(name, i)
                        bank = open_job("rt", l, i)
                        product(bank, lambda k: XTv[:, k, i * P:(i + 1) * P], lambda k: rw[:, k, :], NG + NE).then_inc(job_done, 1)

                pe.wait_ge(ple_in, 32 * (l + 1))
                for cc in range(2):
                    bank = open_job("pt", l, cc)
                    for i in range(NT):
                        last = nc.tensor.transpose(bank[:, i * P:(i + 1) * P], PIN[:, i, cc * P:(cc + 1) * P], ident[:])
                    last.then_inc(job_done, 1)
                ple_tile = need_wb(WB_PLE[l])
                drained(pe, jobs["pt", l, 1])
                for q in range(NT * NB):
                    if q == GATES_AT:
                        pe.wait_ge(picks, l + 1)
                        cum, cnt = ps[:, 0, 0:NT * NE], ps[:, 1, 0:NE]
                        for i in range(NT):
                            for j in range(i):
                                mm(cum[:, i * NE:(i + 1) * NE], ones[:], MB[:, j, :], start=(j == 0), stop=False)
                            mm(cum[:, i * NE:(i + 1) * NE], strict[:], MB[:, i, :], start=(i == 0), stop=True)
                        for j in range(NT):
                            last = mm(cnt, ones[:], MB[:, j, :], start=(j == 0), stop=(j == NT - 1))
                        last.then_inc(ranked, 1)
                    if q == UNITS_AT:
                        pe.wait_ge(coded, l + 1)
                        for c in range(2 * NT):
                            last = mm(ps[0:BLK, 2, 0:NU], RSH[:, c, :], UVH[:, c, :], start=(c == 0), stop=(c == 2 * NT - 1))
                        last.then_inc(unit_ps, 1)
                    i, n = q // NB, q % NB
                    bank = open_job("pp", l, i, n)
                    for c in range(2):
                        last = mm(bank, PTT[:, c, i * P:(i + 1) * P], ple_tile[:, c, n * BANK:(n + 1) * BANK],
                                  start=(c == 0), stop=(c == 1))
                    last.then_inc(job_done, 1)

                def transposes(slot, k):
                    pe.sem_inc(pe_passed, 1)
                    for b in range(KD):
                        last = nc.tensor.transpose(ps[:, k, b * BLK:(b + 1) * BLK], XG[slot][:, b * P:(b + 1) * P],
                                                   ident[0:BLK, 0:BLK])
                    return last

                def products_in(k, tile):
                    for c in range(KD):
                        for n in range(2):
                            last = mm(ps[n * BLK:(n + 1) * BLK, 2 + k, 0:FF], XGT[k][:, c, :], tile[:, c, n * FF:(n + 1) * FF],
                                      start=(c == 0), stop=(c == KD - 1))
                    return last

                def turn_hidden(k):
                    for c in range(2):
                        last = nc.tensor.transpose(ps[:, 2 + k, FF + c * P:FF + (c + 1) * P], HS[k][:, c * P:(c + 1) * P], ident[:])
                    return last

                def products_out(k, tile):
                    for c in range(2):
                        for n in range(NB):
                            last = mm(ps[n * BLK:(n + 1) * BLK, 4 + 2 * k + n, :], HT[k][:, c, :],
                                      tile[:, c, n * BANK:(n + 1) * BANK], start=(c == 0), stop=(c == 1))
                    return last

                def out_block(b, k, s):
                    ht, full, free = b
                    if full is not None:
                        pe.wait_ge(wb_full[s], full)
                    if free is not None:
                        pe.wait_ge(yo_a[l], free)
                        pe.wait_ge(yo_v[l], free)
                    pe.wait_ge(ht_ready[l], ht)
                    products_out(k, OWB if full is None else wb[s]).then_inc(wb_used, 1)

                def blocks(it):
                    static = isinstance(it, int)
                    num = (lambda v: v) if static else pe.snap
                    for j in range(RING):
                        first = static and it == 0
                        last = static and it == NE // RING - 1 and j == RING - 1
                        aside = static and it * RING + j == ASIDE
                        aside_before = static and it * RING + j - 1 == ASIDE
                        k = j % 2
                        na, nb = WA_E[l] + j, WB_E[l] + j - 1
                        if static and it * RING > ASIDE - RING:
                            na = WA_E[l] + tile_of(it * RING + j) - it * RING
                            nb = WB_E[l] + tile_of(it * RING + j - 1) - it * RING
                        full_a = num(it * 16 + wa_turn(na))
                        full_b = num(it * 16 + 16 * (nb // RING + 1))
                        e1 = num(it * RING + (j + 1))
                        e0 = None if first and j == 0 else num(it * RING + j)
                        em = None if first and j < 2 else num(it * RING + (j - 1))
                        emm = None if first and j < 3 else num(it * RING + (j - 2))
                        rows = num(it * 16 + 16 * (l * NE // RING + (j + 1) // RING + 1))
                        if aside:
                            pe.wait_ge(aside_full, 32 * (l + 1))
                        else:
                            pe.wait_ge(wa_full[na % RING], full_a)
                        if em is not None:
                            pe.wait_ge(ht_ready[l], em)
                        pe.wait_ge(xgt_ready[l], e1)
                        products_in(k, OWA if aside else wa[na % RING]).then_inc(wa_used, 1)
                        if not last:
                            pe.wait_ge(xg_full[(j + 1) % RING], rows)
                            transposes((j + 1) % RING, 1 - k).then_inc(xg_used[l], 1)
                        pe.wait_ge(hs_ready[l], e1)
                        turn_hidden(k).then_inc(hs_ps[l], 1)
                        if e0 is not None:
                            out_block((e0, None if aside_before else full_b, emm), 1 - k, nb % RING)

                pe.wait_ge(xg_full[0], 16 * (l * NE // RING + 1))
                transposes(0, 0).then_inc(xg_used[l], 1)
                blocks(0)
                with pe.Fori(1, NE // RING - 1) as it:
                    blocks(it)
                blocks(NE // RING - 1)
                nb = WB_E[l] + STREAMED - 1
                out_block((NE, 16 * (nb // RING + 1), NE - 2), 1, nb % RING)

                further = pe.value_load(meta[0:1, NOV:NOV + 1], min_val=0, max_val=NOV)
                with pe.If(further > 0):
                    with pe.Fori(0, NOV) as u:
                        with pe.If(u < further):
                            turn = pe.snap(u + 1)
                            copied = pe.snap(u + (NE + 1))
                            rows = pe.snap(u * 16 + 16)
                            weights = pe.snap(u * 32 + 32)
                            pe.wait_ge(ov_g[l], rows)
                            transposes(0, 0).then_inc(ov_t[l], 1)
                            pe.wait_ge(ov_w[l], weights)
                            pe.wait_ge(ov_x[l], turn)
                            products_in(0, OWA).then_inc(ov_h[l], 1)
                            pe.wait_ge(hs_ready[l], copied)
                            turn_hidden(0).then_inc(hs_ps[l], 1)
                            pe.wait_ge(ov_m[l], turn)
                            products_out(0, OWB).then_inc(ov_y[l], 1)
                        pe.nop()
                pe.wait_ge(moe_done[l], 1)

                name = "x2a" if l == 0 else "x2b"

                def normalized(i):
                    pe.wait_ge(ln_done, LN[l, 2] + i + 1)
                    transpose_tile(name, i, X[:, i, :])

                def next_layer(i):
                    pe.wait_ge(ple_done, NB * (i + 1))
                    transpose_tile("x3a", i, X[:, i, :])

                normalized(0)
                for i in range(NT):
                    pe.wait_ge(xs_ready, ROWS.index(("g", l, i)) + 1)
                    for n in range(NB):
                        tile = need_wa(WA_GW[l] + n)
                        product3(open_job("g", l, i, n), lambda k: XH[i % 2][:, k, :], lambda k: XTv[:, k, i * P:(i + 1) * P],
                                 "g", l, n, tile).then_inc(job_done, 1)
                        if n == 0 and i + 1 < NT:
                            normalized(i + 1)
                    if l == 0 and i:
                        next_layer(i - 1)
                if l == 0:
                    next_layer(NT - 1)

        def attention_v(dve, v, link, take, split_weights, split_output_rows):
            dve.wait_ge(kvg_loaded, 16)
            for i in range(NT):
                src = take("ck", i)
                norms[0] += 1
                dve.wait_ge(rstd_ready, norms[0])
                v.tensor_scalar(WI[:, i, :], src[:, LAT:LAT + IH], float(IH * ID) ** -0.5, None, ALU.mult)
                v.scalar_tensor_tensor(CK[:, i, :], src[:, 0:LAT], ss[:, i:i + 1], KVG, ALU.mult, ALU.mult).then_inc(job_v, 1)
            dve.wait_ge(job_v, jobs["ck", NT - 1].nth)
            n = 0
            for qt in range(1, NT):
                for h in range(IH):
                    dve.wait_ge(job_a, jobs["ix", qt, h].nth)
                    r, w = RL[:, n % 2, 0:(qt + 1) * P], WI[:, qt, h:h + 1]
                    if h == 0:
                        last = v.tensor_scalar(SEL[qt], r, w, None, ALU.mult)
                    else:
                        last = v.scalar_tensor_tensor(SEL[qt], r, w, SEL[qt], ALU.mult, ALU.add)
                    last.then_inc(rl_used, 1)
                    n += 1
                    dve.wait_ge(rl_used, n)
            for qt in range(1, NT):
                dve.wait_ge(sel_mask, qt + 1)
                for _ in range(TOPK // 8):
                    link(v.max(m8[:], SEL[qt]))
                    link(v.match_replace(SEL[qt], m8[:], SEL[qt], TAKEN))
                link(v.tensor_scalar(SEL[qt], SEL[qt], TAKEN / 10, -BIG, ALU.is_gt, ALU.mult))
            for u, (qt, hg) in enumerate(UNITS):
                nk = (qt + 1) * P
                if u:
                    dve.wait_ge(job_done, jobs["tr", u - 1, UNITS[u - 1][0]].n + 1)
                for j in range(4):
                    dve.wait_ge(lg_ps, 4 * u + j + 1)
                    v.tensor_tensor_reduce(PR[:, j, 0:nk], ps[:, j, 0:nk], SEL[qt], 1.0, TAKEN, ALU.add, ALU.max,
                                           mx[:, j:j + 1]).then_inc(lg_read, 1)
                dve.wait_ge(lg_read, 4 * (u + 1))
                v.tensor_scalar(nmx[:], mx[:], -1.0, None, ALU.mult).then_inc(lg_max, 1)
                dve.wait_ge(p_exp, 4 * (u + 1))
                link(v.reciprocal(rc[:], rs[:]))
                for j in range(4):
                    v.tensor_scalar(PR[:, j, 0:nk], PR[:, j, 0:nk], rc[:, j:j + 1], None, ALU.mult).then_inc(p_norm, 1)
                for kt in range(0, qt + 1, 2):
                    v.tensor_copy(PT[:, kt, :], take("tr", u, kt)).then_inc(job_v, 1)
                v.tensor_copy(OL[:, 1, :], take("pv", u, 1)).then_inc(job_v, 1)
                if u < PARTS:
                    split_weights("out", 1, 0, (u,))
            for i in range(NT):
                dve.wait_ge(job_a, jobs["uv", 2 * i + 1].nth)
                split_output_rows(1, i)
                if i == NT - 2:
                    split_weights("out", 1, 1)

        def route(dve, v, link, l):
            tt, ts, red = v.tensor_tensor, v.tensor_scalar, v.tensor_reduce

            def over(a, n):
                return a.unsqueeze(len(a.shape)).broadcast_to(list(a.shape) + [n])

            def pick(dst, vals, top, work, rank_of, n):
                link(tt(work, vals, over(top, n), ALU.is_equal))
                link(tt(work, work, rank_of.unsqueeze(1).broadcast_to([P, NT, n]), ALU.mult))
                link(red(key, work, AX.X, ALU.max))
                link(tt(dst, work, over(key, n), ALU.is_equal))

            g, e = LG[:, :, 0:NG], LG[:, :, NG:]
            link(red(gmax, g, AX.X, ALU.max))
            pick(gsel, g, gmax, geq, rev[:, NE - NG:], NG)
            tt(gexp, g, over(gmax, NG), ALU.subtract)
            link(ts(pen, gsel, BIG, -BIG, ALU.mult, ALU.add))
            grouped = em.rearrange("p t (g e) -> p t g e", g=NG)
            for i in range(NT):
                last = tt(grouped[:, i], e[:, i].rearrange("p (g e) -> p g e", g=NG), over(pen[:, i], EPG), ALU.add)
            link(last)
            link(red(m1, em, AX.X, ALU.max))
            pick(EK[:, 0], em, m1, eq, rev[:], NE)
            link(v.scalar_tensor_tensor(em, EK[:, 0], -BIG, em, ALU.mult, ALU.add))
            link(red(m2, em, AX.X, ALU.max))
            pick(EK[:, 1], em, m2, eq, rev[:], NE)
            tt(MB, EK[:, 0], EK[:, 1], ALU.add).then_inc(picks, 1)
            tt(dexp, m2, m1, ALU.subtract).then_inc(gate_in, 1)
            ek = EK.rearrange("p k t e -> p (k t) e")
            ew = EW.rearrange("p k t e -> p (k t) e")

            def spread(row, n):
                return row.unsqueeze(1).broadcast_to([P, 2 * NT, n])

            link(tt(ew, ek, spread(iota[:, 0:NE], NE), ALU.mult))
            link(red(eidx, ew, AX.X, ALU.add))
            link(v.memset(one, 1.0))
            dve.wait_ge(ranked, l + 1)
            link(ts(intc, ps[:, 1, 0:NE], -1.0, 0.0, ALU.add, ALU.max))
            link(ts(intc, intc, 6, None, ALU.logical_shift_right))
            link(v.tensor_copy(extra, intc))
            link(v.tensor_tensor_scan(cin, one, extra, 0.0, ALU.mult, ALU.add))
            link(tt(cex, cin, extra, ALU.subtract))
            link(tt(ew, ek, spread(cex, NE), ALU.mult))
            link(red(base, ew, AX.X, ALU.add))
            flat = EK.rearrange("p k t e -> p k (t e)")
            link(tt(EW.rearrange("p k t e -> p k (t e)"), flat,
                    ps[:, 0, 0:NT * NE].unsqueeze(1).broadcast_to([P, 2, NT * NE]), ALU.mult))
            link(red(rank, ew, AX.X, ALU.add))
            link(v.tensor_copy(ints, rank))
            link(ts(inti, ints, 6, None, ALU.logical_shift_right))
            link(v.tensor_copy(blk, inti))
            link(ts(ints, ints, BLK - 1, None, ALU.bitwise_and))
            link(v.tensor_copy(slot, ints))
            link(tt(unit, base, blk, ALU.add))
            link(v.scalar_tensor_tensor(unit, unit, float(NE - 1), eidx, ALU.add, ALU.subtract))
            link(ts(further_blk, blk, 0.0, None, ALU.is_gt))
            link(tt(unit, unit, further_blk, ALU.mult))
            link(tt(unit, unit, eidx, ALU.add))
            link(tt(UVH, spread(iota[:, 0:NU], NU), over(unit, NU), ALU.is_equal))
            link(tt(RSH, spread(iota[:], BLK), over(slot, BLK), ALU.is_equal))
            tt(UVH, UVH, over(val[:], NU), ALU.mult).then_inc(coded, 1)
            link(tt(whose[0:1], cin[0:1].unsqueeze(1).broadcast_to([1, NOV, NE]),
                    iota[0:1, 0:NOV].unsqueeze(2).broadcast_to([1, NOV, NE]), ALU.is_le))
            link(red(owner[0:1], whose[0:1], AX.X, ALU.add))
            link(ts(meta[0:1, 0:NOV], owner[0:1], float(NE - 1), None, ALU.min))
            link(v.tensor_copy(meta[0:1, NOV:NOV + 1], cin[0:1, NE - 1:NE]))
            dve.wait_ge(gate_exp, 2 * (l + 1))
            link(red(gsum, gexp, AX.X, ALU.add))
            link(ts(den, dexp, 1.0, None, ALU.add))
            link(tt(den, den, gsum, ALU.mult))
            link(v.reciprocal(gates[:, 0, :], den))
            link(tt(gates[:, 1, :], gates[:, 0, :], dexp, ALU.mult))
            dve.wait_ge(unit_ps, l + 1)
            rows, off = rowf[0:BLK], offs[0:BLK]
            link(ts(rows, ps[0:BLK, 2, 0:NU], float(NONE), None, ALU.add))
            link(v.tensor_copy(idx_row[:], rows))
            link(ts(off, rows, float(T), -float(T), ALU.is_ge, ALU.mult))
            tt(idx_tok[:], rows, off, ALU.add).then_inc(units_ready, 1)

        @block.vector
        def _(dve):
            v = nc.vector

            def link(ins):
                links_v[0] += 1
                ins.then_inc(chain_v, 1)
                dve.wait_ge(chain_v, links_v[0])

            def take(*name):
                job = jobs[name]
                dve.wait_ge(job_done, job.n + 1)
                return ps[:, job.bank, :]

            def take_transposed(name, i, dst):
                n = TR[name, i]
                dve.wait_ge(tr_ps, 2 * n + 2)
                src = ps[:, 2 * (n % 2) + 1, :].rearrange("p (a b) -> p a b", a=4)
                v.tensor_copy(dst[:, 4:8, i * P:(i + 1) * P], src).then_inc(tr_v, 1)

            def both_halves(name, i):
                dve.wait_ge(tr_a, TR[name, i] + 1)
                dve.wait_ge(tr_v, TR[name, i] + 1)

            def split(high, values, done):
                link(high_half(high, values))
                v.tensor_tensor(rounded(values), values, high, ALU.subtract).then_inc(done, 1)

            def high_half(high, values):
                return v.tensor_scalar(high.bitcast(I32), values.bitcast(I32), HIGH, None, ALU.bitwise_and)

            def split_weights(kind, l, n, parts=range(PARTS)):
                tile_n = {"in": 0, "out": WA_HEAD[l] + 4, "g": WA_GW[l]}[kind] + n
                for q in parts:
                    if tile_n == 0 and q < PARTS // 2:
                        dve.wait_ge(first_half, 16)
                    else:
                        dve.wait_ge(wa_full[tile_n % RING], wa_turn(tile_n))
                    split(*weight_part(kind, l, n, tile_n, q), w_split)

            def high_parts(l, parts):
                n = WA_GW[l] + 1
                dve.wait_ge(wa_full[n % RING], wa_turn(n))
                for q in parts:
                    if q == PARTS // 2:
                        dve.wait_ge(gw_rest, 16 * (l + 1))
                    high, values = weight_part("g", l, 1, n, q)
                    high_half(high, values).then_inc(high_done, 1)

            def split_output_rows(l, i):
                split(*row_halves("out", l, i), x_split)

            def normalize(t, gain, bias):
                for n in range(NB):
                    last = v.bn_stats(bn[:, n, :], t[:, n * BANK:(n + 1) * BANK])
                link(last)
                v.bn_aggr(mv[:], bn[:]).then_inc(var_ready, 1)
                norms[0] += 1
                dve.wait_ge(var_ready, norms[0])
                link(v.scalar_tensor_tensor(t, t, mv[:, 0:1], gain, ALU.subtract, ALU.mult))
                dve.wait_ge(rstd_ready, norms[0])
                v.scalar_tensor_tensor(t, t, rstd[:], bias, ALU.mult, ALU.add).then_inc(ln_done, 1)

            for i in range(NT):
                if i == 2:
                    split_weights("in", 0, 0)
                take_transposed("x0", i, XTv)
                both_halves("x0", i)
                split(*row_halves("in", 0, i), x_split)
            dve.wait_ge(gm_loaded, 16 * 6)

            NORMS = [(2, 1), (2, 3), (3, 0), (3, 1)]

            def norm_v(i):
                dve.wait_ge(z_done, NT + i + 1)
                normalize(V[:, i, :], VNG, VNB)

            for w in range(4):
                area, bias, n = ((V, BINV), (U, BINU))[w // 2] + (w % 2,)
                cols = slice(n * BANK, (n + 1) * BANK)
                for i in range(NT):
                    v.tensor_tensor(area[:, i, cols], take("in", w, i), bias[:, cols], ALU.add).then_inc(job_v, 1)
                    split_weights(*(("in", 0, w + 1) if w < 3 else ("out", 0, 0)), (i,))
                    if (w, i) in NORMS:
                        norm_v(NORMS.index((w, i)))
            dve.wait_ge(z_done, 4 * NT)
            for g in range(8):
                us = U[:, :, g * P:(g + 1) * P]
                src = take("sp", g).rearrange("p (c d) -> p c d", c=NT)
                v.scalar_tensor_tensor(us, src, BS[:, g:g + 1], us, ALU.add, ALU.mult).then_inc(job_v, 1)
            for i in range(NT):
                take_transposed("gated", i, AT)
                if i == 2:
                    split_weights("out", 0, 1)
                both_halves("gated", i)
                split_output_rows(0, i)

            for l in range(DEPTH):
                if l == 1:
                    attention_v(dve, v, link, take, split_weights, split_output_rows)
                name = "x1a" if l == 0 else "x1b"
                for step in range(NT + 1):
                    for n in range(NB):
                        if step < NT:
                            xs = X[:, step, n * BANK:(n + 1) * BANK]
                            last = v.scalar_tensor_tensor(xs, xs, ALPHA, take("out", l, step, n), ALU.mult, ALU.add)
                            last.then_inc(job_v, 1)
                        if step and n == 0:
                            take_transposed(name, step - 1, XTv)
                    if step < NT:
                        dve.wait_ge(job_v, jobs["out", l, step, NB - 1].nth)
                        if step == 0:
                            dve.wait_ge(lnp_loaded, 32 * LNP[l, 1])
                        normalize(X[:, step, :], LNG[:], LNB[:])
                    if step:
                        i = step - 1
                        if i == 0:
                            dve.wait_ge(rw_loaded, 64 * (l + 1))
                        v.tensor_tensor(LG[:, i, :], take("rt", l, i)[:, 0:NG + NE], rb[:], ALU.add).then_inc(job_v, 1)
                dve.wait_ge(job_v, jobs["rt", l, NT - 1].nth)
                route(dve, v, link, l)

                def hidden(k):
                    values = ps[:, 2 + k, FF:2 * FF].rearrange("p (a b) -> p a b", a=2)[:, :, BLK:2 * BLK]
                    return v.tensor_tensor(HT[k], SA[k], values, ALU.mult)

                def half_out(k, slot):
                    return v.tensor_copy(YO[slot][:, BANK:], ps[BLK:2 * BLK, 5 + 2 * k, :])

                def blocks(it):
                    static = isinstance(it, int)
                    num = (lambda a: a) if static else dve.snap
                    for j in range(RING):
                        first = static and it == 0
                        k = j % 2
                        e1 = num(it * RING + (j + 1))
                        wb_0 = num(it * RING + (l * NE + j))
                        scattered = None if first else num(it * 16 + 16 * (l * NE // RING - (j == 0)))
                        if static and scattered == 0:
                            scattered = None
                        dve.wait_ge(sa_ready[l], e1)
                        hidden(k).then_inc(ht_ready[l], 1)
                        if not (first and j == 0):
                            if scattered is not None:
                                dve.wait_ge(sc_done[(j - 1) % RING], scattered)
                            dve.wait_ge(wb_used, wb_0)
                            half_out(1 - k, (j - 1) % RING).then_inc(yo_v[l], 1)

                blocks(0)
                dve.wait_ge(rows_stored, 16 * NT * (l + 1))
                v.tensor_scalar(X[:], X[:], ALPHA, None, ALU.mult).then_inc(x_scaled, 1)
                blocks(1)
                with dve.Fori(2, NE // RING - 1) as it:
                    blocks(it)
                blocks(NE // RING - 1)
                dve.wait_ge(sc_done[RING - 1], 16 * ((l + 1) * NE // RING - 1))
                dve.wait_ge(wb_used, (l + 1) * NE)
                half_out(1, RING - 1).then_inc(yo_v[l], 1)
                further = dve.value_load(meta[0:1, NOV:NOV + 1], min_val=0, max_val=NOV)
                with dve.If(further > 0):
                    with dve.Fori(0, NOV) as u:
                        with dve.If(u < further):
                            turn = dve.snap(u + 1)
                            dve.wait_ge(ov_s[l], turn)
                            hidden(0).then_inc(ov_m[l], 1)
                        dve.nop()

                def combine(i):
                    r, t = RR[l][i], X[:, i, :]
                    dve.wait_ge(rr_full[i], 16 * (l + 1))
                    link(v.scalar_tensor_tensor(t, r[:, 0, :], gates[:, 0, i:i + 1], t, ALU.mult, ALU.add))
                    v.scalar_tensor_tensor(t, r[:, 1, :], gates[:, 1, i:i + 1], t, ALU.mult, ALU.add).then_inc(rr_used, 1)
                    dve.wait_ge(rr_used, l * NT + i + 1)
                    if i == 0:
                        dve.wait_ge(lnp_loaded, 32 * LNP[l, 2])
                    normalize(t, LNG[:], LNB[:])

                name = "x2a" if l == 0 else "x2b"

                def take_rows(i):
                    take_transposed(name, i, XTv)
                    both_halves(name, i)
                    split(*row_halves("g", l, i), x_split)

                split_weights("g", l, 0)
                high_parts(l, range(PARTS // 2))
                dve.wait_ge(x_scaled, l + 1)
                combine(0)
                take_rows(0)
                combine(1)
                high_parts(l, range(PARTS // 2, PARTS))
                dve.wait_ge(ple_in, 32 * (l + 1))
                for i in range(NT):
                    for n in range(NB):
                        q = (l * NT + i) * NB + n
                        if q >= 4:
                            dve.wait_ge(ple_done, q - 3)
                        v.tensor_tensor(GT[q % 4], take("g", l, i, n), GBB[:, n * BANK:(n + 1) * BANK], ALU.add).then_inc(job_v, 1)
                        if n == 0 and i + 1 < NT:
                            take_rows(i + 1)
                        if n == 0 and i + 2 < NT:
                            combine(i + 2)
                    if l == 0 and i:
                        take_transposed("x3a", i - 1, XTv)
                if l == 0:
                    take_transposed("x3a", NT - 1, XTv)
            q = DEPTH * NT * NB - 1
            gate, xs = GT[q % 4], X[:, NT - 1, BANK:]
            dve.wait_ge(g_sig, q + 1)
            link(v.tensor_tensor(gate, gate, PP[:, NT - 1, BANK:], ALU.mult))
            v.tensor_tensor(xs, xs, gate, ALU.add).then_inc(last_added, 1)


_INS = ["x", "p", "a_w_in", "a_b_in", "a_vn_g", "a_vn_b", "a_w_s", "a_b_s", "a_w_out", "b_w_in", "b_kv_g", "b_w_uk",
        "b_w_uv", "b_w_out", "ln1_g", "ln1_b", "ln2_g", "ln2_b", "r_wg", "r_bg", "r_we", "r_be", "e_w_in", "e_w_out",
        "ple_w", "ple_gw", "ple_gb"]


def kernel(**inputs):
    import concourse.bacc as bacc
    from concourse.bass_utils import run_bass_kernel_spmd

    nc = bacc.Bacc("TRN2", target_bir_lowering=False, num_devices=1)
    arrays, aps = {}, {}
    for name in _INS:
        a = np.ascontiguousarray(inputs[name])
        arrays[f"in_{name}"] = a
        aps[name] = nc.dram_tensor(f"in_{name}", a.shape, mybir.dt.from_np(a.dtype), kind="ExternalInput").ap()
    aps["out"] = nc.dram_tensor("out_x", (1, T, D), F32, kind="ExternalOutput").ap()
    trunk(nc, **aps)
    r = run_bass_kernel_spmd(nc, [arrays], core_ids=[0])
    return r.results[0]["out_x"]
```
